# Optimizing a Trainium2 kernel written in Bass

```python
import math
import jax
import jax.numpy as jnp
from jax import lax
import numpy as np

D_MODEL = 1024
BATCH = 1
SEQ = 512
DEPTH = 2

CTX_LEN = 256
GRID_W = 64
N_MIXERS = 2
N_S5_LAYERS = (DEPTH + N_MIXERS - 1) // N_MIXERS
N_MLA_LAYERS = DEPTH // N_MIXERS

S5_GROUP = 16
S5_GROUPS = D_MODEL // S5_GROUP
S5_STATE = 64
S5_CHUNK = 128
S5_DT_MIN = 0.001
S5_DT_MAX = 0.1

MLA_HEADS = D_MODEL // 128
MLA_NOPE = 128
MLA_ROPE = 64
MLA_V = 128
MLA_Q_RANK = 768
MLA_KV_RANK = 256
MLA_QK_DIM = MLA_NOPE + MLA_ROPE
ATTN_SCALE = 1.0 / math.sqrt(MLA_QK_DIM)
Q_BLOCK = 128
ROPE_BASE = 10000.0
ROPE_AXIS = MLA_ROPE // 2
ROPE_FREQS = ROPE_AXIS // 2

FFN_DIM = 2816
CONV_WIDTH = 3
EPS = 1e-6

kernel_name = 'hybrid_s5_mla_convffn_dit'

def rms_norm(x, g):
    xf = x.astype(jnp.float32)
    y = xf * lax.rsqrt(jnp.mean(xf * xf, axis=-1, keepdims=True) + EPS)
    return (y * g.astype(jnp.float32)).astype(x.dtype)

def adaln(cond, w, b):
    m = jax.nn.silu(cond.astype(jnp.float32)) @ w + b
    return jnp.split(m, 6, axis=-1)

def modulate(h, shift, scale):
    return h * (1.0 + scale) + shift

def s5_discretize(lam_re, lam_im, log_dt, b_re, b_im):
    lam_re = lam_re.astype(jnp.float32)
    lam_im = lam_im.astype(jnp.float32)
    dt = jnp.exp(log_dt.astype(jnp.float32))[:, None]
    mag = jnp.exp(lam_re * dt)
    ang = lam_im * dt
    ab_re = mag * jnp.cos(ang)
    ab_im = mag * jnp.sin(ang)
    den = lam_re * lam_re + lam_im * lam_im
    zr = ab_re - 1.0
    zi = ab_im
    fr = (zr * lam_re + zi * lam_im) / den
    fi = (zi * lam_re - zr * lam_im) / den
    b_re = b_re.astype(jnp.float32)
    b_im = b_im.astype(jnp.float32)
    bb_re = fr[..., None] * b_re - fi[..., None] * b_im
    bb_im = fr[..., None] * b_im + fi[..., None] * b_re
    return ab_re, ab_im, bb_re, bb_im

def _s5_combine(e1, e2):
    a1r, a1i, b1r, b1i = e1
    a2r, a2i, b2r, b2i = e2
    ar = a2r * a1r - a2i * a1i
    ai = a2r * a1i + a2i * a1r
    br = a2r * b1r - a2i * b1i + b2r
    bi = a2r * b1i + a2i * b1r + b2i
    return (ar, ai, br, bi)

def s5_scan(u, h0_re, h0_im, ab_re, ab_im, bb_re, bb_im, c_re, c_im):
    bsz, L, _ = u.shape
    n_chunks = L // S5_CHUNK
    uc = u.reshape(bsz, n_chunks, S5_CHUNK, S5_GROUPS, S5_GROUP).transpose(1, 0, 2, 3, 4)
    full = (bsz, S5_CHUNK, S5_GROUPS, S5_STATE)
    a_re = jnp.broadcast_to(ab_re, full)
    a_im = jnp.broadcast_to(ab_im, full)
    c_re = c_re.astype(jnp.float32)
    c_im = c_im.astype(jnp.float32)

    def chunk_step(carry, xc):
        hr, hi = carry
        bu_r = jnp.einsum('blgc,gpc->blgp', xc, bb_re)
        bu_i = jnp.einsum('blgc,gpc->blgp', xc, bb_im)
        pr, pi, sr, si = lax.associative_scan(_s5_combine, (a_re, a_im, bu_r, bu_i), axis=1)
        h_r = pr * hr[:, None] - pi * hi[:, None] + sr
        h_i = pr * hi[:, None] + pi * hr[:, None] + si
        y = jnp.einsum('blgp,gcp->blgc', h_r, c_re) - jnp.einsum('blgp,gcp->blgc', h_i, c_im)
        return (h_r[:, -1], h_i[:, -1]), y

    (hr, hi), ys = lax.scan(chunk_step, (h0_re, h0_im), uc)
    y = ys.transpose(1, 0, 2, 3, 4).reshape(bsz, L, D_MODEL)
    return y, hr, hi

def _maybe_flip(t, rev):
    return jnp.flip(t, axis=1) if rev else t

def s5_glu(y, glu_w, glu_b):
    z = jax.nn.gelu(y)
    a, g = jnp.split(z @ glu_w + glu_b, 2, axis=-1)
    return a * jax.nn.sigmoid(g)

def s5_mixer(h_lat, h_ctx, lam_re, lam_im, log_dt, b_re, b_im, c_re, c_im, d_skip, glu_w, glu_b, need_ctx):
    u_lat = h_lat.astype(jnp.float32)
    u_ctx = h_ctx.astype(jnp.float32)
    bsz = u_lat.shape[0]
    d32 = d_skip.astype(jnp.float32)
    y_lat = d32 * u_lat
    y_ctx = d32 * u_ctx
    zero = jnp.zeros((bsz, S5_GROUPS, S5_STATE), jnp.float32)
    for d in range(2):
        rev = d == 1
        ab_re, ab_im, bb_re, bb_im = s5_discretize(lam_re[d], lam_im[d], log_dt[d], b_re[d], b_im[d])
        yc, hr, hi = s5_scan(_maybe_flip(u_ctx, rev), zero, zero, ab_re, ab_im, bb_re, bb_im, c_re[d], c_im[d])
        yl, _, _ = s5_scan(_maybe_flip(u_lat, rev), hr, hi, ab_re, ab_im, bb_re, bb_im, c_re[d], c_im[d])
        y_lat = y_lat + _maybe_flip(yl, rev)
        if need_ctx:
            y_ctx = y_ctx + _maybe_flip(yc, rev)
    out_lat = s5_glu(y_lat, glu_w, glu_b).astype(h_lat.dtype)
    out_ctx = s5_glu(y_ctx, glu_w, glu_b).astype(h_ctx.dtype) if need_ctx else None
    return out_lat, out_ctx

def _rotate_half_block(x, cos, sin):
    x1 = x[..., :ROPE_FREQS]
    x2 = x[..., ROPE_FREQS:]
    return jnp.concatenate([x1 * cos - x2 * sin, x1 * sin + x2 * cos], axis=-1)

def axial_rope(x, cos_r, sin_r, cos_c, sin_c):
    return jnp.concatenate([_rotate_half_block(x[..., :ROPE_AXIS], cos_r, sin_r),
                            _rotate_half_block(x[..., ROPE_AXIS:], cos_c, sin_c)], axis=-1)

def mla_queries(h, w_dq, g_q, w_uq, g_qn, g_qr, rope):
    bsz, L, _ = h.shape
    q = (rms_norm(h @ w_dq, g_q) @ w_uq).reshape(bsz, L, MLA_HEADS, MLA_QK_DIM)
    q_nope = rms_norm(q[..., :MLA_NOPE], g_qn)
    q_rope = rms_norm(q[..., MLA_NOPE:], g_qr)
    if rope is not None:
        q_rope = axial_rope(q_rope, *rope)
    return jnp.concatenate([q_nope, q_rope], axis=-1)

def mla_keys_values(h, w_dkv, g_kv, w_ukv, g_kn, g_kr, rope):
    bsz, L, _ = h.shape
    kv = h @ w_dkv
    c_kv = rms_norm(kv[..., :MLA_KV_RANK], g_kv)
    k_rope = rms_norm(kv[..., MLA_KV_RANK:], g_kr)[:, :, None, :]
    if rope is not None:
        k_rope = axial_rope(k_rope, *rope)
    kvu = (c_kv @ w_ukv).reshape(bsz, L, MLA_HEADS, MLA_NOPE + MLA_V)
    k_nope = rms_norm(kvu[..., :MLA_NOPE], g_kn)
    v = kvu[..., MLA_NOPE:]
    k = jnp.concatenate([k_nope, jnp.broadcast_to(k_rope, (bsz, L, MLA_HEADS, MLA_ROPE))], axis=-1)
    return k, v

def block_attention(q, k, v):
    bsz, Lq = q.shape[0], q.shape[1]
    nb = Lq // Q_BLOCK
    qb = q.reshape(bsz, nb, Q_BLOCK, MLA_HEADS, MLA_QK_DIM).transpose(1, 0, 2, 3, 4)

    def one_block(qblk):
        s = jnp.einsum('bqhd,bkhd->bhqk', qblk, k).astype(jnp.float32) * ATTN_SCALE
        p = jax.nn.softmax(s, axis=-1).astype(v.dtype)
        return jnp.einsum('bhqk,bkhd->bqhd', p, v)

    o = lax.map(one_block, qb)
    return o.transpose(1, 0, 2, 3, 4).reshape(bsz, Lq, MLA_HEADS * MLA_V)

def mla_mixer(h_lat, h_ctx, w_dq, g_q, w_uq, w_dkv, g_kv, w_ukv, g_qn, g_qr, g_kn, g_kr, w_o, rope, need_ctx):
    k_ctx, v_ctx = mla_keys_values(h_ctx, w_dkv, g_kv, w_ukv, g_kn, g_kr, None)
    k_lat, v_lat = mla_keys_values(h_lat, w_dkv, g_kv, w_ukv, g_kn, g_kr, rope)
    q_lat = mla_queries(h_lat, w_dq, g_q, w_uq, g_qn, g_qr, rope)
    k_all = jnp.concatenate([k_ctx, k_lat], axis=1)
    v_all = jnp.concatenate([v_ctx, v_lat], axis=1)
    out_lat = block_attention(q_lat, k_all, v_all) @ w_o
    out_ctx = None
    if need_ctx:
        q_ctx = mla_queries(h_ctx, w_dq, g_q, w_uq, g_qn, g_qr, None)
        out_ctx = block_attention(q_ctx, k_ctx, v_ctx) @ w_o
    return out_lat, out_ctx

def conv_ffn(h, w_in, conv_w, conv_b, w_out):
    L = h.shape[1]
    a, b = jnp.split(h @ w_in, 2, axis=-1)
    pad = CONV_WIDTH // 2
    ap = jnp.pad(a, ((0, 0), (pad, pad), (0, 0)))
    conv = conv_b
    for t in range(CONV_WIDTH):
        conv = conv + ap[:, t:t + L] * conv_w[t]
    return (jax.nn.silu(conv) * b) @ w_out

def _normal(key, shape, scale):
    return scale * jax.random.normal(key, shape, jnp.float32)

def _gain(key, shape):
    return 1.0 + 0.05 * jax.random.normal(key, shape, jnp.float32)

def setup_inputs(seed: int = 0) -> dict:
    key = jax.random.key(seed)
    ks = jax.random.split(key, 33)
    D = D_MODEL
    s5_lam_shape = (N_S5_LAYERS, 2, S5_GROUPS, S5_STATE)
    n_idx = jnp.arange(S5_STATE, dtype=jnp.float32)
    return {
        'x': jax.random.normal(ks[0], (BATCH, SEQ, D), jnp.float32),
        'c': jax.random.normal(ks[1], (BATCH, D), jnp.float32),
        'ctx': jax.random.normal(ks[2], (BATCH, CTX_LEN, D), jnp.float32),
        'c_ctx': jax.random.normal(ks[3], (D,), jnp.float32),
        'ada_w': _normal(ks[4], (DEPTH, D, 6 * D), 0.5 * D ** -0.5),
        'ada_b': _normal(ks[5], (DEPTH, 6 * D), 0.01),
        'norm_mix': _gain(ks[6], (DEPTH, D)),
        'norm_ffn': _gain(ks[7], (DEPTH, D)),
        's5_lam_re': -0.5 + _normal(ks[8], s5_lam_shape, 0.01),
        's5_lam_im': jnp.pi * n_idx + _normal(ks[9], s5_lam_shape, 0.01),
        's5_log_dt': jax.random.uniform(ks[10], (N_S5_LAYERS, 2, S5_GROUPS), jnp.float32,
                                        minval=math.log(S5_DT_MIN), maxval=math.log(S5_DT_MAX)),
        's5_b_re': _normal(ks[11], (N_S5_LAYERS, 2, S5_GROUPS, S5_STATE, S5_GROUP), (2.0 * S5_GROUP) ** -0.5),
        's5_b_im': _normal(ks[12], (N_S5_LAYERS, 2, S5_GROUPS, S5_STATE, S5_GROUP), (2.0 * S5_GROUP) ** -0.5),
        's5_c_re': _normal(ks[13], (N_S5_LAYERS, 2, S5_GROUPS, S5_GROUP, S5_STATE), (2.0 * S5_STATE) ** -0.5),
        's5_c_im': _normal(ks[14], (N_S5_LAYERS, 2, S5_GROUPS, S5_GROUP, S5_STATE), (2.0 * S5_STATE) ** -0.5),
        's5_d': _normal(ks[15], (N_S5_LAYERS, D), 1.0),
        's5_glu_w': _normal(ks[16], (N_S5_LAYERS, D, 2 * D), D ** -0.5),
        's5_glu_b': _normal(ks[17], (N_S5_LAYERS, 2 * D), 0.01),
        'mla_w_dq': _normal(ks[18], (N_MLA_LAYERS, D, MLA_Q_RANK), D ** -0.5),
        'mla_g_q': _gain(ks[19], (N_MLA_LAYERS, MLA_Q_RANK)),
        'mla_w_uq': _normal(ks[20], (N_MLA_LAYERS, MLA_Q_RANK, MLA_HEADS * MLA_QK_DIM), MLA_Q_RANK ** -0.5),
        'mla_w_dkv': _normal(ks[21], (N_MLA_LAYERS, D, MLA_KV_RANK + MLA_ROPE), D ** -0.5),
        'mla_g_kv': _gain(ks[22], (N_MLA_LAYERS, MLA_KV_RANK)),
        'mla_w_ukv': _normal(ks[23], (N_MLA_LAYERS, MLA_KV_RANK, MLA_HEADS * (MLA_NOPE + MLA_V)), MLA_KV_RANK ** -0.5),
        'mla_g_qn': _gain(ks[24], (N_MLA_LAYERS, MLA_NOPE)),
        'mla_g_qr': _gain(ks[25], (N_MLA_LAYERS, MLA_ROPE)),
        'mla_g_kn': _gain(ks[26], (N_MLA_LAYERS, MLA_NOPE)),
        'mla_g_kr': _gain(ks[27], (N_MLA_LAYERS, MLA_ROPE)),
        'mla_w_o': _normal(ks[28], (N_MLA_LAYERS, MLA_HEADS * MLA_V, D), (MLA_HEADS * MLA_V) ** -0.5),
        'ffn_w_in': _normal(ks[29], (DEPTH, D, 2 * FFN_DIM), D ** -0.5),
        'ffn_conv_w': _normal(ks[30], (DEPTH, CONV_WIDTH, FFN_DIM), CONV_WIDTH ** -0.5),
        'ffn_conv_b': _normal(ks[31], (DEPTH, FFN_DIM), 0.01),
        'ffn_w_out': _normal(ks[32], (DEPTH, FFN_DIM, D), FFN_DIM ** -0.5),
    }

def reference(x, c, ctx, c_ctx, ada_w, ada_b, norm_mix, norm_ffn,
              s5_lam_re, s5_lam_im, s5_log_dt, s5_b_re, s5_b_im, s5_c_re, s5_c_im, s5_d, s5_glu_w, s5_glu_b,
              mla_w_dq, mla_g_q, mla_w_uq, mla_w_dkv, mla_g_kv, mla_w_ukv, mla_g_qn, mla_g_qr, mla_g_kn, mla_g_kr, mla_w_o,
              ffn_w_in, ffn_conv_w, ffn_conv_b, ffn_w_out):
    L = x.shape[1]
    ROWS = L // GRID_W
    rows = jnp.repeat(jnp.arange(ROWS, dtype=jnp.int32), GRID_W)
    cols = jnp.tile(jnp.arange(GRID_W, dtype=jnp.int32), ROWS)
    inv_freq = ROPE_BASE ** (-jnp.arange(ROPE_FREQS, dtype=jnp.float32) / ROPE_FREQS)
    ang_r = rows.astype(jnp.float32)[:, None] * inv_freq
    ang_c = cols.astype(jnp.float32)[:, None] * inv_freq
    rope = (jnp.cos(ang_r)[:, None, :], jnp.sin(ang_r)[:, None, :],
            jnp.cos(ang_c)[:, None, :], jnp.sin(ang_c)[:, None, :])

    for i in range(DEPTH):
        last = i == DEPTH - 1
        need_ctx = not last
        j = i // N_MIXERS
        sh_m, sc_m, g_m, sh_f, sc_f, g_f = adaln(c[:, None, :], ada_w[i], ada_b[i])
        csh_m, csc_m, cg_m, csh_f, csc_f, cg_f = adaln(c_ctx[None, None, :], ada_w[i], ada_b[i])
        hx = modulate(rms_norm(x, norm_mix[i]), sh_m, sc_m)
        hc = modulate(rms_norm(ctx, norm_mix[i]), csh_m, csc_m)
        if i % N_MIXERS == 0:
            y_lat, y_ctx = s5_mixer(hx, hc, s5_lam_re[j], s5_lam_im[j], s5_log_dt[j], s5_b_re[j], s5_b_im[j],
                                    s5_c_re[j], s5_c_im[j], s5_d[j], s5_glu_w[j], s5_glu_b[j], need_ctx)
        else:
            y_lat, y_ctx = mla_mixer(hx, hc, mla_w_dq[j], mla_g_q[j], mla_w_uq[j], mla_w_dkv[j], mla_g_kv[j],
                                     mla_w_ukv[j], mla_g_qn[j], mla_g_qr[j], mla_g_kn[j], mla_g_kr[j], mla_w_o[j],
                                     rope, need_ctx)
        x = x + g_m * y_lat
        hx = modulate(rms_norm(x, norm_ffn[i]), sh_f, sc_f)
        x = x + g_f * conv_ffn(hx, ffn_w_in[i], ffn_conv_w[i], ffn_conv_b[i], ffn_w_out[i])
        if need_ctx:
            ctx = ctx + cg_m * y_ctx
            hc = modulate(rms_norm(ctx, norm_ffn[i]), csh_f, csc_f)
            ctx = ctx + cg_f * conv_ffn(hc, ffn_w_in[i], ffn_conv_w[i], ffn_conv_b[i], ffn_w_out[i])
    return x


_drawn_inputs = setup_inputs


def setup_inputs(seed=0):
    import zlib

    import numpy as np

    out = dict(_drawn_inputs(seed))
    spreads = {}
    factors = {'ctx': 5.655,
     'ada_b': 4.437,
     'norm_mix': 7.445,
     's5_lam_re': 64.0,
     's5_lam_im': 37.12,
     's5_log_dt': 42.752,
     's5_b_re': 54.336,
     's5_b_im': 52.448,
     's5_c_re': 52.384,
     's5_c_im': 51.0,
     's5_glu_b': 8.0,
     'mla_g_q': 8.0,
     'mla_g_kv': 8.0,
     'mla_g_qn': 8.0,
     'mla_g_qr': 8.0,
     'mla_g_kn': 8.0,
     'mla_g_kr': 8.0,
     'ffn_conv_b': 8.0}
    for name, (base, spread) in spreads.items():
        noise = np.random.default_rng([zlib.crc32(name.encode()), seed]).standard_normal(out[name].shape)
        drawn = base * np.exp(spread * noise) if base else spread * noise
        out[name] = jnp.asarray(drawn.astype(out[name].dtype))
    for name, factor in factors.items():
        out[name] = (out[name] * factor).astype(out[name].dtype)
    return out
```

```python
from contextlib import ExitStack

import numpy as np

import concourse.bass as bass
from concourse import mybir

F32 = mybir.dt.float32
F32R = mybir.dt.float32r
ALU = mybir.AluOpType
ACT = mybir.ActivationFunctionType
AX = mybir.AxisListType

P = 128
D = 1024
KD = D // P
NLAT, NCTX = 512, 256
T = NLAT + NCTX
EPS = 1e-6
GROUPS, CH, STATES, CK = 64, 16, 64, 8
GP = GROUPS // 2
JCTX, JLAT = NCTX // CK, NLAT // CK
J = JCTX + JLAT
DG = 2 * GP
HEADS, NOPE, ROPE, VD, QR, KVR = 8, 128, 64, 128, 768, 256
SCALE = 1.0 / float(np.sqrt(NOPE + ROPE))
FFN = 2816
KF = FFN // P
GF = KF // 2
SLOT = 2 * KD * P
ADA_CHUNKS = 6 * D // 256
TWO_PI_HI, TWO_PI_LO = 6.28125, 0.0019353071795864769
ROUND = 12582912.0
PI = 3.1415925

TAB_IDENT, TAB_SWAP, TAB_HALF, TAB_COS, TAB_SIN = 0, P, 2 * P, 3 * P, 3 * P + NLAT
TAB_N = 3 * P + 2 * NLAT

C_ADAB, C_NMIX, C_NFFN = 0, 96, 112
C_C, C_CC, C_GLUB, C_GQ, C_GKV, C_GQN, C_GKN, C_GQR, C_GKR, C_CONVB = 0, 8, 16, 32, 38, 40, 41, 42, 43, 44
SH_M, SC_M, G_M, SH_F, SC_F, G_F = 0, 8, 16, 24, 32, 40


class Chain:

    def __init__(self, eng, sem):
        self.eng, self.sem, self.count, self.turn, self.per = eng, sem, 0, None, 0

    def mark(self, op):
        op.then_inc(self.sem, 1)
        self.count += 1

    def need(self, back):
        n = self.count - back
        self.eng.wait_ge(self.sem, n if self.turn is None else self.turn * self.per + n)

    def link(self, op):
        self.mark(op)
        self.need(0)

    def enter(self, turn, per):
        self.turn, self.per, self.start = turn, per, self.count

    def leave(self, turns):
        assert self.count - self.start == self.per, (self.count - self.start, self.per)
        self.count, self.turn = self.start + self.per * turns, None


B_GLU = 2 * ADA_CHUNKS
B_FFN = (B_GLU + KD, B_GLU + KD + 2 * (GF + KD) + 3 + 6 + 4 + 12 + KD)
B_DKV = B_FFN[0] + 2 * (GF + KD)
B_DQ = B_DKV + 3
B_UKV = B_DQ + QR // P
B_UQ = B_UKV + 4
B_WO = B_UQ + HEADS + HEADS // 2
KV_USES = (4, 4, 6, 6)


JOB_UNITS = (2, 3) + tuple(range(9, 30))


def used_after(c):
    return c + 1 + sum(n - 1 for n in KV_USES[:max(0, c + 1 - B_UKV)])


class Chunk:

    def __init__(self, first, turn=None):
        step = 0 if turn is None else 2 * turn
        self.slot = first % 2
        self.reuse = first >= 2 or turn is not None
        self.n = first + step
        self.nth = first // 2 + (0 if turn is None else turn)
        self.done = used_after(first) + step
        self.free = used_after(first - 2) + step
        self.drains = self.done - B_GLU


def stage_turns(eng, count, split, epi):
    split(0, None)
    for m in range(2):
        split(m + 1, None)
        epi(m, m, None)
    pairs = (count - 3) // 2
    if pairs > 0:
        with eng.Fori(1, 1 + pairs) as i:
            for m in range(2):
                split(m + 1, i)
                epi(2 * i + m, m, i)
    for m in range(2 + 2 * max(pairs, 0), count - 1):
        split(m + 1, None)
        epi(m, m, None)
    epi(count - 1, count - 1, None)


def chunk_turns(eng, count, one):
    for m in range(2):
        one(m, m, None)
    if count >= 4:
        with eng.Fori(1, count // 2) as i:
            for m in range(2):
                one(2 * i + m, m, i)
    if count % 2:
        one(count - 1, count - 1, None)


def build(nc, a):
    with ExitStack() as ctx:
        def sb(name, shape, dt=F32, stack=None):
            return (stack or ctx).enter_context(nc.sbuf_tensor(name, shape, dt))

        def sem(name):
            return ctx.enter_context(nc.semaphore(name))

        wraw = sb("wraw", [P, 2, SLOT])
        ident = sb("ident", [P, P])
        ones = sb("ones", [P, P])
        swap = sb("swap", [P, P])
        half_ones = sb("half_ones", [P, P])
        colsA = sb("colsA", [P, 128])
        colsB = sb("colsB", [P, 88])
        colsW = sb("colsW", [P, 2, 66])
        modc = sb("modc", [P, 2, 48, 2])
        gain = sb("gain", [P, 2, 2, KD, 2])
        cond_r = sb("cond_r", [P, KD, 4], F32R)
        eps = sb("eps", [P, 1])
        wt = sb("wt", [P, 1])
        zero = sb("zero", [P, 1])

        s5 = ExitStack()
        Mr = sb("Mr", [P, 2, 2, 4, P], stack=s5)
        Nr = sb("Nr", [P, 2, 2, 4, P], stack=s5)
        MT = sb("MT", [P, 2, 4, P], stack=s5)
        Kext = sb("Kext", [CH, 4, 15, CH], stack=s5)
        tD = sb("tD", [P, 2, 4, CK, CH], stack=s5)
        tP = sb("tP", [P, 2, 4, CK, CH], stack=s5)
        sb("s5_pad", [P, 64], stack=s5)
        Sarr = sb("Sarr", [P, J + 1, 2, 2, GP], stack=s5)
        TT = sb("TT", [P, GROUPS, P], stack=s5)
        Bc = sb("Bc", [P, 2, DG, CH], stack=s5)
        Cc = sb("Cc", [P, 2, DG, CH], stack=s5)
        pw = sb("pw", [P, 2, DG, 9], stack=s5)
        Qk = sb("Qk", [P, 2, DG, CK], stack=s5)
        Pk = sb("Pk", [P, 2, DG, CK], stack=s5)
        Pn = sb("Pn", [P, 2, DG, CK], stack=s5)
        U = sb("U", [P, GROUPS, J], stack=s5)
        s5.close()
        pre = ExitStack()
        sb("pre_gap", [P, 4 * SLOT], stack=pre)
        rowsA = sb("rowsA", [P, P], stack=pre)
        rowsB = sb("rowsB", [88, P], stack=pre)
        rowsW = sb("rowsW", [66, 2, P], stack=pre)
        lam = sb("lam", [DG, 2, P], stack=pre)
        ldt = sb("ldt", [DG, 2], stack=pre)
        brow = sb("brow", [DG, 2, 2048], stack=pre)
        crow = sb("crow", [DG, 2, 2048], stack=pre)
        disc = sb("disc", [DG, 12, P], stack=pre)
        sc4 = sb("sc4", [P, 8, CK * 4], stack=pre)
        sgc = sb("sgc", [P, 16], stack=pre)
        drow = sb("drow", [GROUPS, CH], stack=pre)
        cs = sb("cs", [P, 16], stack=pre)
        pre.close()
        pre3 = ExitStack()
        sb("pre3_gap", [P, 4 * SLOT], stack=pre3)
        xn = sb("xn", [J, GROUPS, CK, CH], stack=pre3)
        pre3.close()
        pre2 = ExitStack()
        sb("pre2_gap", [P, 4 * SLOT + (J + 1) * P], stack=pre2)
        xin = sb("xin", [J, CK, D], stack=pre2)
        pre2.close()
        late = ExitStack()
        sb("late_gap", [P, 4 * SLOT + (J + 1) * P + GROUPS * P + 2 * 2 * DG * CH + 2 * DG * 9 + 6 * DG * CK + GROUPS * J],
           stack=late)
        acoef = sb("acoef", [P, 4, DG], stack=late)
        cm = sb("cm", [P, 2, DG, 8], stack=late)
        stat = sb("stat", [J, 2, CK], stack=late)
        urep = sb("urep", [P, 2, 2, GROUPS], stack=late)
        kd = sb("kd", [CH, GROUPS, CH], stack=late)
        d16 = sb("d16", [CH, GROUPS], stack=late)
        a8 = sb("a8", [P, 2, 2, 2, GP], stack=late)
        scF = sb("scF", [P, 3, 2, GP], stack=late)
        scB = sb("scB", [P, 3, 2, GP], stack=late)
        pick = sb("pick", [P, KD, CK, CH], stack=late)
        yst = pick[0:J].rearrange("j a k c -> j (a k c)").rearrange("j (k n) -> j k n", k=CK)
        late.close()

        whi = sb("whi", [P, 2, SLOT], F32R)
        wlo = sb("wlo", [P, 2, SLOT], F32R)
        kv = ExitStack()
        kn = sb("kn", [P, HEADS, T], stack=kv)
        val = sb("val", [P, 6, HEADS * VD], stack=kv)
        kv.close()
        hhi = sb("hhi", [P, KD, T], F32R)
        hlo = sb("hlo", [P, KD, T], F32R)
        xT = sb("xT", [P, KD, T])
        ffn = ExitStack()
        ghi = sb("ghi", [P, GF, T], F32R, stack=ffn)
        glo = sb("glo", [P, GF, T], F32R, stack=ffn)
        acc = sb("acc", [P, 2, T], stack=ffn)
        ffn.close()
        nrm = ExitStack()
        sq = sb("sq", [P, KD, T], stack=nrm)
        ssum = sb("ssum", [P, T], stack=nrm)
        rstd = sb("rstd", [P, T], stack=nrm)
        hx = sb("hx", [P, 2, T], stack=nrm)
        nrm.close()
        mla = ExitStack()
        q_all = sb("q_all", [P, 12, NLAT], stack=mla)
        kr = sb("kr", [P, T], stack=mla)
        rope_cs = sb("rope_cs", [P, 2, NLAT], stack=mla)
        rs = sb("rs", [P, T], stack=mla)
        ckv_hi = sb("ckv_hi", [P, 2, T], F32R, stack=mla)
        ckv_lo = sb("ckv_lo", [P, 2, T], F32R, stack=mla)
        cq_hi = sb("cq_hi", [P, 6, NLAT], F32R, stack=mla)
        cq_lo = sb("cq_lo", [P, 6, NLAT], F32R, stack=mla)
        sqr = sb("sqr", [P, 2, T], stack=mla)
        mla.close()
        raw = ExitStack()
        ckv_raw = sb("ckv_raw", [P, 2, T], stack=raw)
        cq_raw = sb("cq_raw", [P, 6, NLAT], stack=raw)
        raw.close()
        att = ExitStack()
        sb("att_gap", [P, 12 * NLAT + T + 2 * NLAT + T], stack=att)
        pr = sb("pr", [P, 2, T], stack=att)
        pT = sb("pT", [P, 2, 6, NLAT], stack=att)
        ot = sb("ot", [P, HEADS, NLAT], stack=att)
        smax = sb("smax", [P, 2, 4], stack=att)
        att.close()
        glu = ExitStack()
        xin2 = sb("xin2", [J, CK, D], stack=glu)
        glu.close()
        glu2 = ExitStack()
        sb("glu2_gap", [P, 2 * GF * T], stack=glu2)
        sig = sb("sig", [P, 2, T], stack=glu2)
        glu2.close()

        ps = ctx.enter_context(nc.psum_tensor("ps", [P, 8, 512], F32))
        flat = ps[:].rearrange("p b n -> p (b n)")

        names = """params_in s5rows_in d16_in x_in tabs_in const_set cols_T cols_out cond_ready act_link dve_link pool_link
            wload0 wload1 hi_ready lo_ready w_used drained
            rowsum_done rstd_set dt_set disc_a disc_b exp_done sin_done disc_T disc_out bc_T bc_out tab_set
            ada0_set rep_done rep_out u_T u_mul u_add kd_set
            m_ready n_ready mt_T mt_out k_done kf_out kext_ready tt_in s_done sf_out sb_out s_zero
            scanF scanB pn_set n2m n2_re n2_im y_done y_out z_T z_out z_hi z_lo x2_in xT_T xT_out
            sig_done act_acc dve_g hi_g g_split mix_done
            sq_done ssum_done stat_T std_done rinv xn_done hx_done h_hi h_lo
            acc_set conv_done silu_done g_done g_hi g_lo rope_in
            unit_sq unit_used job_std ckv_set cq_set swap_T rot_done job_rinv job_out ckv_hi_s ckv_lo_s cq_hi_s cq_lo_s kr_swap kr_set q_swap q_set
            kv_out sc_done mx_set ex_done pr_set p_T pT_out pv_done ot_out o_hi o_lo
            fin_T fin_out out_done ssum_set""".split()
        S = {n: sem(n) for n in names}
        wload = (S["wload0"], S["wload1"])

        def wview(t, slot, k, n=P):
            return t[:, slot, 0:k * n].rearrange("p (k n) -> p k n", k=k)

        def glu_psum(q):
            return ps[:, 3 * q, :], ps[:, 3 * q + 1, :], ps[:, 3 * q + 2, 0:NCTX], ps[:, 3 * q + 2, NCTX:2 * NCTX]

        def hhi_out(t):
            return sq[:].rearrange("p k t -> p (k t)")[:, t * D:(t + 1) * D]

        block = ctx.enter_context(nc.Block())

        @block.sync
        def _(sp):
            sp.dma_start(rowsB[C_C:C_C + 8, :], a["c"].rearrange("o (r c) -> (o r) c", c=P)).then_inc(S["params_in"], 16)
            sp.dma_start(rowsB[C_CC:C_CC + 8, :], a["c_ctx"].rearrange("(r c) -> r c", c=P)).then_inc(S["params_in"], 16)
            sp.dma_start(rowsA[0:96, :], a["ada_b"].rearrange("l (r c) -> (l r) c", c=P)).then_inc(S["params_in"], 16)
            sp.dma_start(rowsA[96:112, :], a["norm_mix"].rearrange("l (r c) -> (l r) c", c=P)).then_inc(S["params_in"], 16)
            sp.dma_start(rowsA[112:128, :], a["norm_ffn"].rearrange("l (r c) -> (l r) c", c=P)).then_inc(S["params_in"], 16)
            for at, name in ((C_GLUB, "s5_glu_b"), (C_GQ, "mla_g_q"), (C_GKV, "mla_g_kv"), (C_GQN, "mla_g_qn"),
                             (C_GKN, "mla_g_kn"), (C_CONVB, "ffn_conv_b")):
                src = a[name].rearrange("l (r c) -> (l r) c", c=P)
                sp.dma_start(rowsB[at:at + src.shape[0], :], src).then_inc(S["params_in"], 16)
            for at, name in ((C_GQR, "mla_g_qr"), (C_GKR, "mla_g_kr")):
                for h in range(2):
                    sp.dma_start(rowsB[at:at + 1, h * ROPE:(h + 1) * ROPE], a[name]).then_inc(S["params_in"], 16)
            for l in range(2):
                sp.dma_start(rowsW[:, l, :], a["ffn_conv_w"][l].rearrange("t (r c) -> (t r) c", c=P))\
                    .then_inc(S["params_in"], 16)
            for t, at in ((ident, TAB_IDENT), (swap, TAB_SWAP), (half_ones, TAB_HALF)):
                sp.dma_start(t[:], a["tabs"][:, at:at + P]).then_inc(S["params_in"], 16)
            rows = "o d (g h) s -> (o d g) (h s)"
            sp.dma_start(lam[:, 0, :], a["s5_lam_re"].rearrange(rows, h=2)).then_inc(S["s5rows_in"], 16)
            sp.dma_start(lam[:, 1, :], a["s5_lam_im"].rearrange(rows, h=2)).then_inc(S["s5rows_in"], 16)
            sp.dma_start(ldt[:], a["s5_log_dt"].rearrange("o d (g h) -> (o d g) h", h=2)).then_inc(S["s5rows_in"], 16)
            for q, name in ((0, "s5_b_re"), (1, "s5_b_im")):
                sp.dma_start(brow[:, q, :], a[name].rearrange("o d (g h) x y -> (o d g) (h x y)", h=2))\
                    .then_inc(S["s5rows_in"], 16)
            for q, name in ((0, "s5_c_re"), (1, "s5_c_im")):
                for h in range(2):
                    sp.dma_start(crow[:, q, :].rearrange("p (c h s) -> p h c s", h=2, c=CH)[:, h],
                                 a[name].rearrange("o d (g h) c s -> (o d g) h c s", h=2)[:, h]).then_inc(S["s5rows_in"], 16)
            sp.dma_start(drow[:], a["s5_d"].rearrange("o (g c) -> (o g) c", c=CH)).then_inc(S["params_in"], 16)
            sp.wait_ge(S["bc_out"], 16)
            sp.wait_ge(S["disc_out"], 1)
            for dst, src in ((xin[0:JCTX], a["ctx"]), (xin[JCTX:J], a["x"])):
                sp.dma_start(dst, src.rearrange("o (j k) d -> (o j) k d", k=CK)).then_inc(S["x_in"], 16)

            def load(ch, dst_n, src):
                if ch.reuse:
                    sp.wait_ge(S["lo_ready"], ch.n - 1)
                sp.dma_start(dst_n, src).then_inc(wload[ch.slot], 32)

            def stream(first, count, k, n, src):
                for m in range(2):
                    load(Chunk(first + m), wview(wraw, (first + m) % 2, k, n), src(m))
                if count > 2:
                    with sp.Fori(1, count // 2) as i:
                        for m in range(2):
                            ch = Chunk(first + m, i)
                            load(ch, wview(wraw, ch.slot, k, n), src(2 * i + m))

            for l in range(2):
                w = a["ada_w"][l].rearrange("(k p) n -> p k n", p=P)
                stream(l * ADA_CHUNKS, ADA_CHUNKS, KD, 256, lambda m, w=w: w[:, :, bass.ds(m * 256, 256)])

            def toeplitz(b, n):
                sp.wait_ge(S["kext_ready"], n + 1)
                for k in range(CK):
                    sp.dma_start(TT[CH * k:CH * (k + 1), bass.ds(4 * b, 4), :],
                                 Kext[:, :, CK - 1 - k:2 * CK - 1 - k, :].rearrange("c g t o -> c g (t o)"))\
                        .then_inc(S["tt_in"], 16)

            with sp.Fori(0, GP // 2) as b:
                toeplitz(b, b)

            sp.wait_ge(S["z_out"], 2 * KD)
            for dst, src in ((xin2[0:JCTX], a["ctx"]), (xin2[JCTX:J], a["x"])):
                sp.dma_start(dst, src.rearrange("o (j k) d -> (o j) k d", k=CK)).then_inc(S["x2_in"], 16)

            def stage(first, count, fill):
                def one(m, c, turn):
                    ch = Chunk(first + c, turn)
                    sp.wait_ge(S["lo_ready"], ch.n - 1)
                    moves = fill(ch.slot, m)
                    for dst, src in moves:
                        sp.dma_start(dst, src).then_inc(wload[ch.slot], 32 // len(moves))
                chunk_turns(sp, count, one)

            def half(w):
                v = w.rearrange("(k p) (h n) -> p k h n", p=P, h=2)
                return lambda slot, m: [(wraw[:, slot, :].rearrange("p (h k n) -> p h k n", h=2, n=P)[:, h],
                                         v[:, :, h, bass.ds(m * P, P)]) for h in range(2)]

            def whole(w):
                v = w.rearrange("(k p) n -> p k n", p=P)
                return lambda slot, m: [(wview(wraw, slot, w.shape[0] // P), v[:, :, bass.ds(m * P, P)])]

            stage(B_GLU, KD, half(a["s5_glu_w"][0]))

            def ffn_weights(l):
                for g in range(2):
                    wi = a["ffn_w_in"][l].rearrange("(k p) (h n) -> p k h n", p=P, h=2)[:, :, :, g * GF * P:(g + 1) * GF * P]
                    stage(B_FFN[l] + g * (GF + KD), GF, lambda slot, m: [
                        (wraw[:, slot, :].rearrange("p (h k n) -> p h k n", h=2, n=P)[:, h],
                         wi[:, :, h, bass.ds(m * P, P)]) for h in range(2)])
                    stage(B_FFN[l] + g * (GF + KD) + GF, KD, whole(a["ffn_w_out"][l][g * GF * P:(g + 1) * GF * P, :]))

            ffn_weights(0)
            dkv = a["mla_w_dkv"][0].rearrange("(k p) n -> p k n", p=P)
            stage(B_DKV, 3, lambda slot, m: [(wview(wraw, slot, KD), dkv[:, :, m * P:(m + 1) * P])] if m < 2 else
                  [(wview(wraw, slot, KD)[:, :, ROPE * h:ROPE * (h + 1)], dkv[:, :, KVR:]) for h in range(2)])
            stage(B_DQ, QR // P, whole(a["mla_w_dq"][0]))
            ukv = a["mla_w_ukv"][0].rearrange("(k p) (h v n) -> p k v h n", p=P, h=HEADS, v=2)
            for m in range(4):
                ch = Chunk(B_UKV + m)
                sp.wait_ge(S["lo_ready"], ch.n - 1)
                for k in range(2):
                    sp.dma_start(wview(wraw, ch.slot, 2, 4 * P)[:, k, :].rearrange("p (h n) -> p h n", h=4),
                                 ukv[:, k, m // 2, 4 * (m % 2):4 * (m % 2) + 4, :]).then_inc(wload[ch.slot], 16)
            uq = a["mla_w_uq"][0].rearrange("(k p) (h n) -> p k h n", p=P, h=HEADS)
            stage(B_UQ, HEADS, lambda slot, m: [(wview(wraw, slot, 6),
                                                 uq[:, :, bass.ds(m, 1), 0:NOPE].rearrange("p k o n -> p k (o n)"))])
            for m in range(HEADS // 2):
                ch = Chunk(B_UQ + HEADS + m)
                sp.wait_ge(S["lo_ready"], ch.n - 1)
                for h in range(2):
                    sp.dma_start(wview(wraw, ch.slot, 6)[:, :, ROPE * h:ROPE * (h + 1)], uq[:, :, 2 * m + h, NOPE:])\
                        .then_inc(wload[ch.slot], 16)
                if m == 0:
                    sp.wait_ge(S["h_lo"], 2 * KD)
                    sp.dma_start(rope_cs[:].rearrange("p a t -> p (a t)"), a["tabs"][:, TAB_COS:]).then_inc(S["rope_in"], 16)
            stage(B_WO, KD, whole(a["mla_w_o"][0]))
            ffn_weights(1)

            sp.wait_ge(S["fin_out"], 8)
            sp.wait_ge(S["out_done"], 16 * 4)

        @block.gpsimd
        def _(pool):
            chain = Chain(pool, S["pool_link"])
            pool.wait_ge(S["params_in"], 16 * 21)
            pool.tensor_copy(pick[:], ident[:].rearrange("p (g c) -> p g c", c=CH).unsqueeze(2)
                             .to_broadcast([P, KD, CK, CH])).then_inc(S["tabs_in"], 1)
            for q in range(GROUPS // 4):
                pool.wait_ge(S["u_mul"], q + 1)
                for j0, j1, cond in ((0, JCTX, 1), (JCTX, J, 0)):
                    v = U[:, 4 * q:4 * q + 4, j0:j1]
                    last = pool.tensor_tensor(v, v, urep[:, 1, cond, 4 * q:4 * q + 4].unsqueeze(2)
                                              .to_broadcast([P, 4, j1 - j0]), ALU.add)
                last.then_inc(S["u_add"], 1)

            def n_block(b, q, n):
                dg = bass.ds(4 * b, 4)
                if n is not None:
                    pool.wait_ge(S["n_ready"], n + 1)
                    pool.wait_ge(S["k_done"], n)
                    pool.tensor_tensor(wt[:], zero[:], zero[:], ALU.add)
                p_re, p_im = (Pk[:, r, dg, :].unsqueeze(3).to_broadcast([P, 4, CK, CH]) for r in range(2))
                c_re, c_ni = (Cc[:, r, dg, :].unsqueeze(2).to_broadcast([P, 4, CK, CH]) for r in range(2))
                dst = [Nr[:, q, r].rearrange("p g (k c) -> p g k c", k=CK) for r in range(2)]
                pool.tensor_tensor(dst[0], p_re, c_re, ALU.mult)
                pool.tensor_tensor(tP[:, 0], p_im, c_ni, ALU.mult)
                pool.tensor_tensor(dst[1], p_re, c_ni, ALU.mult)
                chain.link(pool.tensor_tensor(tP[:, 1], p_im, c_re, ALU.mult))
                pool.tensor_tensor(dst[0], dst[0], tP[:, 0], ALU.add)
                pool.tensor_tensor(dst[1], dst[1], tP[:, 1], ALU.subtract).then_inc(S["n_ready"], 1)

            pool.wait_ge(S["tab_set"], 1)
            pool.wait_ge(S["w_used"], 2 * ADA_CHUNKS)
            for q in range(2):
                n_block(q, q, None)
                if q == 0:
                    pool.wait_ge(S["n_ready"], 1)
            with pool.Fori(1, GP // 4) as i:
                chain.enter(i - 1, 2)
                for q in range(2):
                    n_block(2 * i + q, q, 2 * i + q - 1)
            chain.leave(GP // 4 - 1)

            pool.wait_ge(S["n_ready"], GP // 2)
            pool.wait_ge(S["scanF"], 2)
            for hb in range(GP // 2):
                dg = slice(4 * hb, 4 * hb + 4)
                p_re, p_im = (Pn[:, r, dg, :].unsqueeze(3).to_broadcast([P, 4, CK, CH]) for r in range(2))
                c_re, c_ni = (Cc[:, r, dg, :].unsqueeze(2).to_broadcast([P, 4, CK, CH]) for r in range(2))
                if hb >= 2:
                    pool.wait_ge(S["y_done"], hb - 1)
                pool.tensor_tensor(tP[:, 0], p_re, c_ni, ALU.mult)
                chain.link(pool.tensor_tensor(tP[:, 1], p_im, c_re, ALU.mult))
                pool.tensor_tensor(Nr[:, hb % 2, 1].rearrange("p g (k c) -> p g k c", k=CK),
                                   tP[:, 0], tP[:, 1], ALU.subtract).then_inc(S["n2_im"], 1)
                pool.wait_ge(S["n2_im"], hb + 1)
            for b in range(KD):
                pool.wait_ge(S["z_hi"], b + 1)
                pool.tensor_tensor(hlo[:, b, :], U[:].rearrange("p g j -> p (g j)")[:, T * b:T * b + T],
                                   hhi[:, b, :].bitcast(F32), ALU.subtract).then_inc(S["z_lo"], 1)

            def norm_low(j, toks):
                for b in range(KD):
                    n = KD * j + b + 1
                    pool.wait_ge(S["h_hi"], n)
                    pool.tensor_tensor(hlo[:, b, 0:toks], hx[:, b % 2, 0:toks], hhi[:, b, 0:toks].bitcast(F32),
                                       ALU.subtract).then_inc(S["h_lo"], 1)

            def ffn_low(l, toks):
                for g in range(2):
                    def one(m, c, turn):
                        ch = Chunk(B_FFN[l] + g * (GF + KD) + c, turn)
                        f = KF * l + GF * g + m
                        if l or g or turn is not None or c:
                            pool.wait_ge(S["g_lo"], f)
                        pool.wait_ge(S["g_hi"], f + 1)
                        pool.tensor_tensor(wt[:], zero[:], zero[:], ALU.add)
                        pool.tensor_tensor(glo[:, bass.ds(m, 1), 0:toks].rearrange("p a t -> p (a t)"), acc[:, ch.slot, 0:toks],
                                           ghi[:, bass.ds(m, 1), 0:toks].bitcast(F32).rearrange("p a t -> p (a t)"),
                                           ALU.subtract).then_inc(S["g_lo"], 1)
                    chunk_turns(pool, GF, one)

            norm_low(0, T)
            ffn_low(0, T)
            norm_low(1, T)
            for b in range(2):
                pool.wait_ge(S["ckv_hi_s"], b + 1)
                pool.tensor_tensor(ckv_lo[:, b, :], ckv_raw[:, b, :], ckv_hi[:, b, :].bitcast(F32), ALU.subtract)\
                    .then_inc(S["ckv_lo_s"], 1)
            for b in range(6):
                pool.wait_ge(S["cq_hi_s"], b + 1)
                pool.tensor_tensor(cq_lo[:, b, :], cq_raw[:, b, :], cq_hi[:, b, :].bitcast(F32), ALU.subtract)\
                    .then_inc(S["cq_lo_s"], 1)
            for h in range(HEADS):
                pool.wait_ge(S["o_hi"], h + 1)
                pool.tensor_tensor(hlo[:, h, 0:NLAT], ot[:, h, :], hhi[:, h, 0:NLAT].bitcast(F32), ALU.subtract)\
                    .then_inc(S["o_lo"], 1)
            norm_low(2, NLAT)
            ffn_low(1, NLAT)

        @block.scalar
        def _(act):
            chain = Chain(act, S["act_link"])
            act.wait_ge(S["const_set"], 3)
            act.wait_ge(S["cols_T"], 1)
            act.activation(colsB[:], flat[:, 128:216], ACT.Copy).then_inc(S["cols_out"], 1)
            act.activation(colsA[:], flat[:, 0:128], ACT.Copy).then_inc(S["cols_out"], 1)
            act.activation(colsW[:], flat[:, 256:388], ACT.Copy).then_inc(S["cols_out"], 1)
            act.activation(d16[:], flat[0:CH, 400:464], ACT.Copy).then_inc(S["cols_out"], 1)
            act.wait_ge(S["cols_out"], 4)
            chain.link(act.activation(sgc[:], colsB[:, 0:16], ACT.Sigmoid))
            act.wait_ge(S["const_set"], 4)
            act.activation(cond_r[:, :, 0:2].rearrange("p k w -> p w k"), cs[:].rearrange("p (w k) -> p w k", w=2),
                           ACT.Copy).then_inc(S["cond_ready"], 1)
            act.wait_ge(S["s5rows_in"], 16 * 9)
            act.activation(ldt[:], ldt[:], ACT.Exp).then_inc(S["dt_set"], 1)
            act.wait_ge(S["disc_a"], 1)
            act.activation(disc[:, 2, :], disc[:, 0, :], ACT.Exp).then_inc(S["exp_done"], 1)
            act.wait_ge(S["disc_b"], 1)
            act.activation(disc[:, 3, :], disc[:, 1, :], ACT.Sin)
            act.activation(disc[:, 4, :], disc[:, 1, :], ACT.Sin, scale=0.5).then_inc(S["sin_done"], 1)
            act.wait_ge(S["disc_T"], 1)
            act.activation(acoef[:].rearrange("p q (g d) -> p q d g", d=2),
                           flat[:, 512:768].rearrange("p (q d g) -> p q d g", q=4, d=2), ACT.Copy).then_inc(S["disc_out"], 1)
            for n, (dst, q) in enumerate(((Bc, 0), (Bc, 1), (Cc, 0), (Cc, 1))):
                for h in range(4):
                    act.wait_ge(S["bc_T"], 4 * n + h + 1)
                    act.activation(dst[:, q, :, 4 * h:4 * h + 4].rearrange("p g c -> p c g"),
                                   ps[:, 2 + h % 4, 0:256].rearrange("p (c g) -> p c g", c=4),
                                   ACT.Copy, scale=-1.0 if n == 3 else 1.0).then_inc(S["bc_out"], 1)
            act.wait_ge(S["x_in"], 32)
            for k in range(CK):
                chain.link(act.activation(flat[0:J, 3072:3072 + D], xin[:, k, :], ACT.Square,
                                          accum_out=stat[:, 0, k:k + 1]))
            act.activation(stat[:, 0, :], stat[:, 0, :], ACT.Sqrt, bias=eps[0:J, :], scale=1.0 / D)\
                .then_inc(S["rowsum_done"], 1)

            def hi(ch, n):
                act.wait_ge(wload[ch.slot], 32 * ch.nth + 32)
                if ch.reuse:
                    act.wait_ge(S["w_used"], ch.free)
                act.activation(whi[:, ch.slot, 0:n], wraw[:, ch.slot, 0:n], ACT.Copy).then_inc(S["hi_ready"], 1)

            for m in range(2):
                hi(Chunk(m), SLOT)
            with act.Fori(1, ADA_CHUNKS) as i:
                for m in range(2):
                    hi(Chunk(m, i), SLOT)

            def s5_block(b, n, first):
                act.wait_ge(S["mt_T"], n + 1)
                if not first:
                    act.wait_ge(S["s_done"], n)
                act.activation(MT[:].rearrange("p r g s -> p (r g s)"), flat[:, 0:1024], ACT.Copy).then_inc(S["mt_out"], 1)
                act.wait_ge(S["k_done"], n + 1)
                if not first:
                    act.wait_ge(S["tt_in"], 128 * n)
                act.activation(Kext[:].rearrange("c (g h) t o -> c g h (t o)", h=2)[:, :, :, 7 * CH:],
                               ps[0:CH, 2:4, 0:256].rearrange("c h (g x) -> c g h x", g=2), ACT.Copy).then_inc(S["kf_out"], 1)
                act.wait_ge(S["s_done"], n + 1)
                for h in range(2):
                    rows = slice(STATES * h, STATES * (h + 1))
                    last = act.activation(Sarr[rows, 1:J + 1, 0, :, bass.ds(2 * b, 2)].rearrange("p j r g -> p r g j"),
                                          ps[rows, 4:6, :].rearrange("p r (g x) -> p r g x", g=2)[:, :, :, J * h:J * (h + 1)],
                                          ACT.Copy)
                last.then_inc(S["sf_out"], 1)

            s5_block(0, 0, True)
            with act.Fori(1, GP // 2) as b:
                s5_block(b, b, False)

            for b in range(KD):
                act.wait_ge(S["y_done"], 2 * b + 2)
                if b >= 1:
                    act.wait_ge(S["z_T"], 2 * b)
                for h in range(2):
                    last = act.activation(yst.rearrange("j k (g h c) -> j h g k c", h=2, c=CH)[:, h],
                                          ps[0:J, 2 * (b % 2) + h, :].rearrange("j (g k c) -> j g k c", k=CK, c=CH),
                                          ACT.Gelu_apprx_tanh)
                last.then_inc(S["y_out"], 1)
            for b in range(KD):
                act.wait_ge(S["z_out"], 2 * KD)
                act.wait_ge(S["y_done"], 2 * KD)
                act.activation(hhi[:, b, :], U[:].rearrange("p g j -> p (g j)")[:, T * b:T * b + T], ACT.Copy)\
                    .then_inc(S["z_hi"], 1)

            def stage(first, count, n, epi):
                stage_turns(act, count, lambda c, turn: hi(Chunk(first + c, turn), n),
                            lambda m, c, turn: epi(m, Chunk(first + c, turn), turn is None and c < 2))

            def glu_epi(m, ch, early):
                a_l, g_l, a_c, g_c = glu_psum(ch.slot)
                act.wait_ge(S["w_used"], ch.done)
                if not early:
                    act.wait_ge(S["mix_done"], m - 1)
                bias = colsB[:, bass.ds(C_GLUB + KD + m, 1)]
                act.activation(sig[:, ch.slot, 0:NLAT], g_l, ACT.Sigmoid, bias=bias)
                act.activation(sig[:, ch.slot, NLAT:], g_c, ACT.Sigmoid, bias=bias).then_inc(S["sig_done"], 1)

            stage(B_GLU, KD, SLOT, glu_epi)

            def norm(j, l, q, toks, ready):
                act.wait_ge(*ready)
                for b in range(KD):
                    act.activation(sq[:, b, 0:toks], xT[:, b, 0:toks], ACT.Square).then_inc(S["sq_done"], 1)
                act.wait_ge(S["stat_T"], j + 1)
                act.activation(rstd[:, 0:toks], flat[:, 3072:3072 + toks], ACT.Sqrt, bias=eps[:], scale=1.0 / D)\
                    .then_inc(S["std_done"], 1)
                for b in range(KD):
                    n = KD * j + b + 1
                    act.wait_ge(S["xn_done"], n)
                    for t0, t1, cond in ((0, NLAT, 0), (NLAT, T, 1))[:1 if toks == NLAT else 2]:
                        v = hx[:, b % 2, t0:t1]
                        last = act.activation(v, v, ACT.Identity, scale=gain[:, l, q, b, cond:cond + 1],
                                              bias=modc[:, l, (SH_M, SH_F)[q] + b, cond:cond + 1])
                    last.then_inc(S["hx_done"], 1)
                    act.wait_ge(S["hx_done"], n)
                    act.activation(hhi[:, b, 0:toks], hx[:, b % 2, 0:toks], ACT.Copy).then_inc(S["h_hi"], 1)

            def ffn(l, toks):
                spans = ((0, NLAT), (NLAT, T))[:1 if toks == NLAT else 2]
                for g in range(2):
                    def epi(m, ch, early):
                        f = KF * l + GF * g + m
                        a_l, _, a_c, _ = glu_psum(ch.slot)
                        act.wait_ge(S["w_used"], ch.done)
                        if l or g or not early:
                            act.wait_ge(S["g_lo"], f - 1)
                        for (t0, t1), src in zip(spans, (a_l, a_c)):
                            last = act.activation(acc[:, ch.slot, t0:t1], src, ACT.Identity,
                                                  scale=colsW[:, l, bass.ds(KF + GF * g + m, 1)],
                                                  bias=colsB[:, bass.ds(C_CONVB + KF * l + GF * g + m, 1)])
                        last.then_inc(S["acc_set"], 1)
                        act.wait_ge(S["conv_done"], f + 1)
                        v = acc[:, ch.slot, 0:toks]
                        act.activation(v, v, ACT.Silu).then_inc(S["silu_done"], 1)
                        act.wait_ge(S["drained"], ch.drains)
                        act.activation(ghi[:, bass.ds(m, 1), 0:toks].rearrange("p a t -> p (a t)"), v, ACT.Copy)\
                            .then_inc(S["g_hi"], 1)
                    stage(B_FFN[l] + g * (GF + KD), GF, SLOT, epi)
                    stage(B_FFN[l] + g * (GF + KD) + GF, KD, GF * P, lambda m, ch, early: None)

            norm(0, 0, 1, T, (S["mix_done"], KD))
            ffn(0, T)
            norm(1, 1, 0, T, (S["drained"], B_DKV - B_GLU))

            def square(u, src, n):
                if u >= 2:
                    act.wait_ge(S["unit_used"], u - 1)
                act.activation(sqr[:, u % 2, 0:n], src, ACT.Square).then_inc(S["unit_sq"], 1)

            def root(j, n, mean):
                act.wait_ge(S["unit_used"], JOB_UNITS[j])
                if j >= 1:
                    act.wait_ge(S["job_out"], JOB_UNITS[j - 1])
                act.activation(rs[:, 0:n], flat[:, 3072:3072 + n], ACT.Sqrt, bias=eps[:], scale=1.0 / mean)\
                    .then_inc(S["job_std"], 1)

            hi(Chunk(B_DKV), KD * P)
            for m in range(3):
                if m < 2:
                    hi(Chunk(B_DKV + m + 1), KD * P)
                else:
                    hi(Chunk(B_DQ), KD * P)
                ch = Chunk(B_DKV + m)
                a_l, _, a_c, _ = glu_psum(ch.slot)
                dst = ckv_raw[:, m, :] if m < 2 else kr[:]
                act.wait_ge(S["w_used"], ch.done)
                act.activation(dst[:, 0:NLAT], a_l, ACT.Copy)
                act.activation(dst[:, NLAT:T], a_c, ACT.Copy).then_inc(S["drained"], 1)
                act.wait_ge(S["drained"], ch.drains)
                square(m, dst, T)
            for m in range(6):
                if m < 5:
                    hi(Chunk(B_DQ + m + 1), KD * P)
                else:
                    hi(Chunk(B_UKV), 8 * P)
                ch = Chunk(B_DQ + m)
                act.wait_ge(S["w_used"], ch.done)
                act.activation(cq_raw[:, m, :], glu_psum(ch.slot)[0], ACT.Copy).then_inc(S["drained"], 1)
                act.wait_ge(S["drained"], ch.drains)
                square(3 + m, cq_raw[:, m, :], NLAT)
                if m == 0:
                    root(0, T, KVR)
                if m == 1:
                    root(1, T, ROPE)
                if m in (2, 3):
                    b = m - 2
                    act.wait_ge(S["job_out"], b + 1)
                    act.activation(ckv_hi[:, b, :], ckv_raw[:, b, :], ACT.Copy).then_inc(S["ckv_hi_s"], 1)
            root(2, NLAT, QR)
            use = used_after(B_UKV - 1)
            for m in range(4):
                if m < 3:
                    hi(Chunk(B_UKV + m + 1), 8 * P)
                for t in range(KV_USES[m]):
                    use += 1
                    a_l, _, a_c, _ = glu_psum((use - 1) % 2)
                    act.wait_ge(S["w_used"], use)
                    if m < 2:
                        h = 4 * m + t
                        act.activation(kn[:, h, 0:NLAT], a_l, ACT.Copy)
                        act.activation(kn[:, h, NLAT:T], a_c, ACT.Copy).then_inc(S["drained"], 1)
                        act.wait_ge(S["drained"], use - B_GLU)
                        square(9 + h, kn[:, h, :], T)
                        if h >= 1:
                            root(3 + h - 1, T, NOPE)
                        if h < 6:
                            act.wait_ge(S["job_out"], JOB_UNITS[1] + h + 1)
                            act.activation(cq_hi[:, h, :], cq_raw[:, h, :], ACT.Copy).then_inc(S["cq_hi_s"], 1)
                    else:
                        act.activation(val[:, t, 512 * (m - 2):512 * (m - 1)], a_l, ACT.Copy).then_inc(S["drained"], 1)
                    if m == 2 and t == 0:
                        root(10, T, NOPE)
            hi(Chunk(B_UQ), 6 * P)
            for m in range(12):
                if m < 11:
                    hi(Chunk(B_UQ + m + 1), 6 * P)
                else:
                    hi(Chunk(B_WO), KD * P)
                ch = Chunk(B_UQ + m)
                act.wait_ge(S["w_used"], ch.done)
                act.activation(q_all[:, m, :], glu_psum(ch.slot)[0], ACT.Copy).then_inc(S["drained"], 1)
                act.wait_ge(S["drained"], ch.drains)
                square(17 + m, q_all[:, m, :], NLAT)
                if m >= 1:
                    root(11 + m - 1, NLAT, NOPE if m - 1 < HEADS else ROPE)
            root(22, NLAT, ROPE)

            def exps(i):
                act.wait_ge(S["mx_set"], i + 1)
                if i >= 2:
                    act.wait_ge(S["p_T"], i - 1)
                act.activation(pr[:, i % 2, :], flat[:, 1024 * (i % 2):1024 * (i % 2) + T], ACT.Exp,
                               bias=smax[:, i % 2, 1:2], scale=SCALE, accum_out=smax[:, i % 2, 2:3]).then_inc(S["ex_done"], 1)

            exps(0)
            for i in range(4 * HEADS):
                if i + 1 < 4 * HEADS:
                    exps(i + 1)
                h, t = i // 4, i % 4
                act.wait_ge(S["p_T"], i + 1)
                if h >= 2 and t == 0:
                    act.wait_ge(S["pv_done"], h - 1)
                act.activation(pT[:, h % 2, :, P * t:P * (t + 1)], flat[:, 2048:2048 + T].rearrange("p (b q) -> p b q", b=6),
                               ACT.Copy).then_inc(S["pT_out"], 1)
            for h in range(HEADS):
                act.wait_ge(S["ot_out"], HEADS)
                act.activation(hhi[:, h, 0:NLAT], ot[:, h, :], ACT.Copy).then_inc(S["o_hi"], 1)
            for m in range(KD - 1):
                hi(Chunk(B_WO + m + 1), KD * P)
            norm(2, 1, 1, NLAT, (S["drained"], used_after(B_FFN[1] - 1) - B_GLU))
            ffn(1, NLAT)

            for t in range(4):
                act.wait_ge(S["fin_out"], 2 * t + 2)
                act.dma_start(a["out"].rearrange("o (t p) d -> t p (o d)", p=P)[t], hhi_out(t)).then_inc(S["out_done"], 16)

        @block.vector
        def _(dve):
            chain = Chain(dve, S["dve_link"])
            dve.memset(ones[:], 1.0).then_inc(S["const_set"], 1)
            dve.memset(eps[:], EPS).then_inc(S["const_set"], 1)
            dve.memset(zero[:], 0.0).then_inc(S["const_set"], 1)
            dve.wait_ge(S["act_link"], 1)
            dve.tensor_tensor(cs[:], colsB[:, 0:16], sgc[:], ALU.mult).then_inc(S["const_set"], 1)
            dve.wait_ge(S["const_set"], 4)
            dve.wait_ge(S["cond_ready"], 1)
            dve.tensor_tensor(cond_r[:, :, 2:4].rearrange("p k w -> p w k"), cs[:].rearrange("p (w k) -> p w k", w=2),
                              cond_r[:, :, 0:2].bitcast(F32).rearrange("p k w -> p w k"), ALU.subtract)\
                .then_inc(S["cond_ready"], 1)

            lr, li = lam[:, 0, :], lam[:, 1, :]
            d_ = [disc[:, n, :] for n in range(12)]
            dve.wait_ge(S["dt_set"], 1)
            dtb = ldt[:].unsqueeze(2).to_broadcast([DG, 2, STATES])

            def hs(ap):
                return ap.rearrange("p (h s) -> p h s", h=2)

            dve.tensor_tensor(hs(d_[0]), hs(lr), dtb, ALU.mult).then_inc(S["disc_a"], 1)
            chain.link(dve.tensor_tensor(hs(d_[5]), hs(li), dtb, ALU.mult))
            chain.link(dve.tensor_scalar(d_[6], d_[5], 1.0 / (TWO_PI_HI + TWO_PI_LO), ROUND, ALU.mult, ALU.add))
            chain.link(dve.tensor_scalar(d_[6], d_[6], ROUND, None, ALU.subtract))
            chain.link(dve.scalar_tensor_tensor(d_[5], d_[6], -TWO_PI_HI, d_[5], ALU.mult, ALU.add))
            chain.link(dve.scalar_tensor_tensor(d_[5], d_[6], -TWO_PI_LO, d_[5], ALU.mult, ALU.add))
            dve.tensor_scalar(d_[1], d_[5], PI, -PI, ALU.min, ALU.max).then_inc(S["disc_b"], 1)
            chain.link(dve.tensor_tensor(d_[7], lr, lr, ALU.mult))
            chain.link(dve.tensor_tensor(d_[8], li, li, ALU.mult))
            chain.link(dve.tensor_tensor(d_[7], d_[7], d_[8], ALU.add))
            chain.link(dve.reciprocal(d_[7], d_[7]))
            dve.wait_ge(S["sin_done"], 1)
            dve.wait_ge(S["exp_done"], 1)
            chain.link(dve.tensor_tensor(d_[4], d_[4], d_[4], ALU.mult))
            chain.link(dve.tensor_scalar(d_[4], d_[4], -2.0, 1.0, ALU.mult, ALU.add))
            chain.link(dve.tensor_tensor(d_[8], d_[2], d_[4], ALU.mult))
            chain.link(dve.tensor_tensor(d_[9], d_[2], d_[3], ALU.mult))
            chain.link(dve.tensor_scalar(d_[5], d_[8], 1.0, None, ALU.subtract))
            chain.link(dve.tensor_tensor(d_[0], d_[5], lr, ALU.mult))
            chain.link(dve.tensor_tensor(d_[1], d_[9], li, ALU.mult))
            chain.link(dve.tensor_tensor(d_[0], d_[0], d_[1], ALU.add))
            chain.link(dve.tensor_tensor(d_[10], d_[0], d_[7], ALU.mult))
            chain.link(dve.tensor_tensor(d_[0], d_[9], lr, ALU.mult))
            chain.link(dve.tensor_tensor(d_[1], d_[5], li, ALU.mult))
            chain.link(dve.tensor_tensor(d_[0], d_[0], d_[1], ALU.subtract))
            dve.tensor_tensor(d_[11], d_[0], d_[7], ALU.mult).then_inc(S["disc_b"], 1)

            def cmul(o, x, y, n):
                t = [cm[:, q, :, 0:n] for q in range(2)]
                dve.tensor_tensor(t[0], x[0], y[0], ALU.mult)
                chain.link(dve.tensor_tensor(t[1], x[1], y[1], ALU.mult))
                chain.link(dve.tensor_tensor(o[0], t[0], t[1], ALU.subtract))
                dve.tensor_tensor(t[0], x[0], y[1], ALU.mult)
                chain.link(dve.tensor_tensor(t[1], x[1], y[0], ALU.mult))
                chain.link(dve.tensor_tensor(o[1], t[0], t[1], ALU.add))

            def pows(e0, e1):
                return [pw[:, q, :, e0:e1] for q in range(2)]

            def one(e, n):
                return [pw[:, q, :, e:e + 1].to_broadcast([P, DG, n]) for q in range(2)]

            dve.wait_ge(S["disc_out"], 1)
            dve.memset(pw[:, 0, :, 0], 1.0)
            chain.link(dve.memset(pw[:, 1, :, 0], 0.0))
            for q in range(2):
                chain.link(dve.tensor_copy(pw[:, q, :, 1], acoef[:, q, :]))
            cmul(pows(2, 3), pows(1, 2), pows(1, 2), 1)
            cmul(pows(3, 5), pows(1, 3), one(2, 2), 2)
            cmul(pows(5, 9), pows(1, 5), one(4, 4), 4)

            def by(t, q, dirn):
                return t[:, q].rearrange("p (g d) k -> p g d k", d=2)[:, :, dirn]

            f = [acoef[:, 2 + q, :].unsqueeze(2).to_broadcast([P, DG, CK]) for q in range(2)]
            cmul([Pn[:, q] for q in range(2)], pows(0, 8), f, 8)
            for q in range(2):
                dve.tensor_copy(by(Qk, q, 0), by(Pn, q, 0)[:, :, ::-1])
                chain.link(dve.tensor_copy(by(Qk, q, 1), by(Pn, q, 1)))
                dve.tensor_copy(by(Pk, q, 0), by(pw, q, 0)[:, :, 0:8])
                chain.link(dve.tensor_copy(by(Pk, q, 1), by(pw, q, 1)[:, :, 7::-1]))
                dve.tensor_copy(by(Pn, q, 0), by(pw, q, 0)[:, :, 1:9])
                chain.link(dve.tensor_copy(by(Pn, q, 1), by(pw, q, 1)[:, :, 8:0:-1]))
            for dirn in range(2):
                p8 = [by(pw, q, dirn)[:, :, 8] for q in range(2)]
                dve.tensor_copy(a8[:, dirn, 0, 0], p8[0])
                dve.tensor_copy(a8[:, dirn, 0, 1], p8[0])
                dve.tensor_copy(a8[:, dirn, 1, 0], p8[1])
                chain.link(dve.tensor_scalar(a8[:, dirn, 1, 1], p8[1], -1.0, None, ALU.mult))
            dve.wait_ge(S["cols_out"], 4)
            dve.tensor_tensor(kd[:], ident[0:CH, 0:CH].unsqueeze(1).to_broadcast([CH, GROUPS, CH]),
                              d16[:].unsqueeze(2).to_broadcast([CH, GROUPS, CH]), ALU.mult).then_inc(S["tab_set"], 1)
            dve.wait_ge(S["rowsum_done"], 1)
            chain.link(dve.reciprocal(stat[:, 1, :], stat[:, 0, :]))
            for k in range(CK):
                last = dve.tensor_scalar(xn[:, :, k, :], xin[:, k, :].rearrange("j (g c) -> j g c", c=CH), stat[:, 1, k:k + 1], None, ALU.mult)
            last.then_inc(S["rstd_set"], 1)

            def lo(ch, n):
                dve.wait_ge(S["hi_ready"], ch.n + 1)
                dve.tensor_tensor(wlo[:, ch.slot, 0:n], wraw[:, ch.slot, 0:n], whi[:, ch.slot, 0:n].bitcast(F32),
                                  ALU.subtract).then_inc(S["lo_ready"], 1)

            for l in range(2):
                with dve.Fori(0, ADA_CHUNKS // 2) as i:
                    for m in range(2):
                        lo(Chunk(l * ADA_CHUNKS + m, i), SLOT)
                dve.wait_ge(S["w_used"], (l + 1) * ADA_CHUNKS)
                raw = ps[:, 7 - l, 0:192].rearrange("p (b w) -> p b w", w=4)
                bias = colsA[:, C_ADAB + 48 * l:C_ADAB + 48 * (l + 1)].unsqueeze(2).to_broadcast([P, 48, 2])
                chain.link(dve.tensor_tensor(modc[:, l], raw[:, :, 0:2], bias, ALU.add))
                chain.link(dve.tensor_tensor(modc[:, l], raw[:, :, 2:4], modc[:, l], ALU.add))
                for q, (at, sc) in enumerate(((C_NMIX, SC_M), (C_NFFN, SC_F))):
                    g = colsA[:, at + KD * l:at + KD * (l + 1)].unsqueeze(2).to_broadcast([P, KD, 2])
                    last = dve.scalar_tensor_tensor(gain[:, l, q], modc[:, l, sc:sc + KD, :], 1.0, g, ALU.add, ALU.mult)
                last.then_inc(S["ada0_set"], 1)

            dve.wait_ge(S["rep_done"], 1)
            for v in range(2):
                for c in range(2):
                    last = dve.tensor_copy(urep[:, v, c].rearrange("p (b g) -> p g b", b=KD),
                                           ps[:, 6, 0:256].rearrange("p (g v b c) -> p g v b c", v=2, b=KD, c=2)[:, :, v, :, c])
            last.then_inc(S["rep_out"], 1)
            dve.wait_ge(S["rep_out"], 1)
            for q in range(GROUPS // 4):
                dve.wait_ge(S["u_T"], q + 1)
                src = ps[:, q % 4, :].rearrange("p (g j) -> p g j", g=4)
                for j0, j1, cond in ((0, JCTX, 1), (JCTX, J, 0)):
                    last = dve.tensor_tensor(U[:, 4 * q:4 * q + 4, j0:j1], src[:, :, j0:j1],
                                             urep[:, 0, cond, 4 * q:4 * q + 4].unsqueeze(2).to_broadcast([P, 4, j1 - j0]),
                                             ALU.mult)
                last.then_inc(S["u_mul"], 1)

            def m_block(b, q, n):
                dg = bass.ds(4 * b, 4)
                if n is not None:
                    dve.wait_ge(S["k_done"], n)
                q_re, q_im = (Qk[:, r, dg, :].unsqueeze(3).to_broadcast([P, 4, CK, CH]) for r in range(2))
                b_re, b_im = (Bc[:, r, dg, :].unsqueeze(2).to_broadcast([P, 4, CK, CH]) for r in range(2))
                dst = [Mr[:, q, r].rearrange("p g (k c) -> p g k c", k=CK) for r in range(2)]
                dve.tensor_tensor(tD[:, 0], q_re, b_re, ALU.mult)
                chain.link(dve.tensor_tensor(tD[:, 1], q_im, b_im, ALU.mult))
                chain.link(dve.tensor_tensor(dst[0], tD[:, 0], tD[:, 1], ALU.subtract))
                dve.tensor_tensor(tD[:, 0], q_re, b_im, ALU.mult)
                chain.link(dve.tensor_tensor(tD[:, 1], q_im, b_re, ALU.mult))
                dve.tensor_tensor(dst[1], tD[:, 0], tD[:, 1], ALU.add).then_inc(S["m_ready"], 1)

            def evac_block(b, n):
                dve.wait_ge(S["kf_out"], n + 1)
                back = ps[0:CH, 2:4, 256:512].rearrange("c h (g x) -> c g h x", g=2)
                ke = Kext[:].rearrange("c (g h) t o -> c g h (t o)", h=2)
                dve.tensor_copy(ke[:, :, :, 0:7 * CH], back[:, :, :, 0:7 * CH])
                mid = ke[:, :, :, 7 * CH:8 * CH]
                chain.link(dve.tensor_tensor(mid, mid, back[:, :, :, 7 * CH:], ALU.add))
                midg = Kext[:, :, 7, :]
                dve.tensor_tensor(midg, midg, kd[:, bass.ds(4 * b, 4), :], ALU.add).then_inc(S["kext_ready"], 1)
                dve.wait_ge(S["s_done"], n + 1)
                for h in range(2):
                    rows = slice(STATES * h, STATES * (h + 1))
                    last = dve.tensor_copy(Sarr[rows, 0:J, 1, :, bass.ds(2 * b, 2)].rearrange("p j r g -> p r g j"),
                                           ps[rows, 6:8, :].rearrange("p r (g x) -> p r g x", g=2)[:, :, :, J * h:J * (h + 1)])
                last.then_inc(S["sb_out"], 1)

            dve.wait_ge(S["u_T"], GROUPS // 4)
            dve.memset(Sarr[:, 0, 0], 0.0).then_inc(S["s_zero"], 1)
            m_block(0, 0, None)
            dve.wait_ge(S["m_ready"], 1)
            m_block(1, 1, None)
            evac_block(0, 0)
            dve.wait_ge(S["m_ready"], 2)
            with dve.Fori(1, GP // 4) as i:
                chain.enter(i - 1, 8)
                for q in range(2):
                    m_block(2 * i + q, q, 2 * i + q - 1)
                    dve.wait_ge(S["m_ready"], 2 * i + q + 1)
                    evac_block(2 * i + q - 1, 2 * i + q - 1)
            chain.leave(GP // 4 - 1)
            evac_block(GP // 2 - 1, GP // 2 - 1)

            def views(s, prev, dirn):
                slots = Sarr[:, :, 0] if dirn == 0 else Sarr[:, ::-1, 1]
                return (slots[:, bass.ds(prev, 1)].rearrange("p a r g -> p (a r) g"),
                        slots[:, bass.ds(s, 1)].rearrange("p a r g -> p (a r) g"), (scF, scB)[dirn])

            def step(*moves):
                v = [views(*m) for m in moves]
                back = len(moves) - 1
                for (h, x, t), (_, _, dirn) in zip(v, moves):
                    chain.mark(dve.tensor_tensor(t[:, 0:2], a8[:, dirn], h.unsqueeze(1).to_broadcast([P, 2, 2, GP]), ALU.mult))
                    chain.need(back)
                for h, x, t in v:
                    chain.mark(dve.tensor_tensor(t[:, 2], t[:, 0], x, ALU.add))
                    chain.need(back)
                for h, x, t in v:
                    chain.mark(dve.tensor_tensor(x, t[:, 2], t[:, 1, ::-1], ALU.add))
                    chain.need(back)

            dve.wait_ge(S["sf_out"], GP // 2)
            dve.wait_ge(S["sb_out"], GP // 2)
            with dve.Fori(0, JCTX - 1) as i:
                chain.enter(i, 6)
                step((2 + i, 1 + i, 0), (J - JCTX + 2 + i, J - JCTX + 1 + i, 1))
            chain.leave(JCTX - 1)
            chain.need(0)
            chain.link(dve.tensor_copy(Sarr[:, J, 1], Sarr[:, 0, 1]))
            with dve.Fori(0, JLAT - 1) as i:
                chain.enter(i, 6)
                step((JCTX + 1 + i, JCTX + i, 0), (1 + i, i, 1))
            chain.leave(JLAT - 1)
            chain.need(0)
            dve.memset(Sarr[:, JCTX, 1], 0.0).then_inc(S["scanF"], 2)
            dve.wait_ge(S["k_done"], GP // 2)

            def z_evac(b):
                for h in range(2):
                    dve.wait_ge(S["z_T"], 2 * b + h + 1)
                    src = ps[:, 4 + 2 * (b % 2) + h, :].rearrange("p (k j) -> p k j", k=4)
                    dst = U[:].rearrange("p g j -> p (g j)")[:, T * b:T * b + T]
                    dve.tensor_copy(dst[:, 0:NLAT].rearrange("p (j k) -> p k j", k=CK)[:, 4 * h:4 * h + 4], src[:, :, JCTX:J])
                    dve.tensor_copy(dst[:, NLAT:T].rearrange("p (j k) -> p k j", k=CK)[:, 4 * h:4 * h + 4], src[:, :, 0:JCTX])\
                        .then_inc(S["z_out"], 1)

            for hb in range(GP // 2):
                dg = slice(4 * hb, 4 * hb + 4)
                p_re, p_im = (Pn[:, r, dg, :].unsqueeze(3).to_broadcast([P, 4, CK, CH]) for r in range(2))
                c_re, c_ni = (Cc[:, r, dg, :].unsqueeze(2).to_broadcast([P, 4, CK, CH]) for r in range(2))
                if hb >= 2:
                    dve.wait_ge(S["y_done"], hb - 1)
                dve.tensor_tensor(tD[:, 0], p_re, c_re, ALU.mult)
                chain.link(dve.tensor_tensor(tD[:, 1], p_im, c_ni, ALU.mult))
                dve.tensor_tensor(Nr[:, hb % 2, 0].rearrange("p g (k c) -> p g k c", k=CK),
                                  tD[:, 0], tD[:, 1], ALU.add).then_inc(S["n2_re"], 1)
                dve.wait_ge(S["n2_re"], hb + 1)
                if hb % 2 and hb >= 5:
                    z_evac((hb - 5) // 2)
            z_evac(KD - 2)
            z_evac(KD - 1)
            for b in range(KD):
                for h in range(2):
                    dve.wait_ge(S["xT_T"], 2 * b + h + 1)
                    src = ps[:, 4 + 2 * (b % 2) + h, :].rearrange("p (k j) -> p k j", k=4)
                    dst = xT[:, b, :]
                    dve.tensor_copy(dst[:, 0:NLAT].rearrange("p (j k) -> p k j", k=CK)[:, 4 * h:4 * h + 4], src[:, :, JCTX:J])
                    dve.tensor_copy(dst[:, NLAT:T].rearrange("p (j k) -> p k j", k=CK)[:, 4 * h:4 * h + 4], src[:, :, 0:JCTX])\
                        .then_inc(S["xT_out"], 1)
            dve.wait_ge(S["xT_out"], 2 * KD)

            def stage(first, count, n, epi):
                stage_turns(dve, count, lambda c, turn: lo(Chunk(first + c, turn), n),
                            lambda m, c, turn: epi(m, Chunk(first + c, turn), turn is None and c < 2))

            def glu_epi(m, ch, early):
                a_l, _, a_c, _ = glu_psum(ch.slot)
                dve.wait_ge(S["sig_done"], ch.n - B_GLU + 1)
                bias = colsB[:, bass.ds(C_GLUB + m, 1)]
                for v, pa, cond in ((slice(0, NLAT), a_l, 0), (slice(NLAT, T), a_c, 1)):
                    s_ = sig[:, ch.slot, v]
                    last = dve.scalar_tensor_tensor(s_, pa, bias, s_, ALU.add, ALU.mult)
                last.then_inc(S["drained"], 1)
                dve.wait_ge(S["drained"], ch.n - B_GLU + 1)
                for v, cond in ((slice(0, NLAT), 0), (slice(NLAT, T), 1)):
                    xv = xT[:, bass.ds(m, 1), v].rearrange("p a t -> p (a t)")
                    g = modc[:, 0, bass.ds(G_M + m, 1), cond]
                    last = dve.scalar_tensor_tensor(xv, sig[:, ch.slot, v], g, xv, ALU.mult, ALU.add)
                last.then_inc(S["mix_done"], 1)

            stage(B_GLU, KD, SLOT, glu_epi)

            def norm(j, toks):
                dve.wait_ge(S["sq_done"], KD * j + 2)
                chain.link(dve.tensor_tensor(ssum[:, 0:toks], sq[:, 0, 0:toks], sq[:, 1, 0:toks], ALU.add))
                for b in range(2, KD):
                    dve.wait_ge(S["sq_done"], KD * j + b + 1)
                    op = dve.tensor_tensor(ssum[:, 0:toks], ssum[:, 0:toks], sq[:, b, 0:toks], ALU.add)
                    if b < KD - 1:
                        chain.link(op)
                op.then_inc(S["ssum_done"], 1)
                dve.wait_ge(S["std_done"], j + 1)
                chain.link(dve.reciprocal(rstd[:, 0:toks], rstd[:, 0:toks]))
                for b in range(KD):
                    if b >= 2:
                        dve.wait_ge(S["h_lo"], KD * j + b - 1)
                    dve.tensor_tensor(hx[:, b % 2, 0:toks], xT[:, b, 0:toks], rstd[:, 0:toks], ALU.mult)\
                        .then_inc(S["xn_done"], 1)

            def out_epi(l, at, toks):
                def epi(m, ch, early):
                    a_l, _, a_c, _ = glu_psum(ch.slot)
                    dve.wait_ge(S["w_used"], ch.done)
                    for (t0, t1), src, cond in (((0, NLAT), a_l, 0), ((NLAT, T), a_c, 1))[:1 if toks == NLAT else 2]:
                        xv = xT[:, bass.ds(m, 1), t0:t1].rearrange("p a t -> p (a t)")
                        last = dve.scalar_tensor_tensor(xv, src, modc[:, l, bass.ds(at + m, 1), cond], xv, ALU.mult, ALU.add)
                    last.then_inc(S["drained"], 1)
                return epi

            def ffn(l, toks):
                spans = ((0, NLAT), (NLAT, T))[:1 if toks == NLAT else 2]
                for g in range(2):
                    def epi(m, ch, early):
                        f = KF * l + GF * g + m
                        a_l, b_l, a_c, b_c = glu_psum(ch.slot)
                        dve.wait_ge(S["acc_set"], f + 1)
                        v = acc[:, ch.slot]
                        w = colsW[:, l]
                        for (t0, t1), src in zip(spans, (a_l, a_c)):
                            n = t1 - t0
                            op = dve.scalar_tensor_tensor(v[:, t0 + 1:t1], src[:, 0:n - 1], w[:, bass.ds(GF * g + m, 1)],
                                                          v[:, t0 + 1:t1], ALU.mult, ALU.add)
                        chain.link(op)
                        for (t0, t1), src in zip(spans, (a_l, a_c)):
                            n = t1 - t0
                            op = dve.scalar_tensor_tensor(v[:, t0:t1 - 1], src[:, 1:n], w[:, bass.ds(2 * KF + GF * g + m, 1)],
                                                          v[:, t0:t1 - 1], ALU.mult, ALU.add)
                        op.then_inc(S["conv_done"], 1)
                        dve.wait_ge(S["silu_done"], f + 1)
                        for (t0, t1), src in zip(spans, (b_l, b_c)):
                            op = dve.tensor_tensor(v[:, t0:t1], v[:, t0:t1], src, ALU.mult)
                        op.then_inc(S["drained"], 1)
                    first = B_FFN[l] + g * (GF + KD)
                    pairs = (GF - 3) // 2
                    def turned(m, c, turn):
                        if turn is not None and c == 0:
                            chain.enter(turn - 1, 2)
                        epi(m, Chunk(first + c, turn), turn is None and c < 2)
                        if turn is not None and c == 1:
                            chain.leave(pairs)
                    stage_turns(dve, GF, lambda c, turn: lo(Chunk(first + c, turn), SLOT), turned)
                    stage(first + GF, KD, GF * P, out_epi(l, G_F, toks))

            norm(0, T)
            ffn(0, T)
            norm(1, T)

            def job(j, n, views, gains):
                dve.wait_ge(S["job_std"], j + 1)
                chain.link(dve.reciprocal(rs[:, 0:n], rs[:, 0:n]))
                for v, g in zip(views, gains):
                    op = dve.scalar_tensor_tensor(v, v, colsB[:, g:g + 1], rs[:, 0:n], ALU.mult, ALU.mult)
                    op.then_inc(S["job_out"], 1)

            def rotate(v, swapped, n, done):
                dve.wait_ge(swapped, n)
                dve.tensor_tensor(v, v, rope_cs[:, 0], ALU.mult)
                chain.link(dve.tensor_tensor(rs[:, 0:NLAT], ps[:, 7, :], rope_cs[:, 1], ALU.mult))
                dve.tensor_tensor(v, v, rs[:, 0:NLAT], ALU.add).then_inc(done, 1)

            lo(Chunk(B_DKV), KD * P)
            lo(Chunk(B_DKV + 1), KD * P)
            lo(Chunk(B_DKV + 2), KD * P)
            for m in range(6):
                lo(Chunk(B_DQ + m), KD * P)
                if m == 1:
                    job(0, T, [ckv_raw[:, b, :] for b in range(2)], (C_GKV, C_GKV + 1))
                if m == 2:
                    job(1, T, [kr[:]], (C_GKR,))
            lo(Chunk(B_UKV), 8 * P)
            job(2, NLAT, [cq_raw[:, b, :] for b in range(6)], range(C_GQ, C_GQ + 6))
            lo(Chunk(B_UKV + 1), 8 * P)
            for h in range(HEADS):
                if h in (4, ):
                    lo(Chunk(B_UKV + 2), 8 * P)
                job(3 + h, T, [kn[:, h, :]], (C_GKN,))
            lo(Chunk(B_UKV + 3), 8 * P)
            lo(Chunk(B_UQ), 6 * P)
            for m in range(12):
                if m < 11:
                    lo(Chunk(B_UQ + m + 1), 6 * P)
                else:
                    lo(Chunk(B_WO), KD * P)
                if m >= 1:
                    job(11 + m - 1, NLAT, [q_all[:, m - 1, :]], (C_GQN if m - 1 < HEADS else C_GQR,))
            job(22, NLAT, [q_all[:, 11, :]], (C_GQR,))
            dve.wait_ge(S["rope_in"], 16)
            for n, v in enumerate([kr[:, 0:NLAT]] + [q_all[:, HEADS + m, :] for m in range(4)]):
                rotate(v, S["swap_T"], n + 1, S["rot_done"])
                dve.wait_ge(S["rot_done"], n + 1)

            def maxes(i):
                dve.wait_ge(S["sc_done"], i + 1)
                if i >= 2:
                    dve.wait_ge(S["pr_set"], i - 1)
                chain.link(dve.reduce_max(smax[:, i % 2, 0:1], flat[:, 1024 * (i % 2):1024 * (i % 2) + T], AX.X))
                dve.tensor_scalar(smax[:, i % 2, 1:2], smax[:, i % 2, 0:1], -SCALE, None, ALU.mult).then_inc(S["mx_set"], 1)

            maxes(0)
            for i in range(4 * HEADS):
                if i + 1 < 4 * HEADS:
                    maxes(i + 1)
                dve.wait_ge(S["ex_done"], i + 1)
                chain.link(dve.reciprocal(smax[:, i % 2, 3:4], smax[:, i % 2, 2:3]))
                dve.tensor_scalar(pr[:, i % 2, :], pr[:, i % 2, :], smax[:, i % 2, 3:4], None, ALU.mult)\
                    .then_inc(S["pr_set"], 1)
                if i % 4 == 1 and i > 4:
                    h = i // 4 - 1
                    dve.wait_ge(S["pv_done"], h + 1)
                    dve.tensor_copy(ot[:, h, :], ps[:, 6 + h % 2, :]).then_inc(S["ot_out"], 1)
            dve.wait_ge(S["pv_done"], HEADS)
            dve.tensor_copy(ot[:, HEADS - 1, :], ps[:, 7, :]).then_inc(S["ot_out"], 1)
            for m in range(KD):
                if m < KD - 1:
                    lo(Chunk(B_WO + m + 1), KD * P)
                out_epi(1, G_M, NLAT)(m, Chunk(B_WO + m), False)
            norm(2, NLAT)
            ffn(1, NLAT)

            for t in range(4):
                for h in range(2):
                    dve.wait_ge(S["fin_T"], 2 * t + h + 1)
                    dve.tensor_copy(hhi_out(t)[:, 512 * h:512 * h + 512], ps[:, (2 * t + h) % 4, :]).then_inc(S["fin_out"], 1)

        @block.tensor
        def _(pe):
            pe.wait_ge(S["params_in"], 16 * 21)
            pe.transpose(flat[0:CH, 400:464], drow[:], ident[0:GROUPS, 0:GROUPS])
            pe.transpose(flat[:, 128:216], rowsB[:], ident[0:88, 0:88])
            pe.transpose(flat[:, 0:128], rowsA[:], ident[:])
            for l in range(2):
                last = pe.transpose(flat[:, 256 + 66 * l:322 + 66 * l], rowsW[:, l, :], ident[0:66, 0:66])
            last.then_inc(S["cols_T"], 1)
            pe.wait_ge(S["disc_b"], 2)
            for q in range(4):
                last = pe.transpose(flat[:, 512 + DG * q:512 + DG * (q + 1)], disc[:, 8 + q, :], ident[0:DG, 0:DG])
            last.then_inc(S["disc_T"], 1)
            for n, (src, q, eq) in enumerate(((brow, 0, "p (h s c) -> p c h s"), (brow, 1, "p (h s c) -> p c h s"),
                                              (crow, 0, "p (c h s) -> p c h s"), (crow, 1, "p (c h s) -> p c h s"))):
                v = src[:, q, :].rearrange(eq, h=2, c=CH)
                perm = ident[0:DG, 0:DG].rearrange("p (d g) -> p g d", d=2)
                for h in range(4):
                    if n >= 1:
                        pe.wait_ge(S["bc_out"], 4 * (n - 1) + h + 1)
                    for c in range(4):
                        last = pe.matmul(ps[:, 2 + h, DG * c:DG * (c + 1)], v[:, 4 * h + c].rearrange("p h s -> p (h s)"), perm, start=True, stop=True)
                    last.then_inc(S["bc_T"], 1)

            pe.wait_ge(S["cond_ready"], 2)

            def ada(ch, l, col):
                pe.wait_ge(S["lo_ready"], ch.n + 1)
                for b in range(2):
                    dst = ps[:, 7 - l, bass.ds(col + 4 * b, 4)]
                    for k in range(KD):
                        for w in (whi, wlo):
                            last = pe.matmul(dst, wview(w, ch.slot, KD, 256)[:, k, b * P:(b + 1) * P], cond_r[:, k, :],
                                             start=k == 0 and w is whi, stop=k == KD - 1 and w is wlo)
                last.then_inc(S["w_used"], 1)

            for l in range(2):
                with pe.Fori(0, ADA_CHUNKS // 2) as i:
                    for m in range(2):
                        ada(Chunk(l * ADA_CHUNKS + m, i), l, 16 * i + 8 * m)

            pe.wait_ge(S["ada0_set"], 2)
            pe.wait_ge(S["tabs_in"], 1)
            for g in range(KD):
                for v, rhs in enumerate((gain[:, 0, 0], modc[:, 0, SH_M:SH_M + KD, :])):
                    at = 32 * g + 16 * v
                    last = pe.matmul(ps[:, 6, at:at + 16], pick[:, g].rearrange("p k c -> p (k c)"),
                                     rhs.rearrange("p b c -> p (b c)"), start=True, stop=True)
            last.then_inc(S["rep_done"], 1)
            pe.wait_ge(S["rstd_set"], 1)
            for q in range(GROUPS // 4):
                if q >= 4:
                    pe.wait_ge(S["u_mul"], q - 3)
                for r in range(4):
                    g = 4 * q + r
                    last = pe.transpose(ps[:, q % 4, P * r:P * r + J], xn[:, g].rearrange("j k c -> j (k c)"), ident[0:J, 0:J])
                last.then_inc(S["u_T"], 1)

            def s5_block(b, q, n, first):
                pe.wait_ge(S["m_ready"], n + 1)
                pe.wait_ge(S["n_ready"], n + 1)
                if not first:
                    pe.wait_ge(S["kext_ready"], n)
                if first:
                    pe.wait_ge(S["u_add"], GROUPS // 4)
                else:
                    pe.wait_ge(S["mt_out"], n)
                for r in range(2):
                    for g in range(4):
                        last = pe.transpose(ps[:, r, P * g:P * (g + 1)], Mr[:, q, r, g, :], ident[:])
                last.then_inc(S["mt_T"], 1)
                for g in range(2):
                    for dirn in range(2):
                        k0 = CK - 1 if dirn == 0 else 0
                        for h in range(2):
                            rows = slice(STATES * h, STATES * (h + 1))
                            dst = ps[0:CH, 2 + h, 256 * dirn + P * g:256 * dirn + P * (g + 1)]
                            for r in range(2):
                                last = pe.matmul(dst, Mr[rows, q, r, 2 * g + dirn, CH * k0:CH * (k0 + 1)],
                                                 Nr[rows, q, r, 2 * g + dirn, :], start=r == 0, stop=r == 1)
                last.then_inc(S["k_done"], 1)
                pe.wait_ge(S["mt_out"], n + 1)
                if not first:
                    pe.wait_ge(S["sf_out"], n)
                    pe.wait_ge(S["sb_out"], n)
                for dirn in range(2):
                    for r in range(2):
                        for g in range(2):
                            last = pe.matmul(ps[:, 4 + 2 * dirn + r, 256 * g:256 * g + 2 * J], MT[:, r, 2 * g + dirn, :],
                                             U[:, bass.ds(4 * b + 2 * g, 2), :].rearrange("p a j -> p (a j)"),
                                             start=True, stop=True)
                last.then_inc(S["s_done"], 1)

            s5_block(0, 0, 0, True)
            s5_block(1, 1, 1, False)
            with pe.Fori(1, GP // 4) as i:
                for q in range(2):
                    s5_block(2 * i + q, q, 2 * i + q, False)

            pe.wait_ge(S["tt_in"], 128 * (GP // 2))
            pe.wait_ge(S["scanF"], 2)

            def z_T(b):
                pe.wait_ge(S["y_out"], b + 1)
                for h in range(2):
                    if b >= 2:
                        pe.wait_ge(S["z_out"], 2 * (b - 2) + h + 1)
                    for k in range(4):
                        last = pe.transpose(ps[:, 4 + 2 * (b % 2) + h, P * k:P * k + J], yst[:, 4 * h + k, :], ident[0:J, 0:J])
                    last.then_inc(S["z_T"], 1)

            for hb in range(GP // 2):
                if hb >= 4:
                    pe.wait_ge(S["y_out"], (hb - 4) // 2 + 1)
                pe.wait_ge(S["n2_re"], hb + 1)
                pe.wait_ge(S["n2_im"], hb + 1)
                for gl in range(4):
                    g = 4 * hb + gl
                    gp, h = g // 2, g % 2
                    rows = slice(STATES * h, STATES * (h + 1))
                    at = P * (gp % 4)
                    dst = ps[0:J, 2 * (hb // 2 % 2) + h, at:at + P]
                    pe.matmul(dst, U[:, g, :], TT[:, g, :], start=True, stop=False)
                    for dirn in range(2):
                        for r in range(2):
                            last = pe.matmul(dst, Sarr[rows, dirn:dirn + J, dirn, r, gp],
                                             Nr[rows, hb % 2, r, 2 * (gl // 2) + dirn, :],
                                             start=False, stop=dirn == 1 and r == 1)
                last.then_inc(S["y_done"], 1)
                if hb % 2 and hb >= 3:
                    z_T((hb - 3) // 2)
            z_T(KD - 1)

            pe.wait_ge(S["x2_in"], 32)
            for b in range(KD):
                for h in range(2):
                    if b >= 2:
                        pe.wait_ge(S["xT_out"], 2 * (b - 2) + h + 1)
                    else:
                        pe.wait_ge(S["z_out"], 2 * KD)
                    for k in range(4):
                        last = pe.transpose(ps[:, 4 + 2 * (b % 2) + h, P * k:P * k + J],
                                            xin2[:, 4 * h + k, P * b:P * (b + 1)], ident[0:J, 0:J])
                    last.then_inc(S["xT_T"], 1)

            def psum_free(ch, early):
                if not early:
                    pe.wait_ge(S["drained"], ch.drains - 2)

            def products(ch, dst, w0, nk, hi_, lo_, toks, per_block=None):
                wh, wl = (wview(w, ch.slot, w0 + nk) for w in (whi, wlo))
                for k in range(nk):
                    if per_block is not None:
                        pe.wait_ge(per_block[0], per_block[1] + k + 1)
                    for w, h, first, final in ((wh, hi_, k == 0, False), (wh, lo_, False, False),
                                               (wl, hi_, False, k == nk - 1)):
                        for (t0, t1), d in zip(((0, NLAT), (NLAT, T))[:1 if toks == NLAT else 2], dst):
                            last = pe.matmul(d, w[:, w0 + k, :], h[:, k, t0:t1], start=first, stop=final)
                return last

            def pair_stage(first, count, toks, ready):
                def one(m, c, turn):
                    ch = Chunk(first + c, turn)
                    a_l, b_l, a_c, b_c = glu_psum(ch.slot)
                    pe.wait_ge(S["lo_ready"], ch.n + 1)
                    psum_free(ch, turn is None and first + c < B_GLU + 2)
                    products(ch, (a_l, a_c), 0, KD, hhi, hlo, toks, ready if turn is None and c == 0 else None)
                    products(ch, (b_l, b_c), KD, KD, hhi, hlo, toks).then_inc(S["w_used"], 1)
                chunk_turns(pe, count, one)

            def plain_stage(first, count, nk, hi_, lo_, toks, ready=None):
                def one(m, c, turn):
                    ch = Chunk(first + c, turn)
                    a_l, _, a_c, _ = glu_psum(ch.slot)
                    pe.wait_ge(S["lo_ready"], ch.n + 1)
                    psum_free(ch, False)
                    products(ch, (a_l, a_c), 0, nk, hi_, lo_, toks, ready if turn is None and c == 0 else None)\
                        .then_inc(S["w_used"], 1)
                chunk_turns(pe, count, one)

            def norm(j, toks):
                pe.wait_ge(S["ssum_done"], j + 1)
                for t0, t1 in ((0, NLAT), (NLAT, T))[:1 if toks == NLAT else 2]:
                    last = pe.matmul(flat[:, 3072 + t0:3072 + t1], ones[:], ssum[:, t0:t1], start=True, stop=True)
                last.then_inc(S["stat_T"], 1)

            def ffn(l, toks, j):
                for g in range(2):
                    first = B_FFN[l] + g * (GF + KD)
                    pair_stage(first, GF, toks, (S["h_lo"], KD * j) if g == 0 else None)
                    plain_stage(first + GF, KD, GF, ghi, glo, toks, (S["g_lo"], KF * l + GF * g))

            pe.wait_ge(S["xT_out"], 2 * KD)
            pair_stage(B_GLU, KD, T, (S["z_lo"], 0))
            norm(0, T)
            ffn(0, T, 0)
            norm(1, T)

            unit = [0]
            job = [0]

            def sums(n, lhs, first, final):
                u = unit[0]
                unit[0] += 1
                pe.wait_ge(S["unit_sq"], u + 1)
                if first and job[0] >= 1:
                    pe.wait_ge(S["job_std"], job[0])
                for t0, t1 in ((0, NLAT), (NLAT, T))[:1 if n == NLAT else 2]:
                    last = pe.matmul(flat[:, 3072 + t0:3072 + t1], lhs[:], sqr[:, u % 2, t0:t1], start=first, stop=final)
                last.then_inc(S["unit_used"], 1)
                if final:
                    job[0] += 1

            def low_rank(c, nk, toks, ready=None):
                ch = Chunk(c)
                a_l, _, a_c, _ = glu_psum(ch.slot)
                pe.wait_ge(S["lo_ready"], ch.n + 1)
                psum_free(ch, False)
                products(ch, (a_l, a_c), 0, nk, *((hhi, hlo) if nk == KD else (cq_hi, cq_lo)), toks, ready)\
                    .then_inc(S["w_used"], 1)

            for m in range(3):
                low_rank(B_DKV + m, KD, T, (S["h_lo"], KD) if m == 0 else None)
                if m >= 1:
                    sums(T, ones, m == 1, m == 2)
            for m in range(6):
                low_rank(B_DQ + m, KD, NLAT)
                if m == 0:
                    sums(T, half_ones, True, True)
                else:
                    sums(NLAT, ones, m == 1, False)
            sums(NLAT, ones, False, True)
            use = used_after(B_UKV - 1)
            for m in range(4):
                ch = Chunk(B_UKV + m)
                pe.wait_ge(S["lo_ready"], ch.n + 1)
                wh, wl = (wview(w, ch.slot, 2, 4 * P) for w in (whi, wlo))
                for t in range(KV_USES[m]):
                    use += 1
                    a_l, _, a_c, _ = glu_psum((use - 1) % 2)
                    pe.wait_ge(S["drained"], use - B_GLU - 2)
                    if m == 0 and t == 0:
                        pe.wait_ge(S["ckv_lo_s"], 2)
                    for k in range(2):
                        for w, h, first, final in ((wh, ckv_hi, k == 0, False), (wh, ckv_lo, False, False),
                                                   (wl, ckv_hi, False, k == 1)):
                            if m < 2:
                                for (t0, t1), d in zip(((0, NLAT), (NLAT, T)), (a_l, a_c)):
                                    last = pe.matmul(d, w[:, k, P * t:P * (t + 1)], h[:, k, t0:t1], start=first, stop=final)
                            else:
                                last = pe.matmul(a_l, h[:, k, P * t:P * (t + 1)], w[:, k, :], start=first, stop=final)
                    last.then_inc(S["w_used"], 1)
                    if m < 2 and 4 * m + t >= 1:
                        sums(T, ones, True, True)
                    if m == 2 and t == 0:
                        sums(T, ones, True, True)
            for m in range(12):
                low_rank(B_UQ + m, 6, NLAT, (S["cq_lo_s"], 0) if m == 0 else None)
                if m >= 1:
                    sums(NLAT, ones if m - 1 < HEADS else half_ones, True, True)
            sums(NLAT, half_ones, True, True)
            pe.wait_ge(S["job_out"], JOB_UNITS[-1])
            for n, v in enumerate([kr[:, 0:NLAT]] + [q_all[:, HEADS + m, :] for m in range(4)]):
                if n >= 1:
                    pe.wait_ge(S["rot_done"], n)
                pe.matmul(ps[:, 7, :], swap[:], v, start=True, stop=True).then_inc(S["swap_T"], 1)
            pe.wait_ge(S["rot_done"], 5)

            def scores(i):
                h, t = i // 4, i % 4
                if i >= 2:
                    pe.wait_ge(S["ex_done"], i - 1)
                rows = slice(ROPE * (h % 2), ROPE * (h % 2 + 1))
                for t0, t1 in ((0, NLAT), (NLAT, T)):
                    d = flat[:, 1024 * (i % 2) + t0:1024 * (i % 2) + t1]
                    pe.matmul(d, q_all[:, h, P * t:P * (t + 1)], kn[:, h, t0:t1], start=True, stop=False)
                    last = pe.matmul(d, q_all[rows, HEADS + h // 2, P * t:P * (t + 1)], kr[rows, t0:t1], start=False, stop=True)
                last.then_inc(S["sc_done"], 1)

            def head_out(h):
                pe.wait_ge(S["pT_out"], 4 * h + 4)
                if h >= 2:
                    pe.wait_ge(S["ot_out"], h - 1)
                for b in range(6):
                    last = pe.matmul(ps[:, 6 + h % 2, :], val[:, b, VD * h:VD * (h + 1)], pT[:, h % 2, b, :],
                                     start=b == 0, stop=b == 5)
                last.then_inc(S["pv_done"], 1)

            scores(0)
            for i in range(4 * HEADS):
                if i + 1 < 4 * HEADS:
                    scores(i + 1)
                pe.wait_ge(S["pr_set"], i + 1)
                if i >= 1:
                    pe.wait_ge(S["pT_out"], i)
                for b in range(6):
                    last = pe.transpose(flat[:, 2048 + P * b:2048 + P * (b + 1)], pr[:, i % 2, P * b:P * (b + 1)], ident[:])
                last.then_inc(S["p_T"], 1)
                if i % 4 == 0 and i:
                    head_out(i // 4 - 1)
            head_out(HEADS - 1)
            plain_stage(B_WO, KD, KD, hhi, hlo, NLAT, (S["o_lo"], 0))
            norm(2, NLAT)
            ffn(1, NLAT, 2)

            pe.wait_ge(S["drained"], used_after(B_FFN[1] + 2 * (GF + KD) - 1) - B_GLU)
            for t in range(4):
                for h in range(2):
                    if 2 * t + h >= 4:
                        pe.wait_ge(S["fin_out"], 2 * t + h - 3)
                    for b in range(4):
                        last = pe.transpose(ps[:, (2 * t + h) % 4, P * b:P * (b + 1)], xT[:, 4 * h + b, P * t:P * (t + 1)],
                                            ident[:])
                    last.then_inc(S["fin_T"], 1)


INPUTS = ("x", "c", "ctx", "c_ctx", "ada_w", "ada_b", "norm_mix", "norm_ffn", "s5_lam_re", "s5_lam_im", "s5_log_dt",
          "s5_b_re", "s5_b_im", "s5_c_re", "s5_c_im", "s5_d", "s5_glu_w", "s5_glu_b", "mla_w_dq", "mla_g_q", "mla_w_uq",
          "mla_w_dkv", "mla_g_kv", "mla_w_ukv", "mla_g_qn", "mla_g_qr", "mla_g_kn", "mla_g_kr", "mla_w_o",
          "ffn_w_in", "ffn_conv_w", "ffn_conv_b", "ffn_w_out")


def tables():
    grid, axis, freqs = 64, ROPE // 2, ROPE // 4
    tabs = np.zeros((P, TAB_N), np.float32)
    tabs[:, TAB_IDENT:TAB_IDENT + P] = np.eye(P, dtype=np.float32)
    inv = (np.float32(10000.0) ** (-np.arange(freqs, dtype=np.float32) / np.float32(freqs))).astype(np.float32)
    tok = np.arange(NLAT)
    for p in range(P):
        q, f = p % axis, p % freqs
        pos = tok // grid if (p % ROPE) < axis else tok % grid
        ang = pos.astype(np.float32) * inv[f]
        tabs[p, TAB_COS:TAB_COS + NLAT] = np.cos(ang)
        tabs[p, TAB_SIN:TAB_SIN + NLAT] = np.sin(ang)
        if q < freqs:
            tabs[p + freqs, TAB_SWAP + p] = -1.0
        else:
            tabs[p - freqs, TAB_SWAP + p] = 1.0
        h = p // ROPE
        tabs[p, TAB_HALF + h * ROPE:TAB_HALF + (h + 1) * ROPE] = 1.0
    return tabs


def kernel(**inputs):
    import concourse.bacc as bacc
    from concourse.bass_utils import run_bass_kernel_spmd

    nc = bacc.Bacc("TRN2", target_bir_lowering=False, num_devices=1)
    arrays = {f"in_{n}": np.ascontiguousarray(inputs[n]) for n in INPUTS}
    arrays["in_tabs"] = tables()
    a = {n[3:]: nc.dram_tensor(n, v.shape, mybir.dt.from_np(v.dtype), kind="ExternalInput").ap()
         for n, v in arrays.items()}
    a["out"] = nc.dram_tensor("out", (1, NLAT, D), F32, kind="ExternalOutput").ap()
    build(nc, a)
    r = run_bass_kernel_spmd(nc, [arrays], core_ids=[0])
    return r.results[0]["out"]
```

```python
from contextlib import ExitStack

import numpy as np

import concourse.bass as bass
from concourse import mybir

F32 = mybir.dt.float32
F32R = mybir.dt.float32r
ALU = mybir.AluOpType
ACT = mybir.ActivationFunctionType
AX = mybir.AxisListType

P = 128
D = 1024
KD = D // P
NLAT, NCTX = 512, 256
T = NLAT + NCTX
EPS = 1e-6
GROUPS, CH, STATES, CK = 64, 16, 64, 8
GP = GROUPS // 2
JCTX, JLAT = NCTX // CK, NLAT // CK
J = JCTX + JLAT
DG = 2 * GP
HEADS, NOPE, ROPE, VD, QR, KVR = 8, 128, 64, 128, 768, 256
SCALE = 1.0 / float(np.sqrt(NOPE + ROPE))
FFN = 2816
KF = FFN // P
GF = KF // 2
SLOT = 2 * KD * P
ADA_CHUNKS = 6 * D // 256
ADA_RING = 4
ADA_TURNS = ADA_CHUNKS // ADA_RING
CTX_HOP = (J + 1) + JLAT
LAT_HOP = (J + 1) - JCTX
TWO_PI_HI, TWO_PI_LO = 6.28125, 0.0019353071795864769
ROUND = 12582912.0
PI = 3.1415925

TAB_IDENT, TAB_SWAP, TAB_HALF, TAB_COS, TAB_SIN = 0, P, 2 * P, 3 * P, 3 * P + NLAT
TAB_N = 3 * P + 2 * NLAT

C_ADAB, C_NMIX, C_NFFN = 0, 96, 112
C_C, C_CC, C_GLUB, C_GQ, C_GKV, C_GQN, C_GKN, C_GQR, C_GKR, C_CONVB = 0, 8, 16, 32, 38, 40, 41, 42, 43, 44
SH_M, SC_M, G_M, SH_F, SC_F, G_F = 0, 8, 16, 24, 32, 40


class Chain:

    def __init__(self, eng, sem):
        self.eng, self.sem, self.count, self.turn, self.per = eng, sem, 0, None, 0

    def mark(self, op):
        op.then_inc(self.sem, 1)
        self.count += 1

    def need(self, back):
        n = self.count - back
        self.eng.wait_ge(self.sem, n if self.turn is None else self.turn * self.per + n)

    def link(self, op):
        self.mark(op)
        self.need(0)

    def enter(self, turn, per):
        self.turn, self.per, self.start = turn, per, self.count

    def leave(self, turns):
        assert self.count - self.start == self.per, (self.count - self.start, self.per)
        self.count, self.turn = self.start + self.per * turns, None


B_GLU = 0
B_FFN = (B_GLU + KD, B_GLU + KD + 2 * (GF + KD) + 3 + 6 + 4 + 12 + KD)
B_DKV = B_FFN[0] + 2 * (GF + KD)
B_DQ = B_DKV + 3
B_UKV = B_DQ + QR // P
B_UQ = B_UKV + 4
B_WO = B_UQ + HEADS + HEADS // 2
KV_USES = (4, 4, 6, 6)


JOB_UNITS = (2, 3) + tuple(range(9, 30))


def used_after(c):
    return c + 1 + sum(n - 1 for n in KV_USES[:max(0, c + 1 - B_UKV)])


class Chunk:

    def __init__(self, first, turn=None):
        step = 0 if turn is None else 2 * turn
        self.slot = first % 2
        self.reuse = first >= 2 or turn is not None
        self.n = first + step
        self.nth = (first - B_GLU) // 2 + (0 if turn is None else turn)
        self.done = used_after(first) + step
        self.free = used_after(first - 2) + step
        self.drains = self.done - B_GLU


def stage_turns(eng, count, split, epi):
    split(0, None)
    for m in range(2):
        split(m + 1, None)
        epi(m, m, None)
    pairs = (count - 3) // 2
    if pairs > 0:
        with eng.Fori(1, 1 + pairs) as i:
            for m in range(2):
                split(m + 1, i)
                epi(2 * i + m, m, i)
    for m in range(2 + 2 * max(pairs, 0), count - 1):
        split(m + 1, None)
        epi(m, m, None)
    epi(count - 1, count - 1, None)


def chunk_turns(eng, count, one):
    for m in range(2):
        one(m, m, None)
    if count >= 4:
        with eng.Fori(1, count // 2) as i:
            for m in range(2):
                one(2 * i + m, m, i)
    if count % 2:
        one(count - 1, count - 1, None)


def build(nc, a):
    with ExitStack() as ctx:
        def sb(name, shape, dt=F32, stack=None):
            return (stack or ctx).enter_context(nc.sbuf_tensor(name, shape, dt))

        def sem(name):
            return ctx.enter_context(nc.semaphore(name))

        wraw = sb("wraw", [P, 2, SLOT])
        ident = sb("ident", [P, P])
        ones = sb("ones", [P, P])
        swap = sb("swap", [P, P])
        half_ones = sb("half_ones", [P, P])
        colsA = sb("colsA", [P, 128])
        colsB = sb("colsB", [P, 88])
        colsW = sb("colsW", [P, 2, 66])
        modc = sb("modc", [P, 2, 48, 2])
        gain = sb("gain", [P, 2, 2, KD, 2])
        cond_r = sb("cond_r", [P, KD, 4], F32R)
        fold = sb("fold", [4, 2])
        ada_rows = sb("ada_rows", [4, 256])
        eps = sb("eps", [P, 1])
        wt = sb("wt", [P, 1])
        zero = sb("zero", [P, 1])

        s5 = ExitStack()
        Mr = sb("Mr", [P, 2, 2, 4, P], stack=s5)
        Nr = sb("Nr", [P, 2, 2, 4, P], stack=s5)
        MT = sb("MT", [P, 2, 4, P], stack=s5)
        Kext = sb("Kext", [CH, 4, 15, CH], stack=s5)
        tD = sb("tD", [P, 2, 4, CK, CH], stack=s5)
        tP = sb("tP", [P, 2, 4, CK, CH], stack=s5)
        sb("s5_pad", [P, 64], stack=s5)
        Sarr = sb("Sarr", [P, 2, J + 1, 2, GP], stack=s5)
        TT = sb("TT", [P, GROUPS, P], stack=s5)
        Bc = sb("Bc", [P, 2, DG, CH], stack=s5)
        Cc = sb("Cc", [P, 2, DG, CH], stack=s5)
        pw = sb("pw", [P, 2, DG, 9], stack=s5)
        QP = sb("QP", [P, 2, 2, DG, CK], stack=s5)
        Qk, Pk = QP[:, 0], QP[:, 1]
        Pn = sb("Pn", [P, 2, DG, CK], stack=s5)
        U = sb("U", [P, GROUPS, J], stack=s5)
        s5.close()
        pre = ExitStack()
        sb("pre_gap", [P, 4 * SLOT], stack=pre)
        rowsA = sb("rowsA", [P, P], stack=pre)
        rowsB = sb("rowsB", [88, P], stack=pre)
        rowsW = sb("rowsW", [66, 2, P], stack=pre)
        lam = sb("lam", [DG, 2, P], stack=pre)
        ldt = sb("ldt", [DG, 2], stack=pre)
        brow = sb("brow", [DG, 2, 2048], stack=pre)
        crow = sb("crow", [DG, 2, 2048], stack=pre)
        disc = sb("disc", [DG, 12, P], stack=pre)
        sc4 = sb("sc4", [P, 8, CK * 4], stack=pre)
        sgc = sb("sgc", [P, 16], stack=pre)
        drow = sb("drow", [GROUPS, CH], stack=pre)
        cs = sb("cs", [P, 16], stack=pre)
        pre.close()
        pre3 = ExitStack()
        sb("pre3_gap", [P, 4 * SLOT], stack=pre3)
        xn = sb("xn", [J, GROUPS, CK, CH], stack=pre3)
        pre3.close()
        pre2 = ExitStack()
        sb("pre2_gap", [P, 4 * SLOT + (J + 1) * P], stack=pre2)
        xin = sb("xin", [J, CK, D], stack=pre2)
        pre2.close()
        late = ExitStack()
        sb("late_gap", [P, 4 * SLOT + (J + 1) * P + GROUPS * P + 2 * 2 * DG * CH + 2 * DG * 9 + 6 * DG * CK + GROUPS * J],
           stack=late)
        acoef = sb("acoef", [P, 4, DG], stack=late)
        cm = sb("cm", [P, 2, DG, 8], stack=late)
        stat = sb("stat", [J, 2, CK], stack=late)
        urep = sb("urep", [P, 2, 2, GROUPS], stack=late)
        kd = sb("kd", [CH, GROUPS, CH], stack=late)
        d16 = sb("d16", [CH, GROUPS], stack=late)
        a8 = sb("a8", [P, 2, 2, 2, GP], stack=late)
        sc = sb("sc", [P, 2, 3, 2, GP], stack=late)
        pick = sb("pick", [P, KD, CK, CH], stack=late)
        yst = pick[0:J].rearrange("j a k c -> j (a k c)").rearrange("j (k n) -> j k n", k=CK)
        late.close()

        whi = sb("whi", [P, 2, SLOT], F32R)
        wlo = sb("wlo", [P, 2, SLOT], F32R)
        kv = ExitStack()
        kn = sb("kn", [P, HEADS, T], stack=kv)
        val = sb("val", [P, 6, HEADS * VD], stack=kv)
        kv.close()
        hhi = sb("hhi", [P, KD, T], F32R)
        hlo = sb("hlo", [P, KD, T], F32R)
        xT = sb("xT", [P, KD, T])
        ffn = ExitStack()
        ghi = sb("ghi", [P, GF, T], F32R, stack=ffn)
        glo = sb("glo", [P, GF, T], F32R, stack=ffn)
        acc = sb("acc", [P, 2, T], stack=ffn)
        ffn.close()
        nrm = ExitStack()
        sq = sb("sq", [P, KD, T], stack=nrm)
        ssum = sb("ssum", [P, T], stack=nrm)
        rstd = sb("rstd", [P, T], stack=nrm)
        hx = sb("hx", [P, 2, T], stack=nrm)
        nrm.close()
        mla = ExitStack()
        q_all = sb("q_all", [P, 12, NLAT], stack=mla)
        kr = sb("kr", [P, T], stack=mla)
        rope_cs = sb("rope_cs", [P, 2, NLAT], stack=mla)
        rs = sb("rs", [P, T], stack=mla)
        ckv_hi = sb("ckv_hi", [P, 2, T], F32R, stack=mla)
        ckv_lo = sb("ckv_lo", [P, 2, T], F32R, stack=mla)
        cq_hi = sb("cq_hi", [P, 6, NLAT], F32R, stack=mla)
        cq_lo = sb("cq_lo", [P, 6, NLAT], F32R, stack=mla)
        sqr = sb("sqr", [P, 2, T], stack=mla)
        mla.close()
        raw = ExitStack()
        ckv_raw = sb("ckv_raw", [P, 2, T], stack=raw)
        cq_raw = sb("cq_raw", [P, 6, NLAT], stack=raw)
        raw.close()
        att = ExitStack()
        sb("att_gap", [P, 12 * NLAT + T + 2 * NLAT + T], stack=att)
        pr = sb("pr", [P, 2, T], stack=att)
        pT = sb("pT", [P, 2, 6, NLAT], stack=att)
        ot = sb("ot", [P, HEADS, NLAT], stack=att)
        smax = sb("smax", [P, 2, 4], stack=att)
        att.close()
        glu = ExitStack()
        xin2 = sb("xin2", [J, CK, D], stack=glu)
        glu.close()
        glu2 = ExitStack()
        sb("glu2_gap", [P, 2 * GF * T], stack=glu2)
        sig = sb("sig", [P, 2, T], stack=glu2)
        glu2.close()

        ps = ctx.enter_context(nc.psum_tensor("ps", [P, 8, 512], F32))
        flat = ps[:].rearrange("p b n -> p (b n)")

        names = """params_in lam_in s5rows_in d16_in x_in tabs_in const_set cols_T cols_out cond_ready act_link dve_link pool_link
            ada_in0 ada_in1 ada_in2 ada_in3 wload0 wload1 ada_hi_set ada_lo_dve ada_lo_pool ada_used row_out ada_folded hi_ready lo_ready w_used drained
            rowsum_done rstd_set dt_set disc_a disc_b exp_done sin_done disc_T disc_out bc_T bc_out tab_set
            ada0_set rep_done rep_out u_T u_dve u_act kd_set
            m_ready n_ready mt_T mt_out k_done kf_out kext_ready tt_in s_done sf_out sb_out s_zero
            scanned half_scanned half_saved pn_set n2m n2_re n2_im y_done y_out z_T z_out z_hi z_lo x2_in xT_T xT_out
            sig_done act_acc dve_g hi_g g_split mix_done
            sq_done ssum_done stat_T std_done rinv xn_done hx_done h_hi h_lo
            acc_set conv_done silu_done g_done g_hi g_lo rope_in
            unit_sq unit_used job_std ckv_set cq_set swap_T rot_done job_rinv job_out ckv_hi_s ckv_lo_s cq_hi_s cq_lo_s kr_swap kr_set q_swap q_set
            kv_out sc_done mx_set ex_done pr_set p_T pT_out pv_done ot_out o_hi o_lo
            fin_T fin_out out_done ssum_set""".split()
        S = {n: sem(n) for n in names}
        wload = (S["wload0"], S["wload1"])

        def wview(t, slot, k, n=P):
            return t[:, slot, 0:k * n].rearrange("p (k n) -> p k n", k=k)

        def glu_psum(q):
            return ps[:, 3 * q, :], ps[:, 3 * q + 1, :], ps[:, 3 * q + 2, 0:NCTX], ps[:, 3 * q + 2, NCTX:2 * NCTX]

        U_rows = U[:].rearrange("p g j -> p (g j)")
        ada_raw = ([wraw[:, 0], wraw[:, 1], U_rows[:, 0:SLOT], U_rows[:, SLOT:2 * SLOT]],
                   [wraw[:, 0], wraw[:, 1], Bc[:].rearrange("p r g c -> p (r g c)"), QP[:].rearrange("p q r g k -> p (q r g k)")])
        ada_in = [S[f"ada_in{r}"] for r in range(ADA_RING)]

        def hhi_out(t):
            return sq[:].rearrange("p k t -> p (k t)")[:, t * D:(t + 1) * D]

        ada_whi, ada_wlo = (w[:].rearrange("p s n -> p (s n)").rearrange("p (s n) -> p s n", s=4) for w in (whi, wlo))

        def ada_half(l, r, q):
            return ada_raw[l][r][:, SLOT // 2 * q:SLOT // 2 * (q + 1)]

        def u_parts(q):
            return [(4 * q + r, j0, j1, cond) for r in range(4) for j0, j1, cond in ((0, JCTX, 1), (JCTX, J, 0))]

        POOL_R = ADA_RING - 1

        def ada_split(eng, l, r, turn, q):
            if l == 0 and r != POOL_R:
                eng.wait_ge(S["ada_lo_dve"], 2 * POOL_R * turn + 2 * r + q + 1)
            elif l == 0:
                eng.wait_ge(S["ada_lo_pool"], 2 * turn + q + 1)
            else:
                eng.wait_ge(S["ada_lo_pool"], 2 * ADA_RING * turn + (2 * ADA_TURNS + 2 * r + q + 1))

        def ada_lo(eng, done, l, r, turn):
            for q in range(2):
                m = 2 * (l * ADA_CHUNKS + ADA_RING * turn + r) + q
                eng.wait_ge(S["ada_hi_set"], m + 1)
                slot = (2 * r + q) % 4
                eng.tensor_tensor(ada_wlo[:, slot], ada_half(l, r, q), ada_whi[:, slot].bitcast(F32), ALU.subtract)\
                    .then_inc(done, 1)

        block = ctx.enter_context(nc.Block())

        @block.sync
        def _(sp):
            rows = "o d (g h) s -> (o d g) (h s)"
            sp.dma_start(lam[:, 0, :], a["s5_lam_re"].rearrange(rows, h=2)).then_inc(S["lam_in"], 16)
            sp.dma_start(lam[:, 1, :], a["s5_lam_im"].rearrange(rows, h=2)).then_inc(S["lam_in"], 16)
            sp.dma_start(ldt[:], a["s5_log_dt"].rearrange("o d (g h) -> (o d g) h", h=2)).then_inc(S["lam_in"], 16)
            sp.dma_start(rowsB[C_C:C_C + 8, :], a["c"].rearrange("o (r c) -> (o r) c", c=P)).then_inc(S["params_in"], 16)
            sp.dma_start(rowsB[C_CC:C_CC + 8, :], a["c_ctx"].rearrange("(r c) -> r c", c=P)).then_inc(S["params_in"], 16)
            sp.dma_start(rowsA[0:96, :], a["ada_b"].rearrange("l (r c) -> (l r) c", c=P)).then_inc(S["params_in"], 16)
            sp.dma_start(rowsA[96:112, :], a["norm_mix"].rearrange("l (r c) -> (l r) c", c=P)).then_inc(S["params_in"], 16)
            sp.dma_start(rowsA[112:128, :], a["norm_ffn"].rearrange("l (r c) -> (l r) c", c=P)).then_inc(S["params_in"], 16)
            for at, name in ((C_GLUB, "s5_glu_b"), (C_GQ, "mla_g_q"), (C_GKV, "mla_g_kv"), (C_GQN, "mla_g_qn"),
                             (C_GKN, "mla_g_kn"), (C_CONVB, "ffn_conv_b")):
                src = a[name].rearrange("l (r c) -> (l r) c", c=P)
                sp.dma_start(rowsB[at:at + src.shape[0], :], src).then_inc(S["params_in"], 16)
            for at, name in ((C_GQR, "mla_g_qr"), (C_GKR, "mla_g_kr")):
                for h in range(2):
                    sp.dma_start(rowsB[at:at + 1, h * ROPE:(h + 1) * ROPE], a[name]).then_inc(S["params_in"], 16)
            for l in range(2):
                sp.dma_start(rowsW[:, l, :], a["ffn_conv_w"][l].rearrange("t (r c) -> (t r) c", c=P))\
                    .then_inc(S["params_in"], 16)
            for t, at in ((ident, TAB_IDENT), (swap, TAB_SWAP), (half_ones, TAB_HALF)):
                sp.dma_start(t[:], a["tabs"][:, at:at + P]).then_inc(S["params_in"], 16)
            sp.dma_start(drow[:], a["s5_d"].rearrange("o (g c) -> (o g) c", c=CH)).then_inc(S["params_in"], 16)

            def ada_load(l, r, turn):
                if not (isinstance(turn, int) and turn == 0):
                    ada_split(sp, l, r, turn - 1, 1)
                w = a["ada_w"][l].rearrange("(k p) n -> p k n", p=P)
                sp.dma_start(ada_raw[l][r].rearrange("p (k n) -> p k n", k=KD),
                             w[:, :, bass.ds((ADA_RING * turn + r) * 256, 256)]).then_inc(ada_in[r], 16)

            def ada_turns(l):
                with sp.Fori(1, ADA_TURNS) as i:
                    for r in range(ADA_RING):
                        ada_load(l, r, i)

            for r in range(ADA_RING):
                ada_load(0, r, 0)
            for q, name in ((0, "s5_b_re"), (1, "s5_b_im")):
                sp.dma_start(brow[:, q, :], a[name].rearrange("o d (g h) x y -> (o d g) (h x y)", h=2))\
                    .then_inc(S["s5rows_in"], 16)
            for q, name in ((0, "s5_c_re"), (1, "s5_c_im")):
                for h in range(2):
                    sp.dma_start(crow[:, q, :].rearrange("p (c h s) -> p h c s", h=2, c=CH)[:, h],
                                 a[name].rearrange("o d (g h) c s -> (o d g) h c s", h=2)[:, h]).then_inc(S["s5rows_in"], 16)
            ada_turns(0)
            for r in range(2):
                ada_split(sp, 0, r, ADA_TURNS - 1, 1)
                ada_load(1, r, 0)

            def toeplitz(b, n):
                sp.wait_ge(S["kext_ready"], n + 1)
                for k in range(CK):
                    sp.dma_start(TT[CH * k:CH * (k + 1), bass.ds(4 * b, 4), :],
                                 Kext[:, :, CK - 1 - k:2 * CK - 1 - k, :].rearrange("c g t o -> c g (t o)"))\
                        .then_inc(S["tt_in"], 16)

            with sp.Fori(0, GP // 2) as b:
                toeplitz(b, b)

            sp.wait_ge(S["m_ready"], GP // 2)
            sp.wait_ge(S["n_ready"], GP // 2)
            for r in range(2, ADA_RING):
                ada_load(1, r, 0)
            ada_turns(1)

            sp.wait_ge(S["scanned"], 2)
            sp.wait_ge(S["z_out"], 2 * KD)
            for dst, src in ((xin2[0:JCTX], a["ctx"]), (xin2[JCTX:J], a["x"])):
                sp.dma_start(dst, src.rearrange("o (j k) d -> (o j) k d", k=CK)).then_inc(S["x2_in"], 16)

            def stage(first, count, fill):
                def one(m, c, turn):
                    ch = Chunk(first + c, turn)
                    if ch.reuse:
                        sp.wait_ge(S["lo_ready"], ch.n - 1)
                    moves = fill(ch.slot, m)
                    for dst, src in moves:
                        sp.dma_start(dst, src).then_inc(wload[ch.slot], 32 // len(moves))
                chunk_turns(sp, count, one)

            def half(w):
                v = w.rearrange("(k p) (h n) -> p k h n", p=P, h=2)
                return lambda slot, m: [(wraw[:, slot, :].rearrange("p (h k n) -> p h k n", h=2, n=P)[:, h],
                                         v[:, :, h, bass.ds(m * P, P)]) for h in range(2)]

            def whole(w):
                v = w.rearrange("(k p) n -> p k n", p=P)
                return lambda slot, m: [(wview(wraw, slot, w.shape[0] // P), v[:, :, bass.ds(m * P, P)])]

            stage(B_GLU, KD, half(a["s5_glu_w"][0]))

            def ffn_weights(l):
                for g in range(2):
                    wi = a["ffn_w_in"][l].rearrange("(k p) (h n) -> p k h n", p=P, h=2)[:, :, :, g * GF * P:(g + 1) * GF * P]
                    stage(B_FFN[l] + g * (GF + KD), GF, lambda slot, m: [
                        (wraw[:, slot, :].rearrange("p (h k n) -> p h k n", h=2, n=P)[:, h],
                         wi[:, :, h, bass.ds(m * P, P)]) for h in range(2)])
                    stage(B_FFN[l] + g * (GF + KD) + GF, KD, whole(a["ffn_w_out"][l][g * GF * P:(g + 1) * GF * P, :]))

            ffn_weights(0)
            dkv = a["mla_w_dkv"][0].rearrange("(k p) n -> p k n", p=P)
            stage(B_DKV, 3, lambda slot, m: [(wview(wraw, slot, KD), dkv[:, :, m * P:(m + 1) * P])] if m < 2 else
                  [(wview(wraw, slot, KD)[:, :, ROPE * h:ROPE * (h + 1)], dkv[:, :, KVR:]) for h in range(2)])
            stage(B_DQ, QR // P, whole(a["mla_w_dq"][0]))
            ukv = a["mla_w_ukv"][0].rearrange("(k p) (h v n) -> p k v h n", p=P, h=HEADS, v=2)
            for m in range(4):
                ch = Chunk(B_UKV + m)
                sp.wait_ge(S["lo_ready"], ch.n - 1)
                for k in range(2):
                    sp.dma_start(wview(wraw, ch.slot, 2, 4 * P)[:, k, :].rearrange("p (h n) -> p h n", h=4),
                                 ukv[:, k, m // 2, 4 * (m % 2):4 * (m % 2) + 4, :]).then_inc(wload[ch.slot], 16)
            uq = a["mla_w_uq"][0].rearrange("(k p) (h n) -> p k h n", p=P, h=HEADS)
            stage(B_UQ, HEADS, lambda slot, m: [(wview(wraw, slot, 6),
                                                 uq[:, :, bass.ds(m, 1), 0:NOPE].rearrange("p k o n -> p k (o n)"))])
            for m in range(HEADS // 2):
                ch = Chunk(B_UQ + HEADS + m)
                sp.wait_ge(S["lo_ready"], ch.n - 1)
                for h in range(2):
                    sp.dma_start(wview(wraw, ch.slot, 6)[:, :, ROPE * h:ROPE * (h + 1)], uq[:, :, 2 * m + h, NOPE:])\
                        .then_inc(wload[ch.slot], 16)
                if m == 0:
                    sp.wait_ge(S["h_lo"], 2 * KD)
                    sp.dma_start(rope_cs[:].rearrange("p a t -> p (a t)"), a["tabs"][:, TAB_COS:]).then_inc(S["rope_in"], 16)
            stage(B_WO, KD, whole(a["mla_w_o"][0]))
            ffn_weights(1)

            sp.wait_ge(S["fin_out"], 8)
            sp.wait_ge(S["out_done"], 16 * 4)

        @block.gpsimd
        def _(pool):
            chain = Chain(pool, S["pool_link"])
            pool.wait_ge(S["params_in"], 16 * 21)
            pool.tensor_copy(pick[:], ident[:].rearrange("p (g c) -> p g c", c=CH).unsqueeze(2)
                             .to_broadcast([P, KD, CK, CH])).then_inc(S["tabs_in"], 1)
            with pool.Fori(0, ADA_TURNS) as i:
                ada_lo(pool, S["ada_lo_pool"], 0, POOL_R, i)
            def n_block(b, q, n):
                dg = bass.ds(4 * b, 4)
                if n is not None:
                    pool.wait_ge(S["n_ready"], n + 1)
                    pool.wait_ge(S["k_done"], n)
                    pool.tensor_tensor(wt[:], zero[:], zero[:], ALU.add)
                p_re, p_im = (Pk[:, r, dg, :].unsqueeze(3).to_broadcast([P, 4, CK, CH]) for r in range(2))
                c_re, c_ni = (Cc[:, r, dg, :].unsqueeze(2).to_broadcast([P, 4, CK, CH]) for r in range(2))
                dst = [Nr[:, q, r].rearrange("p g (k c) -> p g k c", k=CK) for r in range(2)]
                pool.tensor_tensor(dst[0], p_re, c_re, ALU.mult)
                pool.tensor_tensor(tP[:, 0], p_im, c_ni, ALU.mult)
                pool.tensor_tensor(dst[1], p_re, c_ni, ALU.mult)
                chain.link(pool.tensor_tensor(tP[:, 1], p_im, c_re, ALU.mult))
                pool.tensor_tensor(dst[0], dst[0], tP[:, 0], ALU.add)
                pool.tensor_tensor(dst[1], dst[1], tP[:, 1], ALU.subtract).then_inc(S["n_ready"], 1)

            pool.wait_ge(S["tab_set"], 1)
            pool.wait_ge(S["ada_used"], 2 * ADA_CHUNKS)
            for q in range(2):
                n_block(q, q, None)
                if q == 0:
                    pool.wait_ge(S["n_ready"], 1)
            with pool.Fori(1, GP // 4) as i:
                chain.enter(i - 1, 2)
                for q in range(2):
                    n_block(2 * i + q, q, 2 * i + q - 1)
            chain.leave(GP // 4 - 1)

            pool.wait_ge(S["s_done"], GP // 2)
            pool.wait_ge(S["tt_in"], 128 * (GP // 2))
            with pool.Fori(0, ADA_TURNS) as i:
                for r in range(ADA_RING):
                    ada_lo(pool, S["ada_lo_pool"], 1, r, i)
            pool.wait_ge(S["ada_used"], 4 * ADA_CHUNKS)
            pool.wait_ge(S["scanned"], 2)
            for hb in range(GP // 2):
                dg = slice(4 * hb, 4 * hb + 4)
                p_re, p_im = (Pn[:, r, dg, :].unsqueeze(3).to_broadcast([P, 4, CK, CH]) for r in range(2))
                c_re, c_ni = (Cc[:, r, dg, :].unsqueeze(2).to_broadcast([P, 4, CK, CH]) for r in range(2))
                if hb >= 2:
                    pool.wait_ge(S["y_done"], hb - 1)
                pool.tensor_tensor(tP[:, 0], p_re, c_ni, ALU.mult)
                chain.link(pool.tensor_tensor(tP[:, 1], p_im, c_re, ALU.mult))
                pool.tensor_tensor(Nr[:, hb % 2, 1].rearrange("p g (k c) -> p g k c", k=CK),
                                   tP[:, 0], tP[:, 1], ALU.subtract).then_inc(S["n2_im"], 1)
                pool.wait_ge(S["n2_im"], hb + 1)
            for b in range(KD):
                pool.wait_ge(S["z_hi"], b + 1)
                pool.tensor_tensor(hlo[:, b, :], U[:].rearrange("p g j -> p (g j)")[:, T * b:T * b + T],
                                   hhi[:, b, :].bitcast(F32), ALU.subtract).then_inc(S["z_lo"], 1)

            def norm_low(j, toks):
                for b in range(KD):
                    n = KD * j + b + 1
                    pool.wait_ge(S["h_hi"], n)
                    pool.tensor_tensor(hlo[:, b, 0:toks], hx[:, b % 2, 0:toks], hhi[:, b, 0:toks].bitcast(F32),
                                       ALU.subtract).then_inc(S["h_lo"], 1)

            def ffn_low(l, toks):
                for g in range(2):
                    def one(m, c, turn):
                        ch = Chunk(B_FFN[l] + g * (GF + KD) + c, turn)
                        f = KF * l + GF * g + m
                        if l or g or turn is not None or c:
                            pool.wait_ge(S["g_lo"], f)
                        pool.wait_ge(S["g_hi"], f + 1)
                        pool.tensor_tensor(wt[:], zero[:], zero[:], ALU.add)
                        pool.tensor_tensor(glo[:, bass.ds(m, 1), 0:toks].rearrange("p a t -> p (a t)"), acc[:, ch.slot, 0:toks],
                                           ghi[:, bass.ds(m, 1), 0:toks].bitcast(F32).rearrange("p a t -> p (a t)"),
                                           ALU.subtract).then_inc(S["g_lo"], 1)
                    chunk_turns(pool, GF, one)

            norm_low(0, T)
            ffn_low(0, T)
            norm_low(1, T)
            for b in range(2):
                pool.wait_ge(S["ckv_hi_s"], b + 1)
                pool.tensor_tensor(ckv_lo[:, b, :], ckv_raw[:, b, :], ckv_hi[:, b, :].bitcast(F32), ALU.subtract)\
                    .then_inc(S["ckv_lo_s"], 1)
            for b in range(6):
                pool.wait_ge(S["cq_hi_s"], b + 1)
                pool.tensor_tensor(cq_lo[:, b, :], cq_raw[:, b, :], cq_hi[:, b, :].bitcast(F32), ALU.subtract)\
                    .then_inc(S["cq_lo_s"], 1)
            for h in range(HEADS):
                pool.wait_ge(S["o_hi"], h + 1)
                pool.tensor_tensor(hlo[:, h, 0:NLAT], ot[:, h, :], hhi[:, h, 0:NLAT].bitcast(F32), ALU.subtract)\
                    .then_inc(S["o_lo"], 1)
            norm_low(2, NLAT)
            ffn_low(1, NLAT)

        @block.scalar
        def _(act):
            chain = Chain(act, S["act_link"])
            act.wait_ge(S["const_set"], 3)
            act.wait_ge(S["cols_T"], 1)
            act.activation(colsB[:], flat[:, 128:216], ACT.Copy).then_inc(S["cols_out"], 1)
            act.activation(colsA[:], flat[:, 0:128], ACT.Copy).then_inc(S["cols_out"], 1)
            act.activation(colsW[:], flat[:, 256:388], ACT.Copy).then_inc(S["cols_out"], 1)
            act.activation(d16[:], flat[0:CH, 400:464], ACT.Copy).then_inc(S["cols_out"], 1)
            act.wait_ge(S["cols_out"], 4)
            chain.link(act.activation(sgc[:], colsB[:, 0:16], ACT.Sigmoid))
            act.wait_ge(S["const_set"], 4)
            act.activation(cond_r[:, :, 0:2].rearrange("p k w -> p w k"), cs[:].rearrange("p (w k) -> p w k", w=2),
                           ACT.Copy).then_inc(S["cond_ready"], 1)
            def ada_row(n, r):
                act.wait_ge(S["ada_used"], 2 * n + 2)
                if not (isinstance(n, int) and n < 1):
                    act.wait_ge(S["ada_folded"], n)
                act.activation(ada_rows[:], ps[0:4, 6 * (r % 2), 0:256], ACT.Copy).then_inc(S["row_out"], 1)

            def ada_hi(l, r, turn):
                n = l * ADA_CHUNKS + ADA_RING * turn + r
                act.wait_ge(ada_in[r], 16 * (l * ADA_TURNS + turn + 1))
                for q in range(2):
                    if not (isinstance(n, int) and n < 2):
                        act.wait_ge(S["ada_used"], 2 * n + q - 3)
                    act.activation(ada_whi[:, (2 * r + q) % 4], ada_half(l, r, q), ACT.Copy).then_inc(S["ada_hi_set"], 1)
                if not (isinstance(turn, int) and turn == r == 0):
                    ada_row(n - 1, r - 1)

            def ada_turn(turn):
                for r in range(ADA_RING):
                    ada_hi(0, r, turn)

            def hi(ch, n):
                act.wait_ge(wload[ch.slot], 32 * ch.nth + 32)
                if ch.reuse:
                    act.wait_ge(S["w_used"], ch.free)
                act.activation(whi[:, ch.slot, 0:n], wraw[:, ch.slot, 0:n], ACT.Copy).then_inc(S["hi_ready"], 1)

            act.wait_ge(S["lam_in"], 16 * 3)
            act.activation(ldt[:], ldt[:], ACT.Exp).then_inc(S["dt_set"], 1)
            act.wait_ge(S["disc_a"], 1)
            act.activation(disc[:, 2, :], disc[:, 0, :], ACT.Exp).then_inc(S["exp_done"], 1)
            act.wait_ge(S["disc_b"], 1)
            act.activation(disc[:, 3, :], disc[:, 1, :], ACT.Sin)
            act.activation(disc[:, 4, :], disc[:, 1, :], ACT.Sin, scale=0.5).then_inc(S["sin_done"], 1)
            ada_turn(0)
            ada_turn(1)
            act.wait_ge(S["disc_T"], 1)
            act.activation(acoef[:].rearrange("p q (g d) -> p q d g", d=2),
                           flat[:, 512:768].rearrange("p (q d g) -> p q d g", q=4, d=2), ACT.Copy).then_inc(S["disc_out"], 1)
            for n, (dst, q) in enumerate(((Bc, 0), (Bc, 1), (Cc, 0), (Cc, 1))):
                if n == 2:
                    ada_turn(2)
                for h in range(4):
                    act.wait_ge(S["bc_T"], 4 * n + h + 1)
                    act.activation(dst[:, q, :, 4 * h:4 * h + 4].rearrange("p g c -> p c g"),
                                   ps[:, 2 + h % 4, 0:256].rearrange("p (c g) -> p c g", c=4),
                                   ACT.Copy, scale=-1.0 if n == 3 else 1.0).then_inc(S["bc_out"], 1)
            act.wait_ge(S["bc_out"], 16)
            act.wait_ge(S["disc_out"], 1)
            for dst, src in ((xin[0:JCTX], a["ctx"]), (xin[JCTX:J], a["x"])):
                act.dma_start(dst, src.rearrange("o (j k) d -> (o j) k d", k=CK)).then_inc(S["x_in"], 16)
            ada_turn(3)
            act.wait_ge(S["x_in"], 32)
            for k in range(CK):
                chain.link(act.activation(flat[0:J, 2048:2048 + D], xin[:, k, :], ACT.Square,
                                          accum_out=stat[:, 0, k:k + 1]))
            act.activation(stat[:, 0, :], stat[:, 0, :], ACT.Sqrt, bias=eps[0:J, :], scale=1.0 / D)\
                .then_inc(S["rowsum_done"], 1)
            ada_turn(4)
            ada_turn(5)
            ada_row(ADA_CHUNKS - 1, ADA_RING - 1)

            act.wait_ge(S["rep_out"], 1)
            for q in range(1, GROUPS // 4, 2):
                act.wait_ge(S["u_T"], q + 1)
                for g, j0, j1, cond in u_parts(q):
                    last = act.activation(U[:, g, j0:j1], ps[:, q % 4, P * (g % 4) + j0:P * (g % 4) + j1], ACT.Identity,
                                          scale=urep[:, 0, cond, g:g + 1], bias=urep[:, 1, cond, g:g + 1])
                last.then_inc(S["u_act"], 1)

            def s5_block(b, n, first):
                act.wait_ge(S["mt_T"], n + 1)
                if not first:
                    act.wait_ge(S["s_done"], n)
                act.activation(MT[:].rearrange("p r g s -> p (r g s)"), flat[:, 0:1024], ACT.Copy).then_inc(S["mt_out"], 1)
                act.wait_ge(S["k_done"], n + 1)
                if not first:
                    act.wait_ge(S["tt_in"], 128 * n)
                act.activation(Kext[:].rearrange("c (g h) t o -> c g h (t o)", h=2)[:, :, :, 7 * CH:],
                               ps[0:CH, 2:4, 0:256].rearrange("c h (g x) -> c g h x", g=2), ACT.Copy).then_inc(S["kf_out"], 1)
                act.wait_ge(S["s_done"], n + 1)
                for h in range(2):
                    rows = slice(STATES * h, STATES * (h + 1))
                    last = act.activation(Sarr[rows, 0, 1:J + 1, :, bass.ds(2 * b, 2)].rearrange("p j r g -> p r g j"),
                                          ps[rows, 4:6, :].rearrange("p r (g x) -> p r g x", g=2)[:, :, :, J * h:J * (h + 1)],
                                          ACT.Copy)
                last.then_inc(S["sf_out"], 1)

            s5_block(0, 0, True)
            with act.Fori(1, GP // 2) as b:
                s5_block(b, b, False)

            for r in range(ADA_RING):
                ada_hi(1, r, 0)
            with act.Fori(1, ADA_TURNS) as i:
                for r in range(ADA_RING):
                    ada_hi(1, r, i)
            ada_row(2 * ADA_CHUNKS - 1, ADA_RING - 1)

            ada_split(act, 1, ADA_RING - 1, ADA_TURNS - 1, 1)
            act.wait_ge(S["half_scanned"], 1)
            saved = wraw[:].rearrange("p s n -> p (s n)")[:, 0:J // 2 * 2 * GP].rearrange("p (s x) -> p s x", x=2 * GP)
            back = Sarr[:, 1].rearrange("p s r g -> p s (r g)")
            act.activation(saved, back[:, 0:J // 2], ACT.Copy).then_inc(S["half_saved"], 1)
            act.wait_ge(S["scanned"], 1)
            act.activation(back[:, J - 1:J // 2 - 1:-1], saved, ACT.Copy).then_inc(S["scanned"], 1)

            for b in range(KD):
                act.wait_ge(S["y_done"], 2 * b + 2)
                if b >= 1:
                    act.wait_ge(S["z_T"], 2 * b)
                for h in range(2):
                    last = act.activation(yst.rearrange("j k (g h c) -> j h g k c", h=2, c=CH)[:, h],
                                          ps[0:J, 2 * (b % 2) + h, :].rearrange("j (g k c) -> j g k c", k=CK, c=CH),
                                          ACT.Gelu_apprx_tanh)
                last.then_inc(S["y_out"], 1)
            for b in range(KD):
                act.wait_ge(S["z_out"], 2 * KD)
                act.wait_ge(S["y_done"], 2 * KD)
                act.activation(hhi[:, b, :], U[:].rearrange("p g j -> p (g j)")[:, T * b:T * b + T], ACT.Copy)\
                    .then_inc(S["z_hi"], 1)

            def stage(first, count, n, epi):
                stage_turns(act, count, lambda c, turn: hi(Chunk(first + c, turn), n),
                            lambda m, c, turn: epi(m, Chunk(first + c, turn), turn is None and c < 2))

            def glu_epi(m, ch, early):
                a_l, g_l, a_c, g_c = glu_psum(ch.slot)
                act.wait_ge(S["w_used"], ch.done)
                if not early:
                    act.wait_ge(S["mix_done"], m - 1)
                bias = colsB[:, bass.ds(C_GLUB + KD + m, 1)]
                act.activation(sig[:, ch.slot, 0:NLAT], g_l, ACT.Sigmoid, bias=bias)
                act.activation(sig[:, ch.slot, NLAT:], g_c, ACT.Sigmoid, bias=bias).then_inc(S["sig_done"], 1)

            stage(B_GLU, KD, SLOT, glu_epi)

            def norm(j, l, q, toks, ready):
                act.wait_ge(*ready)
                for b in range(KD):
                    act.activation(sq[:, b, 0:toks], xT[:, b, 0:toks], ACT.Square).then_inc(S["sq_done"], 1)
                act.wait_ge(S["stat_T"], j + 1)
                act.activation(rstd[:, 0:toks], flat[:, 3072:3072 + toks], ACT.Sqrt, bias=eps[:], scale=1.0 / D)\
                    .then_inc(S["std_done"], 1)
                for b in range(KD):
                    n = KD * j + b + 1
                    act.wait_ge(S["xn_done"], n)
                    for t0, t1, cond in ((0, NLAT, 0), (NLAT, T, 1))[:1 if toks == NLAT else 2]:
                        v = hx[:, b % 2, t0:t1]
                        last = act.activation(v, v, ACT.Identity, scale=gain[:, l, q, b, cond:cond + 1],
                                              bias=modc[:, l, (SH_M, SH_F)[q] + b, cond:cond + 1])
                    last.then_inc(S["hx_done"], 1)
                    act.wait_ge(S["hx_done"], n)
                    act.activation(hhi[:, b, 0:toks], hx[:, b % 2, 0:toks], ACT.Copy).then_inc(S["h_hi"], 1)

            def ffn(l, toks):
                spans = ((0, NLAT), (NLAT, T))[:1 if toks == NLAT else 2]
                for g in range(2):
                    def epi(m, ch, early):
                        f = KF * l + GF * g + m
                        a_l, _, a_c, _ = glu_psum(ch.slot)
                        act.wait_ge(S["w_used"], ch.done)
                        if l or g or not early:
                            act.wait_ge(S["g_lo"], f - 1)
                        for (t0, t1), src in zip(spans, (a_l, a_c)):
                            last = act.activation(acc[:, ch.slot, t0:t1], src, ACT.Identity,
                                                  scale=colsW[:, l, bass.ds(KF + GF * g + m, 1)],
                                                  bias=colsB[:, bass.ds(C_CONVB + KF * l + GF * g + m, 1)])
                        last.then_inc(S["acc_set"], 1)
                        act.wait_ge(S["conv_done"], f + 1)
                        v = acc[:, ch.slot, 0:toks]
                        act.activation(v, v, ACT.Silu).then_inc(S["silu_done"], 1)
                        act.wait_ge(S["drained"], ch.drains)
                        act.activation(ghi[:, bass.ds(m, 1), 0:toks].rearrange("p a t -> p (a t)"), v, ACT.Copy)\
                            .then_inc(S["g_hi"], 1)
                    stage(B_FFN[l] + g * (GF + KD), GF, SLOT, epi)
                    stage(B_FFN[l] + g * (GF + KD) + GF, KD, GF * P, lambda m, ch, early: None)

            norm(0, 0, 1, T, (S["mix_done"], KD))
            ffn(0, T)
            norm(1, 1, 0, T, (S["drained"], B_DKV - B_GLU))

            def square(u, src, n):
                if u >= 2:
                    act.wait_ge(S["unit_used"], u - 1)
                act.activation(sqr[:, u % 2, 0:n], src, ACT.Square).then_inc(S["unit_sq"], 1)

            def root(j, n, mean):
                act.wait_ge(S["unit_used"], JOB_UNITS[j])
                if j >= 1:
                    act.wait_ge(S["job_out"], JOB_UNITS[j - 1])
                act.activation(rs[:, 0:n], flat[:, 3072:3072 + n], ACT.Sqrt, bias=eps[:], scale=1.0 / mean)\
                    .then_inc(S["job_std"], 1)

            hi(Chunk(B_DKV), KD * P)
            for m in range(3):
                if m < 2:
                    hi(Chunk(B_DKV + m + 1), KD * P)
                else:
                    hi(Chunk(B_DQ), KD * P)
                ch = Chunk(B_DKV + m)
                a_l, _, a_c, _ = glu_psum(ch.slot)
                dst = ckv_raw[:, m, :] if m < 2 else kr[:]
                act.wait_ge(S["w_used"], ch.done)
                act.activation(dst[:, 0:NLAT], a_l, ACT.Copy)
                act.activation(dst[:, NLAT:T], a_c, ACT.Copy).then_inc(S["drained"], 1)
                act.wait_ge(S["drained"], ch.drains)
                square(m, dst, T)
            for m in range(6):
                if m < 5:
                    hi(Chunk(B_DQ + m + 1), KD * P)
                else:
                    hi(Chunk(B_UKV), 8 * P)
                ch = Chunk(B_DQ + m)
                act.wait_ge(S["w_used"], ch.done)
                act.activation(cq_raw[:, m, :], glu_psum(ch.slot)[0], ACT.Copy).then_inc(S["drained"], 1)
                act.wait_ge(S["drained"], ch.drains)
                square(3 + m, cq_raw[:, m, :], NLAT)
                if m == 0:
                    root(0, T, KVR)
                if m == 1:
                    root(1, T, ROPE)
                if m in (2, 3):
                    b = m - 2
                    act.wait_ge(S["job_out"], b + 1)
                    act.activation(ckv_hi[:, b, :], ckv_raw[:, b, :], ACT.Copy).then_inc(S["ckv_hi_s"], 1)
            root(2, NLAT, QR)
            use = used_after(B_UKV - 1)
            for m in range(4):
                if m < 3:
                    hi(Chunk(B_UKV + m + 1), 8 * P)
                for t in range(KV_USES[m]):
                    use += 1
                    a_l, _, a_c, _ = glu_psum((use - 1) % 2)
                    act.wait_ge(S["w_used"], use)
                    if m < 2:
                        h = 4 * m + t
                        act.activation(kn[:, h, 0:NLAT], a_l, ACT.Copy)
                        act.activation(kn[:, h, NLAT:T], a_c, ACT.Copy).then_inc(S["drained"], 1)
                        act.wait_ge(S["drained"], use - B_GLU)
                        square(9 + h, kn[:, h, :], T)
                        if h >= 1:
                            root(3 + h - 1, T, NOPE)
                        if h < 6:
                            act.wait_ge(S["job_out"], JOB_UNITS[1] + h + 1)
                            act.activation(cq_hi[:, h, :], cq_raw[:, h, :], ACT.Copy).then_inc(S["cq_hi_s"], 1)
                    else:
                        act.activation(val[:, t, 512 * (m - 2):512 * (m - 1)], a_l, ACT.Copy).then_inc(S["drained"], 1)
                    if m == 2 and t == 0:
                        root(10, T, NOPE)
            hi(Chunk(B_UQ), 6 * P)
            for m in range(12):
                if m < 11:
                    hi(Chunk(B_UQ + m + 1), 6 * P)
                else:
                    hi(Chunk(B_WO), KD * P)
                ch = Chunk(B_UQ + m)
                act.wait_ge(S["w_used"], ch.done)
                act.activation(q_all[:, m, :], glu_psum(ch.slot)[0], ACT.Copy).then_inc(S["drained"], 1)
                act.wait_ge(S["drained"], ch.drains)
                square(17 + m, q_all[:, m, :], NLAT)
                if m >= 1:
                    root(11 + m - 1, NLAT, NOPE if m - 1 < HEADS else ROPE)
            root(22, NLAT, ROPE)

            def exps(i):
                act.wait_ge(S["mx_set"], i + 1)
                if i >= 2:
                    act.wait_ge(S["p_T"], i - 1)
                act.activation(pr[:, i % 2, :], flat[:, 1024 * (i % 2):1024 * (i % 2) + T], ACT.Exp,
                               bias=smax[:, i % 2, 1:2], scale=SCALE, accum_out=smax[:, i % 2, 2:3]).then_inc(S["ex_done"], 1)

            exps(0)
            for i in range(4 * HEADS):
                if i + 1 < 4 * HEADS:
                    exps(i + 1)
                h, t = i // 4, i % 4
                act.wait_ge(S["p_T"], i + 1)
                if h >= 2 and t == 0:
                    act.wait_ge(S["pv_done"], h - 1)
                act.activation(pT[:, h % 2, :, P * t:P * (t + 1)], flat[:, 2048:2048 + T].rearrange("p (b q) -> p b q", b=6),
                               ACT.Copy).then_inc(S["pT_out"], 1)
            for h in range(HEADS):
                act.wait_ge(S["ot_out"], HEADS)
                act.activation(hhi[:, h, 0:NLAT], ot[:, h, :], ACT.Copy).then_inc(S["o_hi"], 1)
            for m in range(KD - 1):
                hi(Chunk(B_WO + m + 1), KD * P)
            norm(2, 1, 1, NLAT, (S["drained"], used_after(B_FFN[1] - 1) - B_GLU))
            ffn(1, NLAT)

            for t in range(4):
                act.wait_ge(S["fin_out"], 2 * t + 2)
                act.dma_start(a["out"].rearrange("o (t p) d -> t p (o d)", p=P)[t], hhi_out(t)).then_inc(S["out_done"], 16)

        @block.vector
        def _(dve):
            chain = Chain(dve, S["dve_link"])
            dve.memset(ones[:], 1.0).then_inc(S["const_set"], 1)
            dve.memset(eps[:], EPS).then_inc(S["const_set"], 1)
            dve.memset(zero[:], 0.0).then_inc(S["const_set"], 1)
            dve.wait_ge(S["params_in"], 16 * 21)
            dve.tensor_tensor(fold[:], ident[0:4, 0:2], ident[0:4, 2:4], ALU.add).then_inc(S["cond_ready"], 1)
            dve.wait_ge(S["act_link"], 1)
            dve.tensor_tensor(cs[:], colsB[:, 0:16], sgc[:], ALU.mult).then_inc(S["const_set"], 1)
            dve.wait_ge(S["const_set"], 4)
            dve.wait_ge(S["cond_ready"], 2)
            dve.tensor_tensor(cond_r[:, :, 2:4].rearrange("p k w -> p w k"), cs[:].rearrange("p (w k) -> p w k", w=2),
                              cond_r[:, :, 0:2].bitcast(F32).rearrange("p k w -> p w k"), ALU.subtract)\
                .then_inc(S["cond_ready"], 1)

            lr, li = lam[:, 0, :], lam[:, 1, :]
            d_ = [disc[:, n, :] for n in range(12)]
            dve.wait_ge(S["dt_set"], 1)
            dtb = ldt[:].unsqueeze(2).to_broadcast([DG, 2, STATES])

            def hs(ap):
                return ap.rearrange("p (h s) -> p h s", h=2)

            dve.tensor_tensor(hs(d_[0]), hs(lr), dtb, ALU.mult).then_inc(S["disc_a"], 1)
            chain.link(dve.tensor_tensor(hs(d_[5]), hs(li), dtb, ALU.mult))
            chain.link(dve.tensor_scalar(d_[6], d_[5], 1.0 / (TWO_PI_HI + TWO_PI_LO), ROUND, ALU.mult, ALU.add))
            chain.link(dve.tensor_scalar(d_[6], d_[6], ROUND, None, ALU.subtract))
            chain.link(dve.scalar_tensor_tensor(d_[5], d_[6], -TWO_PI_HI, d_[5], ALU.mult, ALU.add))
            chain.link(dve.scalar_tensor_tensor(d_[5], d_[6], -TWO_PI_LO, d_[5], ALU.mult, ALU.add))
            dve.tensor_scalar(d_[1], d_[5], PI, -PI, ALU.min, ALU.max).then_inc(S["disc_b"], 1)
            chain.link(dve.tensor_tensor(d_[7], lr, lr, ALU.mult))
            chain.link(dve.tensor_tensor(d_[8], li, li, ALU.mult))
            chain.link(dve.tensor_tensor(d_[7], d_[7], d_[8], ALU.add))
            chain.link(dve.reciprocal(d_[7], d_[7]))

            def ada_turn(turn):
                for r in range(POOL_R):
                    ada_lo(dve, S["ada_lo_dve"], 0, r, turn)

            ada_turn(0)
            dve.wait_ge(S["sin_done"], 1)
            dve.wait_ge(S["exp_done"], 1)
            chain.link(dve.tensor_tensor(d_[4], d_[4], d_[4], ALU.mult))
            chain.link(dve.tensor_scalar(d_[4], d_[4], -2.0, 1.0, ALU.mult, ALU.add))
            chain.link(dve.tensor_tensor(d_[8], d_[2], d_[4], ALU.mult))
            chain.link(dve.tensor_tensor(d_[9], d_[2], d_[3], ALU.mult))
            chain.link(dve.tensor_scalar(d_[5], d_[8], 1.0, None, ALU.subtract))
            chain.link(dve.tensor_tensor(d_[0], d_[5], lr, ALU.mult))
            chain.link(dve.tensor_tensor(d_[1], d_[9], li, ALU.mult))
            chain.link(dve.tensor_tensor(d_[0], d_[0], d_[1], ALU.add))
            chain.link(dve.tensor_tensor(d_[10], d_[0], d_[7], ALU.mult))
            chain.link(dve.tensor_tensor(d_[0], d_[9], lr, ALU.mult))
            chain.link(dve.tensor_tensor(d_[1], d_[5], li, ALU.mult))
            chain.link(dve.tensor_tensor(d_[0], d_[0], d_[1], ALU.subtract))
            dve.tensor_tensor(d_[11], d_[0], d_[7], ALU.mult).then_inc(S["disc_b"], 1)

            ada_turn(1)
            ada_turn(2)
            def cmul(o, x, y, n):
                t = [cm[:, q, :, 0:n] for q in range(2)]
                dve.tensor_tensor(t[0], x[0], y[0], ALU.mult)
                chain.link(dve.tensor_tensor(t[1], x[1], y[1], ALU.mult))
                chain.link(dve.tensor_tensor(o[0], t[0], t[1], ALU.subtract))
                dve.tensor_tensor(t[0], x[0], y[1], ALU.mult)
                chain.link(dve.tensor_tensor(t[1], x[1], y[0], ALU.mult))
                chain.link(dve.tensor_tensor(o[1], t[0], t[1], ALU.add))

            def pows(e0, e1):
                return [pw[:, q, :, e0:e1] for q in range(2)]

            def one(e, n):
                return [pw[:, q, :, e:e + 1].to_broadcast([P, DG, n]) for q in range(2)]

            dve.wait_ge(S["disc_out"], 1)
            dve.memset(pw[:, 0, :, 0], 1.0)
            chain.link(dve.memset(pw[:, 1, :, 0], 0.0))
            for q in range(2):
                chain.link(dve.tensor_copy(pw[:, q, :, 1], acoef[:, q, :]))
            cmul(pows(2, 3), pows(1, 2), pows(1, 2), 1)
            cmul(pows(3, 5), pows(1, 3), one(2, 2), 2)
            cmul(pows(5, 9), pows(1, 5), one(4, 4), 4)

            def by(t, q, dirn):
                return t[:, q].rearrange("p (g d) k -> p g d k", d=2)[:, :, dirn]

            f = [acoef[:, 2 + q, :].unsqueeze(2).to_broadcast([P, DG, CK]) for q in range(2)]
            cmul([Pn[:, q] for q in range(2)], pows(0, 8), f, 8)
            for q in range(2):
                dve.tensor_copy(by(Qk, q, 0), by(Pn, q, 0)[:, :, ::-1])
                chain.link(dve.tensor_copy(by(Qk, q, 1), by(Pn, q, 1)))
                dve.tensor_copy(by(Pk, q, 0), by(pw, q, 0)[:, :, 0:8])
                chain.link(dve.tensor_copy(by(Pk, q, 1), by(pw, q, 1)[:, :, 7::-1]))
                dve.tensor_copy(by(Pn, q, 0), by(pw, q, 0)[:, :, 1:9])
                chain.link(dve.tensor_copy(by(Pn, q, 1), by(pw, q, 1)[:, :, 8:0:-1]))
            for dirn in range(2):
                p8 = [by(pw, q, dirn)[:, :, 8] for q in range(2)]
                dve.tensor_copy(a8[:, dirn, 0, 0], p8[0])
                dve.tensor_copy(a8[:, dirn, 0, 1], p8[0])
                dve.tensor_copy(a8[:, dirn, 1, 0], p8[1])
                chain.link(dve.tensor_scalar(a8[:, dirn, 1, 1], p8[1], -1.0, None, ALU.mult))
            dve.wait_ge(S["cols_out"], 4)
            dve.tensor_tensor(kd[:], ident[0:CH, 0:CH].unsqueeze(1).to_broadcast([CH, GROUPS, CH]),
                              d16[:].unsqueeze(2).to_broadcast([CH, GROUPS, CH]), ALU.mult).then_inc(S["tab_set"], 1)
            ada_turn(3)
            ada_turn(4)
            dve.wait_ge(S["rowsum_done"], 1)
            chain.link(dve.reciprocal(stat[:, 1, :], stat[:, 0, :]))
            for k in range(CK):
                last = dve.tensor_scalar(xn[:, :, k, :], xin[:, k, :].rearrange("j (g c) -> j g c", c=CH), stat[:, 1, k:k + 1], None, ALU.mult)
            last.then_inc(S["rstd_set"], 1)

            def lo(ch, n):
                dve.wait_ge(S["hi_ready"], ch.n + 1)
                dve.tensor_tensor(wlo[:, ch.slot, 0:n], wraw[:, ch.slot, 0:n], whi[:, ch.slot, 0:n].bitcast(F32),
                                  ALU.subtract).then_inc(S["lo_ready"], 1)

            ada_turn(5)
            def ada_columns(l):
                dve.wait_ge(S["ada_folded"], (l + 1) * ADA_CHUNKS)
                bias = colsA[:, C_ADAB + 48 * l:C_ADAB + 48 * (l + 1)].unsqueeze(2).to_broadcast([P, 48, 2])
                chain.link(dve.tensor_tensor(modc[:, l], ps[:, 7, 0:96].rearrange("p (b w) -> p b w", w=2), bias, ALU.add))
                for q, (at, scale) in enumerate(((C_NMIX, SC_M), (C_NFFN, SC_F))):
                    g = colsA[:, at + KD * l:at + KD * (l + 1)].unsqueeze(2).to_broadcast([P, KD, 2])
                    last = dve.scalar_tensor_tensor(gain[:, l, q], modc[:, l, scale:scale + KD, :], 1.0, g, ALU.add, ALU.mult)
                last.then_inc(S["ada0_set"], 1)

            ada_columns(0)

            def m_block(b, q, n):
                dg = bass.ds(4 * b, 4)
                if n is not None:
                    dve.wait_ge(S["k_done"], n)
                q_re, q_im = (Qk[:, r, dg, :].unsqueeze(3).to_broadcast([P, 4, CK, CH]) for r in range(2))
                b_re, b_im = (Bc[:, r, dg, :].unsqueeze(2).to_broadcast([P, 4, CK, CH]) for r in range(2))
                dst = [Mr[:, q, r].rearrange("p g (k c) -> p g k c", k=CK) for r in range(2)]
                dve.tensor_tensor(tD[:, 0], q_re, b_re, ALU.mult)
                chain.link(dve.tensor_tensor(tD[:, 1], q_im, b_im, ALU.mult))
                chain.link(dve.tensor_tensor(dst[0], tD[:, 0], tD[:, 1], ALU.subtract))
                dve.tensor_tensor(tD[:, 0], q_re, b_im, ALU.mult)
                chain.link(dve.tensor_tensor(tD[:, 1], q_im, b_re, ALU.mult))
                dve.tensor_tensor(dst[1], tD[:, 0], tD[:, 1], ALU.add).then_inc(S["m_ready"], 1)

            m_block(0, 0, None)
            dve.wait_ge(S["m_ready"], 1)

            dve.wait_ge(S["rep_done"], 1)
            for v in range(2):
                for c in range(2):
                    last = dve.tensor_copy(urep[:, v, c].rearrange("p (b g) -> p g b", b=KD),
                                           ps[:, 6, 0:256].rearrange("p (g v b c) -> p g v b c", v=2, b=KD, c=2)[:, :, v, :, c])
            last.then_inc(S["rep_out"], 1)
            dve.wait_ge(S["rep_out"], 1)
            for q in range(GROUPS // 4):
                if q % 2 == 0:
                    dve.wait_ge(S["u_T"], q + 1)
                    for g, j0, j1, cond in u_parts(q):
                        last = dve.tensor_scalar(U[:, g, j0:j1], ps[:, q % 4, P * (g % 4) + j0:P * (g % 4) + j1],
                                                 urep[:, 0, cond, g:g + 1], urep[:, 1, cond, g:g + 1], ALU.mult, ALU.add)
                    last.then_inc(S["u_dve"], 1)

            def evac_block(b, n):
                dve.wait_ge(S["kf_out"], n + 1)
                back = ps[0:CH, 2:4, 256:512].rearrange("c h (g x) -> c g h x", g=2)
                ke = Kext[:].rearrange("c (g h) t o -> c g h (t o)", h=2)
                dve.tensor_copy(ke[:, :, :, 0:7 * CH], back[:, :, :, 0:7 * CH])
                mid = ke[:, :, :, 7 * CH:8 * CH]
                chain.link(dve.tensor_tensor(mid, mid, back[:, :, :, 7 * CH:], ALU.add))
                midg = Kext[:, :, 7, :]
                dve.tensor_tensor(midg, midg, kd[:, bass.ds(4 * b, 4), :], ALU.add).then_inc(S["kext_ready"], 1)
                dve.wait_ge(S["s_done"], n + 1)
                for h in range(2):
                    rows = slice(STATES * h, STATES * (h + 1))
                    last = dve.tensor_copy(Sarr[rows, 1, 1:J + 1, :, bass.ds(2 * b, 2)].rearrange("p j r g -> p r g j"),
                                           ps[rows, 6:8, :].rearrange("p r (g x) -> p r g x", g=2)[:, :, :, J * h:J * (h + 1)][:, :, :, ::-1])
                last.then_inc(S["sb_out"], 1)

            dve.wait_ge(S["u_T"], GROUPS // 4)
            dve.memset(Sarr[:, 0, 0], 0.0).then_inc(S["s_zero"], 1)
            m_block(1, 1, None)
            evac_block(0, 0)
            dve.wait_ge(S["m_ready"], 2)
            with dve.Fori(1, GP // 4) as i:
                chain.enter(i - 1, 8)
                for q in range(2):
                    m_block(2 * i + q, q, 2 * i + q - 1)
                    dve.wait_ge(S["m_ready"], 2 * i + q + 1)
                    evac_block(2 * i + q - 1, 2 * i + q - 1)
            chain.leave(GP // 4 - 1)
            evac_block(GP // 2 - 1, GP // 2 - 1)

            slots = Sarr[:].rearrange("p d s r g -> p (d s) (r g)")

            def steps(at, hop, count, unroll):
                def step(slot):
                    h, x = (slots[:, bass.ds(slot - back, 2, step=hop)] for back in (1, 0))
                    chain.link(dve.tensor_tensor(sc[:, :, 0:2].rearrange("p d f r g -> p d f (r g)"),
                                                 a8[:].rearrange("p d f r g -> p d f (r g)"),
                                                 h.unsqueeze(2).to_broadcast([P, 2, 2, 2 * GP]), ALU.mult))
                    chain.link(dve.tensor_tensor(sc[:, :, 2].rearrange("p d r g -> p d (r g)"),
                                                 sc[:, :, 0].rearrange("p d r g -> p d (r g)"), x, ALU.add))
                    chain.link(dve.tensor_tensor(x.rearrange("p d (r g) -> p d r g", r=2), sc[:, :, 2], sc[:, :, 1, ::-1],
                                                 ALU.add))

                with dve.Fori(0, count // unroll) as i:
                    chain.enter(i, 3 * unroll)
                    for u in range(unroll):
                        step(unroll * i + (at + u))
                chain.leave(count // unroll)
                for u in range(count // unroll * unroll, count):
                    step(at + u)

            dve.wait_ge(S["sf_out"], GP // 2)
            dve.wait_ge(S["sb_out"], GP // 2)
            steps(2, CTX_HOP, JCTX - 1, 6)
            chain.link(dve.tensor_copy(Sarr[:, 1, 0], Sarr[:, 1, J]))
            steps(JCTX + 1, LAT_HOP, J // 2, 8)
            dve.memset(Sarr[:, 1, JLAT], 0.0).then_inc(S["half_scanned"], 1)
            steps(JCTX + 1 + J // 2, LAT_HOP, JLAT - 1 - J // 2, 8)
            dve.wait_ge(S["half_scanned"], 1)
            dve.wait_ge(S["half_saved"], 1)
            dve.tensor_copy(Sarr[:, 1, J // 2 - 1::-1], Sarr[:, 1, J // 2:J]).then_inc(S["scanned"], 1)
            ada_columns(1)
            dve.wait_ge(S["k_done"], GP // 2)

            def z_evac(b):
                for h in range(2):
                    dve.wait_ge(S["z_T"], 2 * b + h + 1)
                    src = ps[:, 4 + 2 * (b % 2) + h, :].rearrange("p (k j) -> p k j", k=4)
                    dst = U[:].rearrange("p g j -> p (g j)")[:, T * b:T * b + T]
                    dve.tensor_copy(dst[:, 0:NLAT].rearrange("p (j k) -> p k j", k=CK)[:, 4 * h:4 * h + 4], src[:, :, JCTX:J])
                    dve.tensor_copy(dst[:, NLAT:T].rearrange("p (j k) -> p k j", k=CK)[:, 4 * h:4 * h + 4], src[:, :, 0:JCTX])\
                        .then_inc(S["z_out"], 1)

            for hb in range(GP // 2):
                dg = slice(4 * hb, 4 * hb + 4)
                p_re, p_im = (Pn[:, r, dg, :].unsqueeze(3).to_broadcast([P, 4, CK, CH]) for r in range(2))
                c_re, c_ni = (Cc[:, r, dg, :].unsqueeze(2).to_broadcast([P, 4, CK, CH]) for r in range(2))
                if hb >= 2:
                    dve.wait_ge(S["y_done"], hb - 1)
                dve.tensor_tensor(tD[:, 0], p_re, c_re, ALU.mult)
                chain.link(dve.tensor_tensor(tD[:, 1], p_im, c_ni, ALU.mult))
                dve.tensor_tensor(Nr[:, hb % 2, 0].rearrange("p g (k c) -> p g k c", k=CK),
                                  tD[:, 0], tD[:, 1], ALU.add).then_inc(S["n2_re"], 1)
                dve.wait_ge(S["n2_re"], hb + 1)
                if hb % 2 and hb >= 5:
                    z_evac((hb - 5) // 2)
            z_evac(KD - 2)
            z_evac(KD - 1)
            for b in range(KD):
                for h in range(2):
                    dve.wait_ge(S["xT_T"], 2 * b + h + 1)
                    src = ps[:, 4 + 2 * (b % 2) + h, :].rearrange("p (k j) -> p k j", k=4)
                    dst = xT[:, b, :]
                    dve.tensor_copy(dst[:, 0:NLAT].rearrange("p (j k) -> p k j", k=CK)[:, 4 * h:4 * h + 4], src[:, :, JCTX:J])
                    dve.tensor_copy(dst[:, NLAT:T].rearrange("p (j k) -> p k j", k=CK)[:, 4 * h:4 * h + 4], src[:, :, 0:JCTX])\
                        .then_inc(S["xT_out"], 1)
            dve.wait_ge(S["xT_out"], 2 * KD)

            def stage(first, count, n, epi):
                stage_turns(dve, count, lambda c, turn: lo(Chunk(first + c, turn), n),
                            lambda m, c, turn: epi(m, Chunk(first + c, turn), turn is None and c < 2))

            def glu_epi(m, ch, early):
                a_l, _, a_c, _ = glu_psum(ch.slot)
                dve.wait_ge(S["sig_done"], ch.n - B_GLU + 1)
                bias = colsB[:, bass.ds(C_GLUB + m, 1)]
                for v, pa, cond in ((slice(0, NLAT), a_l, 0), (slice(NLAT, T), a_c, 1)):
                    s_ = sig[:, ch.slot, v]
                    last = dve.scalar_tensor_tensor(s_, pa, bias, s_, ALU.add, ALU.mult)
                last.then_inc(S["drained"], 1)
                dve.wait_ge(S["drained"], ch.n - B_GLU + 1)
                for v, cond in ((slice(0, NLAT), 0), (slice(NLAT, T), 1)):
                    xv = xT[:, bass.ds(m, 1), v].rearrange("p a t -> p (a t)")
                    g = modc[:, 0, bass.ds(G_M + m, 1), cond]
                    last = dve.scalar_tensor_tensor(xv, sig[:, ch.slot, v], g, xv, ALU.mult, ALU.add)
                last.then_inc(S["mix_done"], 1)

            stage(B_GLU, KD, SLOT, glu_epi)

            def norm(j, toks):
                dve.wait_ge(S["sq_done"], KD * j + 2)
                chain.link(dve.tensor_tensor(ssum[:, 0:toks], sq[:, 0, 0:toks], sq[:, 1, 0:toks], ALU.add))
                for b in range(2, KD):
                    dve.wait_ge(S["sq_done"], KD * j + b + 1)
                    op = dve.tensor_tensor(ssum[:, 0:toks], ssum[:, 0:toks], sq[:, b, 0:toks], ALU.add)
                    if b < KD - 1:
                        chain.link(op)
                op.then_inc(S["ssum_done"], 1)
                dve.wait_ge(S["std_done"], j + 1)
                chain.link(dve.reciprocal(rstd[:, 0:toks], rstd[:, 0:toks]))
                for b in range(KD):
                    if b >= 2:
                        dve.wait_ge(S["h_lo"], KD * j + b - 1)
                    dve.tensor_tensor(hx[:, b % 2, 0:toks], xT[:, b, 0:toks], rstd[:, 0:toks], ALU.mult)\
                        .then_inc(S["xn_done"], 1)

            def out_epi(l, at, toks):
                def epi(m, ch, early):
                    a_l, _, a_c, _ = glu_psum(ch.slot)
                    dve.wait_ge(S["w_used"], ch.done)
                    for (t0, t1), src, cond in (((0, NLAT), a_l, 0), ((NLAT, T), a_c, 1))[:1 if toks == NLAT else 2]:
                        xv = xT[:, bass.ds(m, 1), t0:t1].rearrange("p a t -> p (a t)")
                        last = dve.scalar_tensor_tensor(xv, src, modc[:, l, bass.ds(at + m, 1), cond], xv, ALU.mult, ALU.add)
                    last.then_inc(S["drained"], 1)
                return epi

            def ffn(l, toks):
                spans = ((0, NLAT), (NLAT, T))[:1 if toks == NLAT else 2]
                for g in range(2):
                    def epi(m, ch, early):
                        f = KF * l + GF * g + m
                        a_l, b_l, a_c, b_c = glu_psum(ch.slot)
                        dve.wait_ge(S["acc_set"], f + 1)
                        v = acc[:, ch.slot]
                        w = colsW[:, l]
                        for (t0, t1), src in zip(spans, (a_l, a_c)):
                            n = t1 - t0
                            op = dve.scalar_tensor_tensor(v[:, t0 + 1:t1], src[:, 0:n - 1], w[:, bass.ds(GF * g + m, 1)],
                                                          v[:, t0 + 1:t1], ALU.mult, ALU.add)
                        chain.link(op)
                        for (t0, t1), src in zip(spans, (a_l, a_c)):
                            n = t1 - t0
                            op = dve.scalar_tensor_tensor(v[:, t0:t1 - 1], src[:, 1:n], w[:, bass.ds(2 * KF + GF * g + m, 1)],
                                                          v[:, t0:t1 - 1], ALU.mult, ALU.add)
                        op.then_inc(S["conv_done"], 1)
                        dve.wait_ge(S["silu_done"], f + 1)
                        for (t0, t1), src in zip(spans, (b_l, b_c)):
                            op = dve.tensor_tensor(v[:, t0:t1], v[:, t0:t1], src, ALU.mult)
                        op.then_inc(S["drained"], 1)
                    first = B_FFN[l] + g * (GF + KD)
                    pairs = (GF - 3) // 2
                    def turned(m, c, turn):
                        if turn is not None and c == 0:
                            chain.enter(turn - 1, 2)
                        epi(m, Chunk(first + c, turn), turn is None and c < 2)
                        if turn is not None and c == 1:
                            chain.leave(pairs)
                    stage_turns(dve, GF, lambda c, turn: lo(Chunk(first + c, turn), SLOT), turned)
                    stage(first + GF, KD, GF * P, out_epi(l, G_F, toks))

            norm(0, T)
            ffn(0, T)
            norm(1, T)

            def job(j, n, views, gains):
                dve.wait_ge(S["job_std"], j + 1)
                chain.link(dve.reciprocal(rs[:, 0:n], rs[:, 0:n]))
                for v, g in zip(views, gains):
                    op = dve.scalar_tensor_tensor(v, v, colsB[:, g:g + 1], rs[:, 0:n], ALU.mult, ALU.mult)
                    op.then_inc(S["job_out"], 1)

            def rotate(v, swapped, n, done):
                dve.wait_ge(swapped, n)
                dve.tensor_tensor(v, v, rope_cs[:, 0], ALU.mult)
                chain.link(dve.tensor_tensor(rs[:, 0:NLAT], ps[:, 7, :], rope_cs[:, 1], ALU.mult))
                dve.tensor_tensor(v, v, rs[:, 0:NLAT], ALU.add).then_inc(done, 1)

            lo(Chunk(B_DKV), KD * P)
            lo(Chunk(B_DKV + 1), KD * P)
            lo(Chunk(B_DKV + 2), KD * P)
            for m in range(6):
                lo(Chunk(B_DQ + m), KD * P)
                if m == 1:
                    job(0, T, [ckv_raw[:, b, :] for b in range(2)], (C_GKV, C_GKV + 1))
                if m == 2:
                    job(1, T, [kr[:]], (C_GKR,))
            lo(Chunk(B_UKV), 8 * P)
            job(2, NLAT, [cq_raw[:, b, :] for b in range(6)], range(C_GQ, C_GQ + 6))
            lo(Chunk(B_UKV + 1), 8 * P)
            for h in range(HEADS):
                if h in (4, ):
                    lo(Chunk(B_UKV + 2), 8 * P)
                job(3 + h, T, [kn[:, h, :]], (C_GKN,))
            lo(Chunk(B_UKV + 3), 8 * P)
            lo(Chunk(B_UQ), 6 * P)
            for m in range(12):
                if m < 11:
                    lo(Chunk(B_UQ + m + 1), 6 * P)
                else:
                    lo(Chunk(B_WO), KD * P)
                if m >= 1:
                    job(11 + m - 1, NLAT, [q_all[:, m - 1, :]], (C_GQN if m - 1 < HEADS else C_GQR,))
            job(22, NLAT, [q_all[:, 11, :]], (C_GQR,))
            dve.wait_ge(S["rope_in"], 16)
            for n, v in enumerate([kr[:, 0:NLAT]] + [q_all[:, HEADS + m, :] for m in range(4)]):
                rotate(v, S["swap_T"], n + 1, S["rot_done"])
                dve.wait_ge(S["rot_done"], n + 1)

            def maxes(i):
                dve.wait_ge(S["sc_done"], i + 1)
                if i >= 2:
                    dve.wait_ge(S["pr_set"], i - 1)
                chain.link(dve.reduce_max(smax[:, i % 2, 0:1], flat[:, 1024 * (i % 2):1024 * (i % 2) + T], AX.X))
                dve.tensor_scalar(smax[:, i % 2, 1:2], smax[:, i % 2, 0:1], -SCALE, None, ALU.mult).then_inc(S["mx_set"], 1)

            maxes(0)
            for i in range(4 * HEADS):
                dve.wait_ge(S["ex_done"], i + 1)
                chain.link(dve.reciprocal(smax[:, i % 2, 3:4], smax[:, i % 2, 2:3]))
                dve.tensor_scalar(pr[:, i % 2, :], pr[:, i % 2, :], smax[:, i % 2, 3:4], None, ALU.mult)\
                    .then_inc(S["pr_set"], 1)
                if i + 1 < 4 * HEADS:
                    maxes(i + 1)
                if i % 4 == 1 and i > 4:
                    h = i // 4 - 1
                    dve.wait_ge(S["pv_done"], h + 1)
                    dve.tensor_copy(ot[:, h, :], ps[:, 6 + h % 2, :]).then_inc(S["ot_out"], 1)
            dve.wait_ge(S["pv_done"], HEADS)
            dve.tensor_copy(ot[:, HEADS - 1, :], ps[:, 7, :]).then_inc(S["ot_out"], 1)
            for m in range(KD):
                if m < KD - 1:
                    lo(Chunk(B_WO + m + 1), KD * P)
                out_epi(1, G_M, NLAT)(m, Chunk(B_WO + m), False)
            norm(2, NLAT)
            ffn(1, NLAT)

            for t in range(4):
                for h in range(2):
                    dve.wait_ge(S["fin_T"], 2 * t + h + 1)
                    dve.tensor_copy(hhi_out(t)[:, 512 * h:512 * h + 512], ps[:, (2 * t + h) % 4, :]).then_inc(S["fin_out"], 1)

        @block.tensor
        def _(pe):
            pe.wait_ge(S["params_in"], 16 * 21)
            pe.transpose(flat[0:CH, 400:464], drow[:], ident[0:GROUPS, 0:GROUPS])
            pe.transpose(flat[:, 128:216], rowsB[:], ident[0:88, 0:88])
            pe.transpose(flat[:, 0:128], rowsA[:], ident[:])
            for l in range(2):
                last = pe.transpose(flat[:, 256 + 66 * l:322 + 66 * l], rowsW[:, l, :], ident[0:66, 0:66])
            last.then_inc(S["cols_T"], 1)
            pe.wait_ge(S["cond_ready"], 3)

            def ada_fold(l, n, col):
                pe.wait_ge(S["row_out"], n + 1)
                for b in range(2):
                    last = pe.matmul(ps[:, 7, bass.ds(col + 2 * b, 2)], ada_rows[:, b * P:(b + 1) * P], fold[:],
                                     start=True, stop=True)
                last.then_inc(S["ada_folded"], 1)

            def ada_chunk(l, r, turn):
                m = ADA_RING * turn + r
                n = l * ADA_CHUNKS + m
                if not (isinstance(n, int) and n < 2):
                    pe.wait_ge(S["row_out"], n - 1)
                for q in range(2):
                    ada_split(pe, l, r, turn, q)
                    for k in range(KD // 2):
                        for w in (ada_whi, ada_wlo):
                            last = pe.matmul(ps[0:4, 6 * (r % 2), 0:256], cond_r[:, KD // 2 * q + k, :],
                                             w[:, (2 * r + q) % 4, 256 * k:256 * (k + 1)],
                                             start=q == 0 and k == 0 and w is ada_whi,
                                             stop=q == 1 and k == KD // 2 - 1 and w is ada_wlo)
                    last.then_inc(S["ada_used"], 1)
                if not (isinstance(m, int) and m == 0):
                    ada_fold(l, n - 1, 4 * (m - 1))

            def ada_turn(turn):
                for r in range(ADA_RING):
                    ada_chunk(0, r, turn)

            ada_turn(0)
            ada_turn(1)
            pe.wait_ge(S["disc_b"], 2)
            for q in range(4):
                last = pe.transpose(flat[:, 512 + DG * q:512 + DG * (q + 1)], disc[:, 8 + q, :], ident[0:DG, 0:DG])
            last.then_inc(S["disc_T"], 1)
            for n, (src, q, eq) in enumerate(((brow, 0, "p (h s c) -> p c h s"), (brow, 1, "p (h s c) -> p c h s"),
                                              (crow, 0, "p (c h s) -> p c h s"), (crow, 1, "p (c h s) -> p c h s"))):
                v = src[:, q, :].rearrange(eq, h=2, c=CH)
                perm = ident[0:DG, 0:DG].rearrange("p (d g) -> p g d", d=2)
                if n == 0:
                    pe.wait_ge(S["s5rows_in"], 16 * 6)
                if n == 2:
                    ada_turn(2)
                for h in range(4):
                    if n >= 1:
                        pe.wait_ge(S["bc_out"], 4 * (n - 1) + h + 1)
                    for c in range(4):
                        last = pe.matmul(ps[:, 2 + h, DG * c:DG * (c + 1)], v[:, 4 * h + c].rearrange("p h s -> p (h s)"), perm, start=True, stop=True)
                    last.then_inc(S["bc_T"], 1)

            for turn in range(3, ADA_TURNS):
                ada_turn(turn)
            ada_fold(0, ADA_CHUNKS - 1, 4 * (ADA_CHUNKS - 1))

            pe.wait_ge(S["ada0_set"], 1)
            pe.wait_ge(S["tabs_in"], 1)
            for g in range(KD):
                for v, rhs in enumerate((gain[:, 0, 0], modc[:, 0, SH_M:SH_M + KD, :])):
                    at = 32 * g + 16 * v
                    last = pe.matmul(ps[:, 6, at:at + 16], pick[:, g].rearrange("p k c -> p (k c)"),
                                     rhs.rearrange("p b c -> p (b c)"), start=True, stop=True)
            last.then_inc(S["rep_done"], 1)
            pe.wait_ge(S["rstd_set"], 1)
            for q in range(GROUPS // 4):
                if q >= 4:
                    pe.wait_ge(S["u_act" if q % 2 else "u_dve"], q // 2 - 1)
                for r in range(4):
                    g = 4 * q + r
                    last = pe.transpose(ps[:, q % 4, P * r:P * r + J], xn[:, g].rearrange("j k c -> j (k c)"), ident[0:J, 0:J])
                last.then_inc(S["u_T"], 1)

            def s5_block(b, q, n, first):
                pe.wait_ge(S["m_ready"], n + 1)
                pe.wait_ge(S["n_ready"], n + 1)
                if not first:
                    pe.wait_ge(S["kext_ready"], n)
                if first:
                    pe.wait_ge(S["u_dve"], GROUPS // 8)
                    pe.wait_ge(S["u_act"], GROUPS // 8)
                else:
                    pe.wait_ge(S["mt_out"], n)
                for r in range(2):
                    for g in range(4):
                        last = pe.transpose(ps[:, r, P * g:P * (g + 1)], Mr[:, q, r, g, :], ident[:])
                last.then_inc(S["mt_T"], 1)
                for g in range(2):
                    for dirn in range(2):
                        k0 = CK - 1 if dirn == 0 else 0
                        for h in range(2):
                            rows = slice(STATES * h, STATES * (h + 1))
                            dst = ps[0:CH, 2 + h, 256 * dirn + P * g:256 * dirn + P * (g + 1)]
                            for r in range(2):
                                last = pe.matmul(dst, Mr[rows, q, r, 2 * g + dirn, CH * k0:CH * (k0 + 1)],
                                                 Nr[rows, q, r, 2 * g + dirn, :], start=r == 0, stop=r == 1)
                last.then_inc(S["k_done"], 1)
                pe.wait_ge(S["mt_out"], n + 1)
                if not first:
                    pe.wait_ge(S["sf_out"], n)
                    pe.wait_ge(S["sb_out"], n)
                for dirn in range(2):
                    for r in range(2):
                        for g in range(2):
                            last = pe.matmul(ps[:, 4 + 2 * dirn + r, 256 * g:256 * g + 2 * J], MT[:, r, 2 * g + dirn, :],
                                             U[:, bass.ds(4 * b + 2 * g, 2), :].rearrange("p a j -> p (a j)"),
                                             start=True, stop=True)
                last.then_inc(S["s_done"], 1)

            s5_block(0, 0, 0, True)
            s5_block(1, 1, 1, False)
            with pe.Fori(1, GP // 4) as i:
                for q in range(2):
                    s5_block(2 * i + q, q, 2 * i + q, False)

            pe.wait_ge(S["sf_out"], GP // 2)
            pe.wait_ge(S["sb_out"], GP // 2)
            for r in range(ADA_RING):
                ada_chunk(1, r, 0)
            with pe.Fori(1, ADA_TURNS) as i:
                for r in range(ADA_RING):
                    ada_chunk(1, r, i)
            ada_fold(1, 2 * ADA_CHUNKS - 1, 4 * (ADA_CHUNKS - 1))

            pe.wait_ge(S["tt_in"], 128 * (GP // 2))
            pe.wait_ge(S["scanned"], 2)

            def z_T(b):
                pe.wait_ge(S["y_out"], b + 1)
                for h in range(2):
                    if b >= 2:
                        pe.wait_ge(S["z_out"], 2 * (b - 2) + h + 1)
                    for k in range(4):
                        last = pe.transpose(ps[:, 4 + 2 * (b % 2) + h, P * k:P * k + J], yst[:, 4 * h + k, :], ident[0:J, 0:J])
                    last.then_inc(S["z_T"], 1)

            for hb in range(GP // 2):
                if hb >= 4:
                    pe.wait_ge(S["y_out"], (hb - 4) // 2 + 1)
                pe.wait_ge(S["n2_re"], hb + 1)
                pe.wait_ge(S["n2_im"], hb + 1)
                for gl in range(4):
                    g = 4 * hb + gl
                    gp, h = g // 2, g % 2
                    rows = slice(STATES * h, STATES * (h + 1))
                    at = P * (gp % 4)
                    dst = ps[0:J, 2 * (hb // 2 % 2) + h, at:at + P]
                    pe.matmul(dst, U[:, g, :], TT[:, g, :], start=True, stop=False)
                    for dirn in range(2):
                        for r in range(2):
                            last = pe.matmul(dst, Sarr[rows, 0, 0:J, r, gp] if dirn == 0 else Sarr[rows, 1, 0:J, r, gp],
                                             Nr[rows, hb % 2, r, 2 * (gl // 2) + dirn, :],
                                             start=False, stop=dirn == 1 and r == 1)
                last.then_inc(S["y_done"], 1)
                if hb % 2 and hb >= 3:
                    z_T((hb - 3) // 2)
            z_T(KD - 1)

            pe.wait_ge(S["x2_in"], 32)
            for b in range(KD):
                for h in range(2):
                    if b >= 2:
                        pe.wait_ge(S["xT_out"], 2 * (b - 2) + h + 1)
                    else:
                        pe.wait_ge(S["z_out"], 2 * KD)
                    for k in range(4):
                        last = pe.transpose(ps[:, 4 + 2 * (b % 2) + h, P * k:P * k + J],
                                            xin2[:, 4 * h + k, P * b:P * (b + 1)], ident[0:J, 0:J])
                    last.then_inc(S["xT_T"], 1)

            def psum_free(ch, early):
                if not early:
                    pe.wait_ge(S["drained"], ch.drains - 2)

            def products(ch, dst, w0, nk, hi_, lo_, toks, per_block=None):
                wh, wl = (wview(w, ch.slot, w0 + nk) for w in (whi, wlo))
                for k in range(nk):
                    if per_block is not None:
                        pe.wait_ge(per_block[0], per_block[1] + k + 1)
                    for w, h, first, final in ((wh, hi_, k == 0, False), (wh, lo_, False, False),
                                               (wl, hi_, False, k == nk - 1)):
                        for (t0, t1), d in zip(((0, NLAT), (NLAT, T))[:1 if toks == NLAT else 2], dst):
                            last = pe.matmul(d, w[:, w0 + k, :], h[:, k, t0:t1], start=first, stop=final)
                return last

            def pair_stage(first, count, toks, ready):
                def one(m, c, turn):
                    ch = Chunk(first + c, turn)
                    a_l, b_l, a_c, b_c = glu_psum(ch.slot)
                    pe.wait_ge(S["lo_ready"], ch.n + 1)
                    psum_free(ch, turn is None and first + c < B_GLU + 2)
                    products(ch, (a_l, a_c), 0, KD, hhi, hlo, toks, ready if turn is None and c == 0 else None)
                    products(ch, (b_l, b_c), KD, KD, hhi, hlo, toks).then_inc(S["w_used"], 1)
                chunk_turns(pe, count, one)

            def plain_stage(first, count, nk, hi_, lo_, toks, ready=None):
                def one(m, c, turn):
                    ch = Chunk(first + c, turn)
                    a_l, _, a_c, _ = glu_psum(ch.slot)
                    pe.wait_ge(S["lo_ready"], ch.n + 1)
                    psum_free(ch, False)
                    products(ch, (a_l, a_c), 0, nk, hi_, lo_, toks, ready if turn is None and c == 0 else None)\
                        .then_inc(S["w_used"], 1)
                chunk_turns(pe, count, one)

            def norm(j, toks):
                pe.wait_ge(S["ssum_done"], j + 1)
                for t0, t1 in ((0, NLAT), (NLAT, T))[:1 if toks == NLAT else 2]:
                    last = pe.matmul(flat[:, 3072 + t0:3072 + t1], ones[:], ssum[:, t0:t1], start=True, stop=True)
                last.then_inc(S["stat_T"], 1)

            def ffn(l, toks, j):
                for g in range(2):
                    first = B_FFN[l] + g * (GF + KD)
                    pair_stage(first, GF, toks, (S["h_lo"], KD * j) if g == 0 else None)
                    plain_stage(first + GF, KD, GF, ghi, glo, toks, (S["g_lo"], KF * l + GF * g))

            pe.wait_ge(S["xT_out"], 2 * KD)
            pair_stage(B_GLU, KD, T, (S["z_lo"], 0))
            norm(0, T)
            ffn(0, T, 0)
            norm(1, T)

            unit = [0]
            job = [0]

            def sums(n, lhs, first, final):
                u = unit[0]
                unit[0] += 1
                pe.wait_ge(S["unit_sq"], u + 1)
                if first and job[0] >= 1:
                    pe.wait_ge(S["job_std"], job[0])
                for t0, t1 in ((0, NLAT), (NLAT, T))[:1 if n == NLAT else 2]:
                    last = pe.matmul(flat[:, 3072 + t0:3072 + t1], lhs[:], sqr[:, u % 2, t0:t1], start=first, stop=final)
                last.then_inc(S["unit_used"], 1)
                if final:
                    job[0] += 1

            def low_rank(c, nk, toks, ready=None):
                ch = Chunk(c)
                a_l, _, a_c, _ = glu_psum(ch.slot)
                pe.wait_ge(S["lo_ready"], ch.n + 1)
                psum_free(ch, False)
                products(ch, (a_l, a_c), 0, nk, *((hhi, hlo) if nk == KD else (cq_hi, cq_lo)), toks, ready)\
                    .then_inc(S["w_used"], 1)

            for m in range(3):
                low_rank(B_DKV + m, KD, T, (S["h_lo"], KD) if m == 0 else None)
                if m >= 1:
                    sums(T, ones, m == 1, m == 2)
            for m in range(6):
                low_rank(B_DQ + m, KD, NLAT)
                if m == 0:
                    sums(T, half_ones, True, True)
                else:
                    sums(NLAT, ones, m == 1, False)
            sums(NLAT, ones, False, True)
            use = used_after(B_UKV - 1)
            for m in range(4):
                ch = Chunk(B_UKV + m)
                pe.wait_ge(S["lo_ready"], ch.n + 1)
                wh, wl = (wview(w, ch.slot, 2, 4 * P) for w in (whi, wlo))
                for t in range(KV_USES[m]):
                    use += 1
                    a_l, _, a_c, _ = glu_psum((use - 1) % 2)
                    pe.wait_ge(S["drained"], use - B_GLU - 2)
                    if m == 0 and t == 0:
                        pe.wait_ge(S["ckv_lo_s"], 2)
                    for k in range(2):
                        for w, h, first, final in ((wh, ckv_hi, k == 0, False), (wh, ckv_lo, False, False),
                                                   (wl, ckv_hi, False, k == 1)):
                            if m < 2:
                                for (t0, t1), d in zip(((0, NLAT), (NLAT, T)), (a_l, a_c)):
                                    last = pe.matmul(d, w[:, k, P * t:P * (t + 1)], h[:, k, t0:t1], start=first, stop=final)
                            else:
                                last = pe.matmul(a_l, h[:, k, P * t:P * (t + 1)], w[:, k, :], start=first, stop=final)
                    last.then_inc(S["w_used"], 1)
                    if m < 2 and 4 * m + t >= 1:
                        sums(T, ones, True, True)
                    if m == 2 and t == 0:
                        sums(T, ones, True, True)
            for m in range(12):
                low_rank(B_UQ + m, 6, NLAT, (S["cq_lo_s"], 0) if m == 0 else None)
                if m >= 1:
                    sums(NLAT, ones if m - 1 < HEADS else half_ones, True, True)
            sums(NLAT, half_ones, True, True)
            pe.wait_ge(S["job_out"], JOB_UNITS[-1])
            for n, v in enumerate([kr[:, 0:NLAT]] + [q_all[:, HEADS + m, :] for m in range(4)]):
                if n >= 1:
                    pe.wait_ge(S["rot_done"], n)
                pe.matmul(ps[:, 7, :], swap[:], v, start=True, stop=True).then_inc(S["swap_T"], 1)
            pe.wait_ge(S["rot_done"], 5)

            def scores(i):
                h, t = i // 4, i % 4
                if i >= 2:
                    pe.wait_ge(S["ex_done"], i - 1)
                rows = slice(ROPE * (h % 2), ROPE * (h % 2 + 1))
                for t0, t1 in ((0, NLAT), (NLAT, T)):
                    d = flat[:, 1024 * (i % 2) + t0:1024 * (i % 2) + t1]
                    pe.matmul(d, q_all[:, h, P * t:P * (t + 1)], kn[:, h, t0:t1], start=True, stop=False)
                    last = pe.matmul(d, q_all[rows, HEADS + h // 2, P * t:P * (t + 1)], kr[rows, t0:t1], start=False, stop=True)
                last.then_inc(S["sc_done"], 1)

            def head_out(h):
                pe.wait_ge(S["pT_out"], 4 * h + 4)
                if h >= 2:
                    pe.wait_ge(S["ot_out"], h - 1)
                for b in range(6):
                    last = pe.matmul(ps[:, 6 + h % 2, :], val[:, b, VD * h:VD * (h + 1)], pT[:, h % 2, b, :],
                                     start=b == 0, stop=b == 5)
                last.then_inc(S["pv_done"], 1)

            scores(0)
            for i in range(4 * HEADS):
                if i + 1 < 4 * HEADS:
                    scores(i + 1)
                pe.wait_ge(S["pr_set"], i + 1)
                if i >= 1:
                    pe.wait_ge(S["pT_out"], i)
                for b in range(6):
                    last = pe.transpose(flat[:, 2048 + P * b:2048 + P * (b + 1)], pr[:, i % 2, P * b:P * (b + 1)], ident[:])
                last.then_inc(S["p_T"], 1)
                if i % 4 == 0 and i:
                    head_out(i // 4 - 1)
            head_out(HEADS - 1)
            plain_stage(B_WO, KD, KD, hhi, hlo, NLAT, (S["o_lo"], 0))
            norm(2, NLAT)
            ffn(1, NLAT, 2)

            pe.wait_ge(S["drained"], used_after(B_FFN[1] + 2 * (GF + KD) - 1) - B_GLU)
            for t in range(4):
                for h in range(2):
                    if 2 * t + h >= 4:
                        pe.wait_ge(S["fin_out"], 2 * t + h - 3)
                    for b in range(4):
                        last = pe.transpose(ps[:, (2 * t + h) % 4, P * b:P * (b + 1)], xT[:, 4 * h + b, P * t:P * (t + 1)],
                                            ident[:])
                    last.then_inc(S["fin_T"], 1)


INPUTS = ("x", "c", "ctx", "c_ctx", "ada_w", "ada_b", "norm_mix", "norm_ffn", "s5_lam_re", "s5_lam_im", "s5_log_dt",
          "s5_b_re", "s5_b_im", "s5_c_re", "s5_c_im", "s5_d", "s5_glu_w", "s5_glu_b", "mla_w_dq", "mla_g_q", "mla_w_uq",
          "mla_w_dkv", "mla_g_kv", "mla_w_ukv", "mla_g_qn", "mla_g_qr", "mla_g_kn", "mla_g_kr", "mla_w_o",
          "ffn_w_in", "ffn_conv_w", "ffn_conv_b", "ffn_w_out")


def tables():
    grid, axis, freqs = 64, ROPE // 2, ROPE // 4
    tabs = np.zeros((P, TAB_N), np.float32)
    tabs[:, TAB_IDENT:TAB_IDENT + P] = np.eye(P, dtype=np.float32)
    inv = (np.float32(10000.0) ** (-np.arange(freqs, dtype=np.float32) / np.float32(freqs))).astype(np.float32)
    tok = np.arange(NLAT)
    for p in range(P):
        q, f = p % axis, p % freqs
        pos = tok // grid if (p % ROPE) < axis else tok % grid
        ang = pos.astype(np.float32) * inv[f]
        tabs[p, TAB_COS:TAB_COS + NLAT] = np.cos(ang)
        tabs[p, TAB_SIN:TAB_SIN + NLAT] = np.sin(ang)
        if q < freqs:
            tabs[p + freqs, TAB_SWAP + p] = -1.0
        else:
            tabs[p - freqs, TAB_SWAP + p] = 1.0
        h = p // ROPE
        tabs[p, TAB_HALF + h * ROPE:TAB_HALF + (h + 1) * ROPE] = 1.0
    return tabs


def kernel(**inputs):
    import concourse.bacc as bacc
    from concourse.bass_utils import run_bass_kernel_spmd

    nc = bacc.Bacc("TRN2", target_bir_lowering=False, num_devices=1)
    arrays = {f"in_{n}": np.ascontiguousarray(inputs[n]) for n in INPUTS}
    arrays["in_tabs"] = tables()
    a = {n[3:]: nc.dram_tensor(n, v.shape, mybir.dt.from_np(v.dtype), kind="ExternalInput").ap()
         for n, v in arrays.items()}
    a["out"] = nc.dram_tensor("out", (1, NLAT, D), F32, kind="ExternalOutput").ap()
    build(nc, a)
    r = run_bass_kernel_spmd(nc, [arrays], core_ids=[0])
    return r.results[0]["out"]
```

```python
from contextlib import ExitStack

import numpy as np

import concourse.bass as bass
from concourse import mybir

F32 = mybir.dt.float32
F32R = mybir.dt.float32r
ALU = mybir.AluOpType
ACT = mybir.ActivationFunctionType
AX = mybir.AxisListType

P = 128
D = 1024
KD = D // P
NLAT, NCTX = 512, 256
T = NLAT + NCTX
EPS = 1e-6
GROUPS, CH, STATES, CK = 64, 16, 64, 8
GP = GROUPS // 2
JCTX, JLAT = NCTX // CK, NLAT // CK
J = JCTX + JLAT
DG = 2 * GP
HEADS, NOPE, ROPE, VD, QR, KVR = 8, 128, 64, 128, 768, 256
SCALE = 1.0 / float(np.sqrt(NOPE + ROPE))
FFN = 2816
KF = FFN // P
GF = KF // 2
SLOT = 2 * KD * P
ADA_CHUNKS = 6 * D // 256
HX = 3
ADA_RING = 4
ADA_TURNS = ADA_CHUNKS // ADA_RING
CTX_HOP = (J + 1) + JLAT
LAT_HOP = (J + 1) - JCTX
TWO_PI_HI, TWO_PI_LO = 6.28125, 0.0019353071795864769
ROUND = 12582912.0
PI = 3.1415925

TAB_IDENT, TAB_SWAP, TAB_HALF, TAB_COS, TAB_SIN = 0, P, 2 * P, 3 * P, 3 * P + NLAT
TAB_N = 3 * P + 2 * NLAT

C_ADAB, C_NMIX, C_NFFN = 0, 96, 112
C_C, C_CC, C_GLUB, C_GQ, C_GKV, C_GQN, C_GKN, C_GQR, C_GKR, C_CONVB = 0, 8, 16, 32, 38, 40, 41, 42, 43, 44
SH_M, SC_M, G_M, SH_F, SC_F, G_F = 0, 8, 16, 24, 32, 40


class Chain:

    def __init__(self, eng, sem):
        self.eng, self.sem, self.count, self.turn, self.per = eng, sem, 0, None, 0

    def mark(self, op):
        op.then_inc(self.sem, 1)
        self.count += 1

    def need(self, back):
        n = self.count - back
        self.eng.wait_ge(self.sem, n if self.turn is None else self.turn * self.per + n)

    def link(self, op):
        self.mark(op)
        self.need(0)

    def enter(self, turn, per):
        self.turn, self.per, self.start = turn, per, self.count

    def leave(self, turns):
        assert self.count - self.start == self.per, (self.count - self.start, self.per)
        self.count, self.turn = self.start + self.per * turns, None


B_GLU = 0
B_FFN = (B_GLU + KD, B_GLU + KD + 2 * (GF + KD) + 3 + 6 + 4 + 12 + KD)
B_DKV = B_FFN[0] + 2 * (GF + KD)
B_DQ = B_DKV + 3
B_UKV = B_DQ + QR // P
B_UQ = B_UKV + 4
B_WO = B_UQ + HEADS + HEADS // 2
ROPE_PAIRS = HEADS // 2
KV_USES = (4, 4, 6, 6)


JOB_UNITS = (2, 3) + tuple(range(9, 30))


def used_after(c):
    return c + 1 + sum(n - 1 for n in KV_USES[:max(0, c + 1 - B_UKV)])


class Chunk:

    def __init__(self, first, turn=None):
        step = 0 if turn is None else 2 * turn
        self.slot = first % 2
        self.reuse = first >= 2 or turn is not None
        self.n = first + step
        self.nth = (first - B_GLU) // 2 + (0 if turn is None else turn)
        self.done = used_after(first) + step
        self.free = used_after(first - 2) + step
        self.drains = self.done - B_GLU


def stage_turns(eng, count, split, epi, ahead):
    for m in range(2):
        split(m + 1, None)
        epi(m, m, None)
    pairs = (count - 3) // 2
    if pairs > 0:
        with eng.Fori(1, 1 + pairs) as i:
            for m in range(2):
                split(m + 1, i)
                epi(2 * i + m, m, i)
    for m in range(2 + 2 * max(pairs, 0), count - 1):
        split(m + 1, None)
        epi(m, m, None)
    ahead()
    epi(count - 1, count - 1, None)


def chunk_turns(eng, count, one):
    for m in range(2):
        one(m, m, None)
    if count >= 4:
        with eng.Fori(1, count // 2) as i:
            for m in range(2):
                one(2 * i + m, m, i)
    if count % 2:
        one(count - 1, count - 1, None)


def build(nc, a):
    with ExitStack() as ctx:
        def sb(name, shape, dt=F32, stack=None):
            return (stack or ctx).enter_context(nc.sbuf_tensor(name, shape, dt))

        def sem(name):
            return ctx.enter_context(nc.semaphore(name))

        wraw = sb("wraw", [P, 2, SLOT])
        ident = sb("ident", [P, P])
        ones = sb("ones", [P, P])
        swap = sb("swap", [P, P])
        half_ones = sb("half_ones", [P, P])
        colsA = sb("colsA", [P, 128])
        colsB = sb("colsB", [P, 88])
        colsW = sb("colsW", [P, 2, 66])
        modc = sb("modc", [P, 2, 48, 2])
        gain = sb("gain", [P, 2, 2, KD, 2])
        silu_c = sb("silu_c", [P, KD, 2])
        ada_rows = sb("ada_rows", [2, 256])
        eps = sb("eps", [P, 1])
        wt = sb("wt", [P, 1])
        zero = sb("zero", [P, 1])

        s5 = ExitStack()
        MN = sb("MN", [P, 2, 2, 2, 4, P], stack=s5)
        Mr = MN[:, 0]
        tN = MN[:, 1, 0]
        MT = sb("MT", [P, 2, 4, P], stack=s5)
        Kext = sb("Kext", [CH, 4, 15, CH], stack=s5)
        kernels = [Kext[:], MN[0:CH, 1, 1].rearrange("c r g x -> c (r g x)")[:, 0:4 * 15 * CH]
                   .rearrange("c (g t o) -> c g t o", g=4, t=15)]
        tD = sb("tD", [P, 2, 4, CK, CH], stack=s5)
        tP = sb("tP", [P, 2, 4, CK, CH], stack=s5)
        sb("s5_pad", [P, 64], stack=s5)
        Sarr = sb("Sarr", [P, 2, J + 1, 2, GP], stack=s5)
        TT = sb("TT", [P, GROUPS, P], stack=s5)
        Bc = sb("Bc", [P, 2, DG, CH], stack=s5)
        Cc = sb("Cc", [P, 2, DG, CH], stack=s5)
        pw = sb("pw", [P, 2, DG, 9], stack=s5)
        QP = sb("QP", [P, 2, 2, DG, CK], stack=s5)
        Qk, Pk = QP[:, 0], QP[:, 1]
        Pn = sb("Pn", [P, 2, DG, CK], stack=s5)
        U = sb("U", [P, GROUPS, J], stack=s5)
        s5.close()
        pre = ExitStack()
        sb("pre_gap", [P, 4 * SLOT], stack=pre)
        rowsA = sb("rowsA", [P, P], stack=pre)
        rowsB = sb("rowsB", [88, P], stack=pre)
        rowsW = sb("rowsW", [66, 2, P], stack=pre)
        lam = sb("lam", [DG, 2, P], stack=pre)
        ldt = sb("ldt", [DG, 2], stack=pre)
        brow = sb("brow", [DG, 2, 2048], stack=pre)
        crow = sb("crow", [DG, 2, 2048], stack=pre)
        disc = sb("disc", [DG, 12, P], stack=pre)
        sc4 = sb("sc4", [P, 8, CK * 4], stack=pre)
        sgc = sb("sgc", [P, 16], stack=pre)
        drow = sb("drow", [GROUPS, CH], stack=pre)
        pre.close()
        pre3 = ExitStack()
        sb("pre3_gap", [P, 4 * SLOT], stack=pre3)
        xn = sb("xn", [J, GROUPS, CK, CH], stack=pre3)
        pre3.close()
        pre2 = ExitStack()
        sb("pre2_gap", [P, 4 * SLOT + (J + 1) * P], stack=pre2)
        xin = sb("xin", [J, CK, D], stack=pre2)
        pre2.close()
        late = ExitStack()
        sb("late_gap", [P, 4 * SLOT + (J + 1) * P + GROUPS * P + 2 * 2 * DG * CH + 2 * DG * 9 + 6 * DG * CK + GROUPS * J],
           stack=late)
        acoef = sb("acoef", [P, 4, DG], stack=late)
        cm = sb("cm", [P, 2, DG, 8], stack=late)
        stat = sb("stat", [J, 2, CK], stack=late)
        urep = sb("urep", [P, 2, 2, GROUPS], stack=late)
        kd = sb("kd", [CH, GROUPS, CH], stack=late)
        d16 = sb("d16", [CH, GROUPS], stack=late)
        a8 = sb("a8", [P, 2, 2, 2, GP], stack=late)
        sc = sb("sc", [P, 2, 3, 2, GP], stack=late)
        pick = sb("pick", [P, KD, CK, CH], stack=late)
        yst = pick[0:J].rearrange("j a k c -> j (a k c)").rearrange("j (k n) -> j k n", k=CK)
        late.close()

        whi = sb("whi", [P, 2, SLOT], F32R)
        wlo = sb("wlo", [P, 2, SLOT], F32R)
        kv = ExitStack()
        kn = sb("kn", [P, HEADS, T], stack=kv)
        val = sb("val", [P, 6, HEADS * VD], stack=kv)
        kv.close()
        hhi = sb("hhi", [P, KD, T], F32R)
        hlo = sb("hlo", [P, KD, T], F32R)
        xT = sb("xT", [P, KD, T])
        ffn = ExitStack()
        ghi = sb("ghi", [P, GF, T], F32R, stack=ffn)
        glo = sb("glo", [P, GF, T], F32R, stack=ffn)
        acc = sb("acc", [P, 2, T], stack=ffn)
        ffn.close()
        nrm = ExitStack()
        sq = sb("sq", [P, KD, T], stack=nrm)
        rstd = sb("rstd", [P, T], stack=nrm)
        hx = sb("hx", [P, HX, T], stack=nrm)
        nrm.close()
        mla = ExitStack()
        q_all = sb("q_all", [P, 12, NLAT], stack=mla)
        kr = sb("kr", [P, T], stack=mla)
        rope_cs = sb("rope_cs", [P, 2, NLAT], stack=mla)
        rs0 = sb("rs0", [P, T], stack=mla)
        ckv_hi = sb("ckv_hi", [P, 2, T], F32R, stack=mla)
        ckv_lo = sb("ckv_lo", [P, 2, T], F32R, stack=mla)
        cq_hi = sb("cq_hi", [P, 6, NLAT], F32R, stack=mla)
        cq_lo = sb("cq_lo", [P, 6, NLAT], F32R, stack=mla)
        sqr = sb("sqr", [P, 2, T], stack=mla)
        rs1 = sb("rs1", [P, T], stack=mla)
        rs = (rs0, rs1)
        mla.close()
        raw = ExitStack()
        ckv_raw = sb("ckv_raw", [P, 2, T], stack=raw)
        cq_raw = sb("cq_raw", [P, 6, NLAT], stack=raw)
        raw.close()
        att = ExitStack()
        sb("att_gap", [P, 12 * NLAT + T + 2 * NLAT + T], stack=att)
        pr = sb("pr", [P, 2, T], stack=att)
        pT = sb("pT", [P, 2, 6, NLAT], stack=att)
        ot = sb("ot", [P, HEADS, NLAT], stack=att)
        smax = sb("smax", [P, 2, 4], stack=att)
        att.close()
        glu = ExitStack()
        xin2 = sb("xin2", [J, CK, D], stack=glu)
        glu.close()
        glu2 = ExitStack()
        sb("glu2_gap", [P, 2 * GF * T], stack=glu2)
        sig = sb("sig", [P, 2, T], stack=glu2)
        glu2.close()

        ps = ctx.enter_context(nc.psum_tensor("ps", [P, 8, 512], F32))
        flat = ps[:].rearrange("p b n -> p (b n)")

        names = """params_in lam_in s5rows_in d16_in x_in tabs_in const_set cols_T cols_out cond_ready act_link dve_link pool_link
            ada_in0 ada_in1 ada_in2 ada_in3 wload0 wload1 ada_used row_out ada_folded hi_ready lo_ready w_used drained
            rowsum_done rstd_set dt_set disc_a disc_b exp_done sin_done disc_T disc_out bc_T bc_out tab_set
            ada0_set rep_done rep_out u_T u_dve u_act kd_set
            m_ready n_ready n_prod n_im mt_T mt_out k_done kf_out kext_ready tt_in0 tt_in1 s_done sf_out sb_out s_zero
            scanned half_scanned half_saved pn_set n2m n2_re n2_im y_done y_out z_T z_out z_hi z_lo x2_in xT_T xT_out
            sig_done act_acc dve_g hi_g g_split mix_done
            sq_done sq_added stat_T std_done rinv xn_done hx_done h_hi h_lo
            acc_set conv_done silu_done g_done g_hi g_lo rope_in
            unit_sq unit_used job_std ckv_set cq_set swap_T rot_done job_rinv job_out ckv_hi_s ckv_lo_s cq_hi_s cq_lo_s kr_swap kr_set q_swap q_set
            kv_out sc_done mx_set ex_done pr_set p_T pT_out pv_done ot_out o_hi o_lo
            fin_T fin_out out_done ssum_set""".split()
        S = {n: sem(n) for n in names}
        wload = (S["wload0"], S["wload1"])

        tt_in = (S["tt_in0"], S["tt_in1"])

        def wview(t, slot, k, n=P):
            return t[:, slot, 0:k * n].rearrange("p (k n) -> p k n", k=k)

        def glu_psum(q):
            return ps[:, 3 * q, :], ps[:, 3 * q + 1, :], ps[:, 3 * q + 2, 0:NCTX], ps[:, 3 * q + 2, NCTX:2 * NCTX]

        U_rows = U[:].rearrange("p g j -> p (g j)")
        ada_raw = ([wraw[:, 0], wraw[:, 1], U_rows[:, 0:SLOT], U_rows[:, SLOT:2 * SLOT]],
                   [Bc[:].rearrange("p r g c -> p (r g c)"), QP[:].rearrange("p q r g k -> p (q r g k)"), wraw[:, 0], wraw[:, 1]])
        ada_in = [S[f"ada_in{r}"] for r in range(ADA_RING)]

        def hhi_out(t):
            return sq[:].rearrange("p k t -> p (k t)")[:, t * D:(t + 1) * D]

        def u_parts(q):
            return [(4 * q + r, j0, j1, cond) for r in range(4) for j0, j1, cond in ((0, JCTX, 1), (JCTX, J, 0))]

        N_loop = wraw[:].rearrange("p s n -> p (s n)").rearrange("p (q r g h x) -> p q r g h x", q=2, r=2, g=4, h=2)
        N_out = MN[:].rearrange("p a b r g x -> p (a b r g x)").rearrange("p (q r g h x) -> p q r g h x", q=2, r=2, g=4, h=2)

        def clear_others(eng, n_all, r):
            for h in range(2):
                last = eng.memset(n_all[STATES * h:STATES * (h + 1), :, r, :, 1 - h, :], 0.0)
            return last

        def own_columns(n_all, q, r, h):
            rows = slice(STATES * h, STATES * (h + 1))
            return rows, n_all[rows, q, r, :, h, :].rearrange("p g (k c) -> p g k c", k=CK)

        squares = ((sq[:, 0], sq[:, 1]), (acc[:, 0], acc[:, 1]), (sq[:, 0], sq[:, 1]))
        SQ_ADDS = KD - 2

        rotated = [kr[:, 0:NLAT]] + [q_all[:, HEADS + m, :] for m in range(ROPE_PAIRS)]
        SWAP_BANKS = (1, 4)

        def q_block(m):
            return q_all[:, HEADS + m if m < ROPE_PAIRS else m - ROPE_PAIRS, :]

        after = ((SLOT, KD * P), (SLOT, 0))

        block = ctx.enter_context(nc.Block())

        @block.sync
        def _(sp):
            rows = "o d (g h) s -> (o d g) (h s)"
            sp.dma_start(lam[:, 0, :], a["s5_lam_re"].rearrange(rows, h=2)).then_inc(S["lam_in"], 16)
            sp.dma_start(lam[:, 1, :], a["s5_lam_im"].rearrange(rows, h=2)).then_inc(S["lam_in"], 16)
            sp.dma_start(ldt[:], a["s5_log_dt"].rearrange("o d (g h) -> (o d g) h", h=2)).then_inc(S["lam_in"], 16)
            sp.dma_start(rowsB[C_C:C_C + 8, :], a["c"].rearrange("o (r c) -> (o r) c", c=P)).then_inc(S["params_in"], 16)
            sp.dma_start(rowsB[C_CC:C_CC + 8, :], a["c_ctx"].rearrange("(r c) -> r c", c=P)).then_inc(S["params_in"], 16)
            sp.dma_start(rowsA[0:96, :], a["ada_b"].rearrange("l (r c) -> (l r) c", c=P)).then_inc(S["params_in"], 16)
            sp.dma_start(rowsA[96:112, :], a["norm_mix"].rearrange("l (r c) -> (l r) c", c=P)).then_inc(S["params_in"], 16)
            sp.dma_start(rowsA[112:128, :], a["norm_ffn"].rearrange("l (r c) -> (l r) c", c=P)).then_inc(S["params_in"], 16)
            for at, name in ((C_GLUB, "s5_glu_b"), (C_GQ, "mla_g_q"), (C_GKV, "mla_g_kv"), (C_GQN, "mla_g_qn"),
                             (C_GKN, "mla_g_kn"), (C_CONVB, "ffn_conv_b")):
                src = a[name].rearrange("l (r c) -> (l r) c", c=P)
                sp.dma_start(rowsB[at:at + src.shape[0], :], src).then_inc(S["params_in"], 16)
            for at, name in ((C_GQR, "mla_g_qr"), (C_GKR, "mla_g_kr")):
                for h in range(2):
                    sp.dma_start(rowsB[at:at + 1, h * ROPE:(h + 1) * ROPE], a[name]).then_inc(S["params_in"], 16)
            for l in range(2):
                sp.dma_start(rowsW[:, l, :], a["ffn_conv_w"][l].rearrange("t (r c) -> (t r) c", c=P))\
                    .then_inc(S["params_in"], 16)
            for t, at in ((ident, TAB_IDENT), (swap, TAB_SWAP), (half_ones, TAB_HALF)):
                sp.dma_start(t[:], a["tabs"][:, at:at + P]).then_inc(S["params_in"], 16)
            sp.dma_start(drow[:], a["s5_d"].rearrange("o (g c) -> (o g) c", c=CH)).then_inc(S["params_in"], 16)

            def ada_load(l, r, turn):
                if not (isinstance(turn, int) and turn == 0):
                    sp.wait_ge(S["ada_used"], ADA_RING * turn + (l * ADA_CHUNKS + r + 1 - ADA_RING))
                w = a["ada_w"][l].rearrange("(k p) n -> p k n", p=P)
                sp.dma_start(ada_raw[l][r].rearrange("p (k n) -> p k n", k=KD),
                             w[:, :, bass.ds((ADA_RING * turn + r) * 256, 256)]).then_inc(ada_in[r], 16)

            def ada_turns(l):
                with sp.Fori(1, ADA_TURNS) as i:
                    for r in range(ADA_RING):
                        ada_load(l, r, i)

            for r in range(ADA_RING):
                ada_load(0, r, 0)
            for q, name in ((0, "s5_b_re"), (1, "s5_b_im")):
                sp.dma_start(brow[:, q, :], a[name].rearrange("o d (g h) x y -> (o d g) (h x y)", h=2))\
                    .then_inc(S["s5rows_in"], 16)
            for q, name in ((0, "s5_c_re"), (1, "s5_c_im")):
                for h in range(2):
                    sp.dma_start(crow[:, q, :].rearrange("p (c h s) -> p h c s", h=2, c=CH)[:, h],
                                 a[name].rearrange("o d (g h) c s -> (o d g) h c s", h=2)[:, h]).then_inc(S["s5rows_in"], 16)
            ada_turns(0)

            def toeplitz(b, q, n):
                sp.wait_ge(S["kext_ready"], n + 1)
                for k in range(CK):
                    sp.dma_start(TT[CH * k:CH * (k + 1), bass.ds(4 * b, 4), :],
                                 kernels[q][:, :, CK - 1 - k:2 * CK - 1 - k, :].rearrange("c g t o -> c g (t o)"))\
                        .then_inc(tt_in[q], 16)

            with sp.Fori(0, GP // 4) as i:
                for q in range(2):
                    toeplitz(2 * i + q, q, 2 * i + q)

            sp.wait_ge(S["m_ready"], GP // 2)
            sp.wait_ge(S["n_ready"], GP // 2)
            for r in range(2):
                ada_load(1, r, 0)
            sp.wait_ge(S["k_done"], GP // 2)
            for r in range(2, ADA_RING):
                ada_load(1, r, 0)
            ada_turns(1)

            sp.wait_ge(S["scanned"], 2)

            def load_x_again():
                sp.wait_ge(S["y_done"], 2 * KD)
                for dst, src in ((xin2[0:JCTX], a["ctx"]), (xin2[JCTX:J], a["x"])):
                    sp.dma_start(dst, src.rearrange("o (j k) d -> (o j) k d", k=CK)).then_inc(S["x2_in"], 16)

            def stage(first, count, fill):
                def one(m, c, turn):
                    ch = Chunk(first + c, turn)
                    if ch.reuse:
                        sp.wait_ge(S["lo_ready"], ch.n - 1)
                    moves = fill(ch.slot, m)
                    for dst, src in moves:
                        sp.dma_start(dst, src).then_inc(wload[ch.slot], 32 // len(moves))
                    if first == B_GLU and isinstance(m, int) and m == 1:
                        load_x_again()
                chunk_turns(sp, count, one)

            def half(w):
                v = w.rearrange("(k p) (h n) -> p k h n", p=P, h=2)
                return lambda slot, m: [(wraw[:, slot, :].rearrange("p (h k n) -> p h k n", h=2, n=P)[:, h],
                                         v[:, :, h, bass.ds(m * P, P)]) for h in range(2)]

            def whole(w):
                v = w.rearrange("(k p) n -> p k n", p=P)
                return lambda slot, m: [(wview(wraw, slot, w.shape[0] // P), v[:, :, bass.ds(m * P, P)])]

            stage(B_GLU, KD, half(a["s5_glu_w"][0]))

            def ffn_weights(l):
                for g in range(2):
                    wi = a["ffn_w_in"][l].rearrange("(k p) (h n) -> p k h n", p=P, h=2)[:, :, :, g * GF * P:(g + 1) * GF * P]
                    stage(B_FFN[l] + g * (GF + KD), GF, lambda slot, m: [
                        (wraw[:, slot, :].rearrange("p (h k n) -> p h k n", h=2, n=P)[:, h],
                         wi[:, :, h, bass.ds(m * P, P)]) for h in range(2)])
                    stage(B_FFN[l] + g * (GF + KD) + GF, KD, whole(a["ffn_w_out"][l][g * GF * P:(g + 1) * GF * P, :]))

            ffn_weights(0)
            dkv = a["mla_w_dkv"][0].rearrange("(k p) n -> p k n", p=P)
            stage(B_DKV, 3, lambda slot, m: [(wview(wraw, slot, KD), dkv[:, :, m * P:(m + 1) * P])] if m < 2 else
                  [(wview(wraw, slot, KD)[:, :, ROPE * h:ROPE * (h + 1)], dkv[:, :, KVR:]) for h in range(2)])
            stage(B_DQ, QR // P, whole(a["mla_w_dq"][0]))
            ukv = a["mla_w_ukv"][0].rearrange("(k p) (h v n) -> p k v h n", p=P, h=HEADS, v=2)
            for m in range(4):
                ch = Chunk(B_UKV + m)
                sp.wait_ge(S["lo_ready"], ch.n - 1)
                for k in range(2):
                    sp.dma_start(wview(wraw, ch.slot, 2, 4 * P)[:, k, :].rearrange("p (h n) -> p h n", h=4),
                                 ukv[:, k, m // 2, 4 * (m % 2):4 * (m % 2) + 4, :]).then_inc(wload[ch.slot], 16)
            sp.wait_ge(S["h_lo"], 2 * KD)
            sp.dma_start(rope_cs[:].rearrange("p a t -> p (a t)"), a["tabs"][:, TAB_COS:]).then_inc(S["rope_in"], 16)
            uq = a["mla_w_uq"][0].rearrange("(k p) (h n) -> p k h n", p=P, h=HEADS)
            for m in range(ROPE_PAIRS):
                ch = Chunk(B_UQ + m)
                sp.wait_ge(S["lo_ready"], ch.n - 1)
                for h in range(2):
                    sp.dma_start(wview(wraw, ch.slot, 6)[:, :, ROPE * h:ROPE * (h + 1)], uq[:, :, 2 * m + h, NOPE:])\
                        .then_inc(wload[ch.slot], 16)
            stage(B_UQ + ROPE_PAIRS, HEADS, lambda slot, m: [(wview(wraw, slot, 6),
                                                              uq[:, :, bass.ds(m, 1), 0:NOPE].rearrange("p k o n -> p k (o n)"))])
            stage(B_WO, KD, whole(a["mla_w_o"][0]))
            ffn_weights(1)

            sp.wait_ge(S["fin_out"], 8)
            sp.wait_ge(S["out_done"], 16 * 4)

        @block.gpsimd
        def _(pool):
            chain = Chain(pool, S["pool_link"])
            pool.wait_ge(S["params_in"], 16 * 21)
            pool.tensor_copy(pick[:], ident[:].rearrange("p (g c) -> p g c", c=CH).unsqueeze(2)
                             .to_broadcast([P, KD, CK, CH])).then_inc(S["tabs_in"], 1)
            pool.wait_ge(S["tabs_in"], 1)
            def n_block(b, q, n):
                dg = bass.ds(4 * b, 4)
                if n is not None:
                    pool.wait_ge(S["n_ready"], n + 1)
                    pool.wait_ge(S["n_im"], n + 1)
                    pool.wait_ge(S["k_done"], n)
                    pool.tensor_tensor(wt[:], zero[:], zero[:], ALU.add)
                p_re, p_im = (Pk[:, r, dg, :].unsqueeze(3).to_broadcast([P, 4, CK, CH]) for r in range(2))
                c_re, c_ni = (Cc[:, r, dg, :].unsqueeze(2).to_broadcast([P, 4, CK, CH]) for r in range(2))
                t_re, t_im = (tN[:, r].rearrange("p g (k c) -> p g k c", k=CK) for r in range(2))
                pool.tensor_tensor(t_im, p_re, c_ni, ALU.mult)
                pool.tensor_tensor(tP[:, 1], p_im, c_re, ALU.mult).then_inc(S["n_prod"], 1)
                pool.tensor_tensor(t_re, p_re, c_re, ALU.mult)
                chain.link(pool.tensor_tensor(tP[:, 0], p_im, c_ni, ALU.mult))
                for h in range(2):
                    rows, dst = own_columns(N_loop, q, 0, h)
                    last = pool.tensor_tensor(dst, t_re[rows], tP[rows, 0], ALU.add)
                last.then_inc(S["n_ready"], 1)

            pool.wait_ge(S["tab_set"], 1)
            pool.wait_ge(S["ada_used"], ADA_CHUNKS)
            clear_others(pool, N_loop, 0)
            chain.link(clear_others(pool, N_loop, 1))
            for q in range(2):
                n_block(q, q, None)
                if q == 0:
                    pool.wait_ge(S["n_ready"], 1)
                    pool.wait_ge(S["n_im"], 1)
            with pool.Fori(1, GP // 4) as i:
                chain.enter(i - 1, 2)
                for q in range(2):
                    n_block(2 * i + q, q, 2 * i + q - 1)
            chain.leave(GP // 4 - 1)

            pool.wait_ge(S["s_done"], GP // 2)
            pool.wait_ge(S["n_im"], GP // 2)
            pool.wait_ge(S["n_ready"], GP // 2)
            for q in range(2):
                pool.wait_ge(tt_in[q], 128 * (GP // 4))
            clear_others(pool, N_out, 0)
            chain.link(clear_others(pool, N_out, 1))
            for hb in range(GP // 2):
                dg = slice(4 * hb, 4 * hb + 4)
                p_re, p_im = (Pn[:, r, dg, :].unsqueeze(3).to_broadcast([P, 4, CK, CH]) for r in range(2))
                c_re, c_ni = (Cc[:, r, dg, :].unsqueeze(2).to_broadcast([P, 4, CK, CH]) for r in range(2))
                if hb >= 2:
                    pool.wait_ge(S["y_done"], hb - 1)
                pool.tensor_tensor(tP[:, 0], p_re, c_ni, ALU.mult)
                chain.link(pool.tensor_tensor(tP[:, 1], p_im, c_re, ALU.mult))
                for h in range(2):
                    rows, dst = own_columns(N_out, hb % 2, 1, h)
                    last = pool.tensor_tensor(dst, tP[rows, 0], tP[rows, 1], ALU.subtract)
                last.then_inc(S["n2_im"], 1)
                pool.wait_ge(S["n2_im"], hb + 1)
            for b in range(KD):
                pool.wait_ge(S["z_hi"], b + 1)
                pool.tensor_tensor(hlo[:, b, :], U[:].rearrange("p g j -> p (g j)")[:, T * b:T * b + T],
                                   hhi[:, b, :].bitcast(F32), ALU.subtract).then_inc(S["z_lo"], 1)

            def add_squares(j, toks):
                total, block = squares[j]
                for b in range(1, KD - 1):
                    pool.wait_ge(S["sq_done"], KD * j + b + 1)
                    if b >= 2:
                        pool.wait_ge(S["sq_added"], SQ_ADDS * j + b - 1)
                    pool.tensor_tensor(total[:, 0:toks], total[:, 0:toks], block[:, 0:toks], ALU.add).then_inc(S["sq_added"], 1)

            def norm_low(j, toks):
                for b in range(KD):
                    n = KD * j + b + 1
                    pool.wait_ge(S["h_hi"], n)
                    pool.tensor_tensor(hlo[:, b, 0:toks], hx[:, b % HX, 0:toks], hhi[:, b, 0:toks].bitcast(F32),
                                       ALU.subtract).then_inc(S["h_lo"], 1)

            def ffn_low(l, toks):
                for g in range(2):
                    def one(m, c, turn):
                        ch = Chunk(B_FFN[l] + g * (GF + KD) + c, turn)
                        f = KF * l + GF * g + m
                        if l or g or turn is not None or c:
                            pool.wait_ge(S["g_lo"], f)
                        pool.wait_ge(S["g_hi"], f + 1)
                        pool.tensor_tensor(wt[:], zero[:], zero[:], ALU.add)
                        pool.tensor_tensor(glo[:, bass.ds(m, 1), 0:toks].rearrange("p a t -> p (a t)"), acc[:, ch.slot, 0:toks],
                                           ghi[:, bass.ds(m, 1), 0:toks].bitcast(F32).rearrange("p a t -> p (a t)"),
                                           ALU.subtract).then_inc(S["g_lo"], 1)
                    chunk_turns(pool, GF, one)

            add_squares(0, T)
            norm_low(0, T)
            ffn_low(0, T)
            add_squares(1, T)
            norm_low(1, T)
            for b in range(2):
                pool.wait_ge(S["ckv_hi_s"], b + 1)
                pool.tensor_tensor(ckv_lo[:, b, :], ckv_raw[:, b, :], ckv_hi[:, b, :].bitcast(F32), ALU.subtract)\
                    .then_inc(S["ckv_lo_s"], 1)

            def lo(ch, n):
                pool.wait_ge(S["hi_ready"], ch.n + 1)
                pool.tensor_tensor(wlo[:, ch.slot, 0:n], wraw[:, ch.slot, 0:n], whi[:, ch.slot, 0:n].bitcast(F32),
                                   ALU.subtract).then_inc(S["lo_ready"], 1)

            pool.wait_ge(S["lo_ready"], B_UKV)
            for m in range(4):
                if m == 0:
                    lo(Chunk(B_UKV), 8 * P)
                if m < 3:
                    lo(Chunk(B_UKV + m + 1), 8 * P)
                for b in range(4 * m, min(4 * m + 4, 6)):
                    pool.wait_ge(S["cq_hi_s"], b + 1)
                    pool.tensor_tensor(cq_lo[:, b, :], cq_raw[:, b, :], cq_hi[:, b, :].bitcast(F32), ALU.subtract)\
                        .then_inc(S["cq_lo_s"], 1)
            for m in range(12):
                lo(Chunk(B_UQ + m), 6 * P)
            lo(Chunk(B_WO), KD * P)
            for h in range(HEADS):
                pool.wait_ge(S["o_hi"], h + 1)
                pool.tensor_tensor(hlo[:, h, 0:NLAT], ot[:, h, :], hhi[:, h, 0:NLAT].bitcast(F32), ALU.subtract)\
                    .then_inc(S["o_lo"], 1)
            add_squares(2, NLAT)
            norm_low(2, NLAT)
            ffn_low(1, NLAT)

        @block.scalar
        def _(act):
            chain = Chain(act, S["act_link"])
            act.wait_ge(S["const_set"], 3)
            act.wait_ge(S["cols_T"], 1)
            act.activation(colsB[:], flat[:, 128:216], ACT.Copy).then_inc(S["cols_out"], 1)
            act.activation(colsA[:], flat[:, 0:128], ACT.Copy).then_inc(S["cols_out"], 1)
            act.activation(colsW[:], flat[:, 256:388], ACT.Copy).then_inc(S["cols_out"], 1)
            act.activation(d16[:], flat[0:CH, 400:464], ACT.Copy).then_inc(S["cols_out"], 1)
            act.wait_ge(S["cols_out"], 4)
            chain.link(act.activation(sgc[:], colsB[:, 0:16], ACT.Sigmoid))
            def ada_row(n, r):
                act.wait_ge(S["ada_used"], n + 1)
                if not (isinstance(n, int) and n < 1):
                    act.wait_ge(S["ada_folded"], n)
                act.activation(ada_rows[:], ps[0:2, 6 * (r % 2), 0:256], ACT.Copy).then_inc(S["row_out"], 1)

            def ada_turn(turn, l=0):
                for r in range(ADA_RING):
                    ada_row(l * ADA_CHUNKS + ADA_RING * turn + r, r)

            def hi(ch, n):
                act.wait_ge(wload[ch.slot], 32 * ch.nth + 32)
                if ch.reuse:
                    act.wait_ge(S["w_used"], ch.free)
                act.activation(whi[:, ch.slot, 0:n], wraw[:, ch.slot, 0:n], ACT.Copy).then_inc(S["hi_ready"], 1)

            act.wait_ge(S["lam_in"], 16 * 3)
            act.activation(ldt[:], ldt[:], ACT.Exp).then_inc(S["dt_set"], 1)
            act.wait_ge(S["disc_a"], 1)
            act.activation(disc[:, 2, :], disc[:, 0, :], ACT.Exp).then_inc(S["exp_done"], 1)
            act.wait_ge(S["disc_b"], 1)
            act.activation(disc[:, 3, :], disc[:, 1, :], ACT.Sin)
            act.activation(disc[:, 4, :], disc[:, 1, :], ACT.Sin, scale=0.5).then_inc(S["sin_done"], 1)
            ada_turn(0)
            ada_turn(1)
            act.wait_ge(S["disc_T"], 1)
            act.activation(acoef[:].rearrange("p q (g d) -> p q d g", d=2),
                           flat[:, 512:768].rearrange("p (q d g) -> p q d g", q=4, d=2), ACT.Copy).then_inc(S["disc_out"], 1)
            for n, (dst, q) in enumerate(((Bc, 0), (Bc, 1), (Cc, 0), (Cc, 1))):
                if n == 2:
                    ada_turn(2)
                for h in range(4):
                    act.wait_ge(S["bc_T"], 4 * n + h + 1)
                    act.activation(dst[:, q, :, 4 * h:4 * h + 4].rearrange("p g c -> p c g"),
                                   ps[:, 2 + h % 4, 0:256].rearrange("p (c g) -> p c g", c=4),
                                   ACT.Copy, scale=-1.0 if n == 3 else 1.0).then_inc(S["bc_out"], 1)
            act.wait_ge(S["bc_out"], 16)
            act.wait_ge(S["disc_out"], 1)
            for dst, src in ((xin[0:JCTX], a["ctx"]), (xin[JCTX:J], a["x"])):
                act.dma_start(dst, src.rearrange("o (j k) d -> (o j) k d", k=CK)).then_inc(S["x_in"], 16)
            ada_turn(3)
            act.wait_ge(S["x_in"], 32)
            for k in range(CK):
                chain.link(act.activation(flat[0:J, 2048:2048 + D], xin[:, k, :], ACT.Square,
                                          accum_out=stat[:, 0, k:k + 1]))
            act.activation(stat[:, 0, :], stat[:, 0, :], ACT.Sqrt, bias=eps[0:J, :], scale=1.0 / D)\
                .then_inc(S["rowsum_done"], 1)
            ada_turn(4)
            ada_turn(5)

            act.wait_ge(S["rep_out"], 1)
            for q in range(1, GROUPS // 4, 2):
                act.wait_ge(S["u_T"], q + 1)
                for g, j0, j1, cond in u_parts(q):
                    last = act.activation(U[:, g, j0:j1], ps[:, q % 4, P * (g % 4) + j0:P * (g % 4) + j1], ACT.Identity,
                                          scale=urep[:, 0, cond, g:g + 1], bias=urep[:, 1, cond, g:g + 1])
                last.then_inc(S["u_act"], 1)

            def s5_block(b, q, n, first, turn):
                act.wait_ge(S["mt_T"], n + 1)
                if not first:
                    act.wait_ge(S["s_done"], n)
                act.activation(MT[:].rearrange("p r g s -> p (r g s)"), flat[:, 0:1024], ACT.Copy).then_inc(S["mt_out"], 1)
                act.wait_ge(S["k_done"], n + 1)
                if turn is not None:
                    act.wait_ge(tt_in[q], 128 * turn)
                act.activation(kernels[q].rearrange("c (g h) t o -> c g h (t o)", h=2)[:, :, :, 7 * CH:],
                               ps[0:CH, 2:4, 0:256].rearrange("c g (h x) -> c g h x", h=2), ACT.Copy).then_inc(S["kf_out"], 1)
                act.wait_ge(S["s_done"], n + 1)
                for h in range(2):
                    rows = slice(STATES * h, STATES * (h + 1))
                    last = act.activation(Sarr[rows, 0, 1:J + 1, :, bass.ds(2 * b, 2)].rearrange("p j r g -> p r g j"),
                                          ps[rows, 4:6, :].rearrange("p r (g x) -> p r g x", g=2)[:, :, :, J * h:J * (h + 1)],
                                          ACT.Copy)
                last.then_inc(S["sf_out"], 1)

            s5_block(0, 0, 0, True, None)
            s5_block(1, 1, 1, False, None)
            with act.Fori(1, GP // 4) as i:
                for q in range(2):
                    s5_block(2 * i + q, q, 2 * i + q, False, i)

            with act.Fori(0, ADA_TURNS) as i:
                ada_turn(i, 1)

            act.wait_ge(S["ada_used"], 2 * ADA_CHUNKS)
            act.wait_ge(S["half_scanned"], 1)
            saved = wraw[:].rearrange("p s n -> p (s n)")[:, 0:J // 2 * 2 * GP].rearrange("p (s x) -> p s x", x=2 * GP)
            back = Sarr[:, 1].rearrange("p s r g -> p s (r g)")
            act.activation(saved, back[:, 0:J // 2], ACT.Copy).then_inc(S["half_saved"], 1)
            act.wait_ge(S["scanned"], 1)
            act.activation(back[:, J - 1:J // 2 - 1:-1], saved, ACT.Copy).then_inc(S["scanned"], 1)

            for b in range(KD):
                act.wait_ge(S["y_done"], 2 * b + 2)
                if b >= 1:
                    act.wait_ge(S["z_T"], 2 * b)
                for h in range(2):
                    last = act.activation(yst.rearrange("j k (h g c) -> j h g k c", h=2, c=CH)[:, h],
                                          ps[0:J, 2 * (b % 2) + h, :].rearrange("j (g k c) -> j g k c", k=CK, c=CH),
                                          ACT.Gelu_apprx_tanh)
                last.then_inc(S["y_out"], 1)
            act.wait_ge(S["y_done"], 2 * KD)
            hi(Chunk(B_GLU), SLOT)
            for b in range(KD):
                act.wait_ge(S["z_out"], 2 * KD)
                act.activation(hhi[:, b, :], U[:].rearrange("p g j -> p (g j)")[:, T * b:T * b + T], ACT.Copy)\
                    .then_inc(S["z_hi"], 1)

            def stage(first, count, n, epi, n_next):
                stage_turns(act, count, lambda c, turn: hi(Chunk(first + c, turn), n),
                            lambda m, c, turn: epi(m, Chunk(first + c, turn), turn is None and c < 2),
                            lambda: n_next and hi(Chunk(first + count), n_next))

            def square_block(j, m, toks, updated, n):
                act.wait_ge(updated, n)
                if not isinstance(m, int) or m >= 2:
                    act.wait_ge(S["sq_added"], SQ_ADDS * j + m - 1)
                act.activation(squares[j][not (isinstance(m, int) and m == 0)][:, 0:toks],
                               xT[:, bass.ds(m, 1), 0:toks].rearrange("p a t -> p (a t)"), ACT.Square).then_inc(S["sq_done"], 1)

            def glu_epi(m, ch, early):
                a_l, g_l, a_c, g_c = glu_psum(ch.slot)
                act.wait_ge(S["w_used"], ch.done)
                if not early:
                    act.wait_ge(S["mix_done"], m - 1)
                bias = colsB[:, bass.ds(C_GLUB + KD + m, 1)]
                act.activation(sig[:, ch.slot, 0:NLAT], g_l, ACT.Sigmoid, bias=bias)
                act.activation(sig[:, ch.slot, NLAT:], g_c, ACT.Sigmoid, bias=bias).then_inc(S["sig_done"], 1)
                if not (isinstance(m, int) and m == 0):
                    square_block(0, m - 1, T, S["mix_done"], m)

            stage(B_GLU, KD, SLOT, glu_epi, SLOT)
            square_block(0, KD - 1, T, S["mix_done"], KD)

            def norm(j, l, q, toks):
                act.wait_ge(S["stat_T"], j + 1)
                act.activation(rstd[:, 0:toks], flat[:, 3072:3072 + toks], ACT.Sqrt, bias=eps[:], scale=1.0 / D)\
                    .then_inc(S["std_done"], 1)
                for b in range(KD):
                    n = KD * j + b + 1
                    act.wait_ge(S["xn_done"], n)
                    for t0, t1, cond in ((0, NLAT, 0), (NLAT, T, 1))[:1 if toks == NLAT else 2]:
                        v = hx[:, b % HX, t0:t1]
                        last = act.activation(v, v, ACT.Identity, scale=gain[:, l, q, b, cond:cond + 1],
                                              bias=modc[:, l, (SH_M, SH_F)[q] + b, cond:cond + 1])
                    last.then_inc(S["hx_done"], 1)
                    act.wait_ge(S["hx_done"], n)
                    act.activation(hhi[:, b, 0:toks], hx[:, b % HX, 0:toks], ACT.Copy).then_inc(S["h_hi"], 1)

            def ffn(l, toks):
                spans = ((0, NLAT), (NLAT, T))[:1 if toks == NLAT else 2]
                for g in range(2):
                    def epi(m, ch, early):
                        f = KF * l + GF * g + m
                        a_l, _, a_c, _ = glu_psum(ch.slot)
                        act.wait_ge(S["w_used"], ch.done)
                        if l or g or not early:
                            act.wait_ge(S["g_lo"], f - 1)
                        for (t0, t1), src in zip(spans, (a_l, a_c)):
                            last = act.activation(acc[:, ch.slot, t0:t1], src, ACT.Identity,
                                                  scale=colsW[:, l, bass.ds(KF + GF * g + m, 1)],
                                                  bias=colsB[:, bass.ds(C_CONVB + KF * l + GF * g + m, 1)])
                        last.then_inc(S["acc_set"], 1)
                        act.wait_ge(S["conv_done"], f + 1)
                        v = acc[:, ch.slot, 0:toks]
                        act.activation(v, v, ACT.Silu).then_inc(S["silu_done"], 1)
                        act.wait_ge(S["drained"], ch.drains)
                        act.activation(ghi[:, bass.ds(m, 1), 0:toks].rearrange("p a t -> p (a t)"), v, ACT.Copy)\
                            .then_inc(S["g_hi"], 1)
                    stage(B_FFN[l] + g * (GF + KD), GF, SLOT, epi, GF * P)
                    def out_epi(m, ch, early):
                        if l == 0 and g == 1:
                            square_block(1, m, T, S["drained"], ch.drains)
                    stage(B_FFN[l] + g * (GF + KD) + GF, KD, GF * P, out_epi, after[l][g])

            norm(0, 0, 1, T)
            ffn(0, T)
            norm(1, 1, 0, T)

            def square(u, src, n):
                if u >= 2:
                    act.wait_ge(S["unit_used"], u - 1)
                act.activation(sqr[:, u % 2, 0:n], src, ACT.Square).then_inc(S["unit_sq"], 1)

            def root(j, n, mean):
                act.wait_ge(S["unit_used"], JOB_UNITS[j])
                if j >= 2:
                    act.wait_ge(S["job_out"], JOB_UNITS[j - 2])
                act.activation(rs[j % 2][:, 0:n], flat[:, 3072:3072 + n], ACT.Sqrt, bias=eps[:], scale=1.0 / mean)\
                    .then_inc(S["job_std"], 1)

            for m in range(3):
                if m < 2:
                    hi(Chunk(B_DKV + m + 1), KD * P)
                else:
                    hi(Chunk(B_DQ), KD * P)
                ch = Chunk(B_DKV + m)
                a_l, _, a_c, _ = glu_psum(ch.slot)
                dst = ckv_raw[:, m, :] if m < 2 else kr[:]
                act.wait_ge(S["w_used"], ch.done)
                act.activation(dst[:, 0:NLAT], a_l, ACT.Copy)
                act.activation(dst[:, NLAT:T], a_c, ACT.Copy).then_inc(S["drained"], 1)
                act.wait_ge(S["drained"], ch.drains)
                square(m, dst, T)
            for m in range(6):
                if m < 5:
                    hi(Chunk(B_DQ + m + 1), KD * P)
                else:
                    hi(Chunk(B_UKV), 8 * P)
                ch = Chunk(B_DQ + m)
                act.wait_ge(S["w_used"], ch.done)
                act.activation(cq_raw[:, m, :], glu_psum(ch.slot)[0], ACT.Copy).then_inc(S["drained"], 1)
                act.wait_ge(S["drained"], ch.drains)
                square(3 + m, cq_raw[:, m, :], NLAT)
                if m == 0:
                    root(0, T, KVR)
                if m == 1:
                    root(1, T, ROPE)
                if m in (2, 3):
                    b = m - 2
                    act.wait_ge(S["job_out"], b + 1)
                    act.activation(ckv_hi[:, b, :], ckv_raw[:, b, :], ACT.Copy).then_inc(S["ckv_hi_s"], 1)
            root(2, NLAT, QR)
            use = used_after(B_UKV - 1)
            for m in range(4):
                if m < 3:
                    hi(Chunk(B_UKV + m + 1), 8 * P)
                for t in range(KV_USES[m]):
                    use += 1
                    a_l, _, a_c, _ = glu_psum((use - 1) % 2)
                    act.wait_ge(S["w_used"], use)
                    if m < 2:
                        h = 4 * m + t
                        act.activation(kn[:, h, 0:NLAT], a_l, ACT.Copy)
                        act.activation(kn[:, h, NLAT:T], a_c, ACT.Copy).then_inc(S["drained"], 1)
                        act.wait_ge(S["drained"], use - B_GLU)
                        square(9 + h, kn[:, h, :], T)
                        if h >= 1:
                            root(3 + h - 1, T, NOPE)
                        if h < 6:
                            act.wait_ge(S["job_out"], JOB_UNITS[1] + h + 1)
                            act.activation(cq_hi[:, h, :], cq_raw[:, h, :], ACT.Copy).then_inc(S["cq_hi_s"], 1)
                    else:
                        act.activation(val[:, t, 512 * (m - 2):512 * (m - 1)], a_l, ACT.Copy).then_inc(S["drained"], 1)
                    if m == 2 and t == 0:
                        root(10, T, NOPE)
            hi(Chunk(B_UQ), 6 * P)
            for m in range(12):
                if m < 11:
                    hi(Chunk(B_UQ + m + 1), 6 * P)
                else:
                    hi(Chunk(B_WO), KD * P)
                ch = Chunk(B_UQ + m)
                act.wait_ge(S["w_used"], ch.done)
                act.activation(q_block(m), glu_psum(ch.slot)[0], ACT.Copy).then_inc(S["drained"], 1)
                act.wait_ge(S["drained"], ch.drains)
                square(17 + m, q_block(m), NLAT)
                if m >= 1:
                    root(11 + m - 1, NLAT, ROPE if m - 1 < ROPE_PAIRS else NOPE)
            root(22, NLAT, NOPE)

            def exps(i):
                act.wait_ge(S["mx_set"], i + 1)
                if i >= 2:
                    act.wait_ge(S["p_T"], i - 1)
                act.activation(pr[:, i % 2, :], flat[:, 1024 * (i % 2):1024 * (i % 2) + T], ACT.Exp,
                               bias=smax[:, i % 2, 1:2], scale=SCALE, accum_out=smax[:, i % 2, 2:3]).then_inc(S["ex_done"], 1)

            exps(0)
            for i in range(4 * HEADS):
                if i + 1 < 4 * HEADS:
                    exps(i + 1)
                h, t = i // 4, i % 4
                act.wait_ge(S["p_T"], i + 1)
                if h >= 2 and t == 0:
                    act.wait_ge(S["pv_done"], h - 1)
                act.activation(pT[:, h % 2, :, P * t:P * (t + 1)], flat[:, 2048:2048 + T].rearrange("p (b q) -> p b q", b=6),
                               ACT.Copy).then_inc(S["pT_out"], 1)
            for h in range(HEADS):
                act.wait_ge(S["ot_out"], HEADS)
                act.activation(hhi[:, h, 0:NLAT], ot[:, h, :], ACT.Copy).then_inc(S["o_hi"], 1)
            for m in range(KD):
                hi(Chunk(B_WO + m + 1), KD * P if m < KD - 1 else SLOT)
                square_block(2, m, NLAT, S["drained"], Chunk(B_WO + m).drains)
            norm(2, 1, 1, NLAT)
            ffn(1, NLAT)

            for t in range(4):
                act.wait_ge(S["fin_out"], 2 * t + 2)
                act.dma_start(a["out"].rearrange("o (t p) d -> t p (o d)", p=P)[t], hhi_out(t)).then_inc(S["out_done"], 16)

        @block.vector
        def _(dve):
            chain = Chain(dve, S["dve_link"])
            dve.memset(ones[:], 1.0).then_inc(S["const_set"], 1)
            dve.memset(eps[:], EPS).then_inc(S["const_set"], 1)
            dve.memset(zero[:], 0.0).then_inc(S["const_set"], 1)
            dve.wait_ge(S["act_link"], 1)
            dve.tensor_tensor(silu_c[:].rearrange("p k w -> p w k"), colsB[:, 0:16].rearrange("p (w k) -> p w k", w=2),
                              sgc[:].rearrange("p (w k) -> p w k", w=2), ALU.mult).then_inc(S["cond_ready"], 1)

            lr, li = lam[:, 0, :], lam[:, 1, :]
            d_ = [disc[:, n, :] for n in range(12)]
            dve.wait_ge(S["dt_set"], 1)
            dtb = ldt[:].unsqueeze(2).to_broadcast([DG, 2, STATES])

            def hs(ap):
                return ap.rearrange("p (h s) -> p h s", h=2)

            dve.tensor_tensor(hs(d_[0]), hs(lr), dtb, ALU.mult).then_inc(S["disc_a"], 1)
            chain.link(dve.tensor_tensor(hs(d_[5]), hs(li), dtb, ALU.mult))
            chain.link(dve.tensor_scalar(d_[6], d_[5], 1.0 / (TWO_PI_HI + TWO_PI_LO), ROUND, ALU.mult, ALU.add))
            chain.link(dve.tensor_scalar(d_[6], d_[6], ROUND, None, ALU.subtract))
            chain.link(dve.scalar_tensor_tensor(d_[5], d_[6], -TWO_PI_HI, d_[5], ALU.mult, ALU.add))
            chain.link(dve.scalar_tensor_tensor(d_[5], d_[6], -TWO_PI_LO, d_[5], ALU.mult, ALU.add))
            dve.tensor_scalar(d_[1], d_[5], PI, -PI, ALU.min, ALU.max).then_inc(S["disc_b"], 1)
            chain.link(dve.tensor_tensor(d_[7], lr, lr, ALU.mult))
            chain.link(dve.tensor_tensor(d_[8], li, li, ALU.mult))
            chain.link(dve.tensor_tensor(d_[7], d_[7], d_[8], ALU.add))
            chain.link(dve.reciprocal(d_[7], d_[7]))

            dve.wait_ge(S["sin_done"], 1)
            dve.wait_ge(S["exp_done"], 1)
            chain.link(dve.tensor_tensor(d_[4], d_[4], d_[4], ALU.mult))
            chain.link(dve.tensor_scalar(d_[4], d_[4], -2.0, 1.0, ALU.mult, ALU.add))
            chain.link(dve.tensor_tensor(d_[8], d_[2], d_[4], ALU.mult))
            chain.link(dve.tensor_tensor(d_[9], d_[2], d_[3], ALU.mult))
            chain.link(dve.tensor_scalar(d_[5], d_[8], 1.0, None, ALU.subtract))
            chain.link(dve.tensor_tensor(d_[0], d_[5], lr, ALU.mult))
            chain.link(dve.tensor_tensor(d_[1], d_[9], li, ALU.mult))
            chain.link(dve.tensor_tensor(d_[0], d_[0], d_[1], ALU.add))
            chain.link(dve.tensor_tensor(d_[10], d_[0], d_[7], ALU.mult))
            chain.link(dve.tensor_tensor(d_[0], d_[9], lr, ALU.mult))
            chain.link(dve.tensor_tensor(d_[1], d_[5], li, ALU.mult))
            chain.link(dve.tensor_tensor(d_[0], d_[0], d_[1], ALU.subtract))
            dve.tensor_tensor(d_[11], d_[0], d_[7], ALU.mult).then_inc(S["disc_b"], 1)

            def cmul(o, x, y, n):
                t = [cm[:, q, :, 0:n] for q in range(2)]
                dve.tensor_tensor(t[0], x[0], y[0], ALU.mult)
                chain.link(dve.tensor_tensor(t[1], x[1], y[1], ALU.mult))
                chain.link(dve.tensor_tensor(o[0], t[0], t[1], ALU.subtract))
                dve.tensor_tensor(t[0], x[0], y[1], ALU.mult)
                chain.link(dve.tensor_tensor(t[1], x[1], y[0], ALU.mult))
                chain.link(dve.tensor_tensor(o[1], t[0], t[1], ALU.add))

            def pows(e0, e1):
                return [pw[:, q, :, e0:e1] for q in range(2)]

            def one(e, n):
                return [pw[:, q, :, e:e + 1].to_broadcast([P, DG, n]) for q in range(2)]

            dve.wait_ge(S["disc_out"], 1)
            dve.memset(pw[:, 0, :, 0], 1.0)
            chain.link(dve.memset(pw[:, 1, :, 0], 0.0))
            for q in range(2):
                chain.link(dve.tensor_copy(pw[:, q, :, 1], acoef[:, q, :]))
            cmul(pows(2, 3), pows(1, 2), pows(1, 2), 1)
            cmul(pows(3, 5), pows(1, 3), one(2, 2), 2)
            cmul(pows(5, 9), pows(1, 5), one(4, 4), 4)

            def by(t, q, dirn):
                return t[:, q].rearrange("p (g d) k -> p g d k", d=2)[:, :, dirn]

            f = [acoef[:, 2 + q, :].unsqueeze(2).to_broadcast([P, DG, CK]) for q in range(2)]
            cmul([Pn[:, q] for q in range(2)], pows(0, 8), f, 8)
            for q in range(2):
                dve.tensor_copy(by(Qk, q, 0), by(Pn, q, 0)[:, :, ::-1])
                chain.link(dve.tensor_copy(by(Qk, q, 1), by(Pn, q, 1)))
                dve.tensor_copy(by(Pk, q, 0), by(pw, q, 0)[:, :, 0:8])
                chain.link(dve.tensor_copy(by(Pk, q, 1), by(pw, q, 1)[:, :, 7::-1]))
                dve.tensor_copy(by(Pn, q, 0), by(pw, q, 0)[:, :, 1:9])
                chain.link(dve.tensor_copy(by(Pn, q, 1), by(pw, q, 1)[:, :, 8:0:-1]))
            for dirn in range(2):
                p8 = [by(pw, q, dirn)[:, :, 8] for q in range(2)]
                dve.tensor_copy(a8[:, dirn, 0, 0], p8[0])
                dve.tensor_copy(a8[:, dirn, 0, 1], p8[0])
                dve.tensor_copy(a8[:, dirn, 1, 0], p8[1])
                chain.link(dve.tensor_scalar(a8[:, dirn, 1, 1], p8[1], -1.0, None, ALU.mult))
            dve.wait_ge(S["cols_out"], 4)
            dve.tensor_tensor(kd[:], ident[0:CH, 0:CH].unsqueeze(1).to_broadcast([CH, GROUPS, CH]),
                              d16[:].unsqueeze(2).to_broadcast([CH, GROUPS, CH]), ALU.mult).then_inc(S["tab_set"], 1)
            dve.wait_ge(S["rowsum_done"], 1)
            chain.link(dve.reciprocal(stat[:, 1, :], stat[:, 0, :]))
            for k in range(CK):
                last = dve.tensor_scalar(xn[:, :, k, :], xin[:, k, :].rearrange("j (g c) -> j g c", c=CH), stat[:, 1, k:k + 1], None, ALU.mult)
            last.then_inc(S["rstd_set"], 1)

            def lo(ch, n):
                dve.wait_ge(S["hi_ready"], ch.n + 1)
                dve.tensor_tensor(wlo[:, ch.slot, 0:n], wraw[:, ch.slot, 0:n], whi[:, ch.slot, 0:n].bitcast(F32),
                                  ALU.subtract).then_inc(S["lo_ready"], 1)

            def ada_columns(l):
                dve.wait_ge(S["ada_folded"], (l + 1) * ADA_CHUNKS)
                bias = colsA[:, C_ADAB + 48 * l:C_ADAB + 48 * (l + 1)].unsqueeze(2).to_broadcast([P, 48, 2])
                chain.link(dve.tensor_tensor(modc[:, l], ps[:, 7, 0:96].rearrange("p (b w) -> p b w", w=2), bias, ALU.add))
                for q, (at, scale) in enumerate(((C_NMIX, SC_M), (C_NFFN, SC_F))):
                    g = colsA[:, at + KD * l:at + KD * (l + 1)].unsqueeze(2).to_broadcast([P, KD, 2])
                    last = dve.scalar_tensor_tensor(gain[:, l, q], modc[:, l, scale:scale + KD, :], 1.0, g, ALU.add, ALU.mult)
                last.then_inc(S["ada0_set"], 1)

            ada_columns(0)

            def m_block(b, q, n):
                dg = bass.ds(4 * b, 4)
                if n is not None:
                    dve.wait_ge(S["k_done"], n)
                q_re, q_im = (Qk[:, r, dg, :].unsqueeze(3).to_broadcast([P, 4, CK, CH]) for r in range(2))
                b_re, b_im = (Bc[:, r, dg, :].unsqueeze(2).to_broadcast([P, 4, CK, CH]) for r in range(2))
                dst = [Mr[:, q, r].rearrange("p g (k c) -> p g k c", k=CK) for r in range(2)]
                dve.tensor_tensor(tD[:, 0], q_re, b_re, ALU.mult)
                chain.link(dve.tensor_tensor(tD[:, 1], q_im, b_im, ALU.mult))
                chain.link(dve.tensor_tensor(dst[0], tD[:, 0], tD[:, 1], ALU.subtract))
                dve.tensor_tensor(tD[:, 0], q_re, b_im, ALU.mult)
                chain.link(dve.tensor_tensor(tD[:, 1], q_im, b_re, ALU.mult))
                dve.tensor_tensor(dst[1], tD[:, 0], tD[:, 1], ALU.add).then_inc(S["m_ready"], 1)

            def n_imag(q, n):
                dve.wait_ge(S["n_prod"], n + 1)
                t_im = tN[:, 1].rearrange("p g (k c) -> p g k c", k=CK)
                for h in range(2):
                    rows, dst = own_columns(N_loop, q, 1, h)
                    last = dve.tensor_tensor(dst, t_im[rows], tP[rows, 1], ALU.subtract)
                last.then_inc(S["n_im"], 1)

            m_block(0, 0, None)
            dve.wait_ge(S["m_ready"], 1)
            n_imag(0, 0)

            dve.wait_ge(S["rep_done"], 1)
            for v in range(2):
                for c in range(2):
                    last = dve.tensor_copy(urep[:, v, c].rearrange("p (b g) -> p g b", b=KD),
                                           ps[:, 6, 0:256].rearrange("p (g v b c) -> p g v b c", v=2, b=KD, c=2)[:, :, v, :, c])
            last.then_inc(S["rep_out"], 1)
            dve.wait_ge(S["rep_out"], 1)
            for q in range(GROUPS // 4):
                if q % 2 == 0:
                    dve.wait_ge(S["u_T"], q + 1)
                    for g, j0, j1, cond in u_parts(q):
                        last = dve.tensor_scalar(U[:, g, j0:j1], ps[:, q % 4, P * (g % 4) + j0:P * (g % 4) + j1],
                                                 urep[:, 0, cond, g:g + 1], urep[:, 1, cond, g:g + 1], ALU.mult, ALU.add)
                    last.then_inc(S["u_dve"], 1)

            def evac_block(b, q, n):
                dve.wait_ge(S["kf_out"], n + 1)
                back = ps[0:CH, 2:4, 256:512].rearrange("c g (h x) -> c g h x", h=2)
                ke = kernels[q].rearrange("c (g h) t o -> c g h (t o)", h=2)
                dve.tensor_copy(ke[:, :, :, 0:7 * CH], back[:, :, :, 0:7 * CH])
                mid = ke[:, :, :, 7 * CH:8 * CH]
                chain.link(dve.tensor_tensor(mid, mid, back[:, :, :, 7 * CH:], ALU.add))
                midg = kernels[q][:, :, 7, :]
                dve.tensor_tensor(midg, midg, kd[:, bass.ds(4 * b, 4), :], ALU.add).then_inc(S["kext_ready"], 1)
                dve.wait_ge(S["s_done"], n + 1)
                for h in range(2):
                    rows = slice(STATES * h, STATES * (h + 1))
                    last = dve.tensor_copy(Sarr[rows, 1, 1:J + 1, :, bass.ds(2 * b, 2)].rearrange("p j r g -> p r g j"),
                                           ps[rows, 6:8, :].rearrange("p r (g x) -> p r g x", g=2)[:, :, :, J * h:J * (h + 1)][:, :, :, ::-1])
                last.then_inc(S["sb_out"], 1)

            dve.wait_ge(S["u_T"], GROUPS // 4)
            dve.memset(Sarr[:, 0, 0], 0.0).then_inc(S["s_zero"], 1)
            m_block(1, 1, None)
            n_imag(1, 1)
            evac_block(0, 0, 0)
            dve.wait_ge(S["m_ready"], 2)
            with dve.Fori(1, GP // 4) as i:
                chain.enter(i - 1, 8)
                for q in range(2):
                    m_block(2 * i + q, q, 2 * i + q - 1)
                    n_imag(q, 2 * i + q)
                    dve.wait_ge(S["m_ready"], 2 * i + q + 1)
                    evac_block(2 * i + q - 1, 1 - q, 2 * i + q - 1)
            chain.leave(GP // 4 - 1)
            evac_block(GP // 2 - 1, 1, GP // 2 - 1)

            slots = Sarr[:].rearrange("p d s r g -> p (d s) (r g)")

            def steps(at, hop, count, unroll):
                def step(window, u):
                    h, x = (window[:, u + e:u + e + hop + 1:hop] for e in (0, 1))
                    chain.link(dve.tensor_tensor(sc[:, :, 0:2].rearrange("p d f r g -> p d f (r g)"),
                                                 a8[:].rearrange("p d f r g -> p d f (r g)"),
                                                 h.unsqueeze(2).to_broadcast([P, 2, 2, 2 * GP]), ALU.mult))
                    chain.link(dve.tensor_tensor(sc[:, :, 2].rearrange("p d r g -> p d (r g)"),
                                                 sc[:, :, 0].rearrange("p d r g -> p d (r g)"), x, ALU.add))
                    chain.link(dve.tensor_tensor(x.rearrange("p d (r g) -> p d r g", r=2), sc[:, :, 2], sc[:, :, 1, ::-1],
                                                 ALU.add))

                with dve.Fori(0, count // unroll) as i:
                    chain.enter(i, 3 * unroll)
                    window = slots[:, bass.ds(unroll * i + (at - 1), hop + unroll + 1)]
                    for u in range(unroll):
                        step(window, u)
                chain.leave(count // unroll)
                for u in range(count // unroll * unroll, count):
                    step(slots, at - 1 + u)

            dve.wait_ge(S["sf_out"], GP // 2)
            dve.wait_ge(S["sb_out"], GP // 2)
            steps(2, CTX_HOP, JCTX - 1, 6)
            chain.link(dve.tensor_copy(Sarr[:, 1, 0], Sarr[:, 1, J]))
            steps(JCTX + 1, LAT_HOP, J // 2, 12)
            dve.memset(Sarr[:, 1, JLAT], 0.0).then_inc(S["half_scanned"], 1)
            steps(JCTX + 1 + J // 2, LAT_HOP, JLAT - 1 - J // 2, 12)
            dve.wait_ge(S["half_scanned"], 1)
            dve.wait_ge(S["half_saved"], 1)
            dve.tensor_copy(Sarr[:, 1, J // 2 - 1::-1], Sarr[:, 1, J // 2:J]).then_inc(S["scanned"], 1)
            ada_columns(1)
            dve.wait_ge(S["k_done"], GP // 2)

            for q in range(2):
                dve.wait_ge(tt_in[q], 128 * (GP // 4))
            def z_evac(b):
                for h in range(2):
                    dve.wait_ge(S["z_T"], 2 * b + h + 1)
                    src = ps[:, 4 + 2 * (b % 2) + h, :].rearrange("p (k j) -> p k j", k=4)
                    dst = U[:].rearrange("p g j -> p (g j)")[:, T * b:T * b + T]
                    dve.tensor_copy(dst[:, 0:NLAT].rearrange("p (j k) -> p k j", k=CK)[:, 4 * h:4 * h + 4], src[:, :, JCTX:J])
                    dve.tensor_copy(dst[:, NLAT:T].rearrange("p (j k) -> p k j", k=CK)[:, 4 * h:4 * h + 4], src[:, :, 0:JCTX])\
                        .then_inc(S["z_out"], 1)

            for hb in range(GP // 2):
                dg = slice(4 * hb, 4 * hb + 4)
                p_re, p_im = (Pn[:, r, dg, :].unsqueeze(3).to_broadcast([P, 4, CK, CH]) for r in range(2))
                c_re, c_ni = (Cc[:, r, dg, :].unsqueeze(2).to_broadcast([P, 4, CK, CH]) for r in range(2))
                if hb >= 2:
                    dve.wait_ge(S["y_done"], hb - 1)
                dve.tensor_tensor(tD[:, 0], p_re, c_re, ALU.mult)
                chain.link(dve.tensor_tensor(tD[:, 1], p_im, c_ni, ALU.mult))
                for h in range(2):
                    rows, dst = own_columns(N_out, hb % 2, 0, h)
                    last = dve.tensor_tensor(dst, tD[rows, 0], tD[rows, 1], ALU.add)
                last.then_inc(S["n2_re"], 1)
                dve.wait_ge(S["n2_re"], hb + 1)
                if hb % 2 and hb >= 5:
                    z_evac((hb - 5) // 2)
            z_evac(KD - 2)
            z_evac(KD - 1)
            lo(Chunk(B_GLU), SLOT)
            for b in range(KD):
                for h in range(2):
                    dve.wait_ge(S["xT_T"], 2 * b + h + 1)
                    src = ps[:, 4 + 2 * (b % 2) + h, :].rearrange("p (k j) -> p k j", k=4)
                    dst = xT[:, b, :]
                    dve.tensor_copy(dst[:, 0:NLAT].rearrange("p (j k) -> p k j", k=CK)[:, 4 * h:4 * h + 4], src[:, :, JCTX:J])
                    dve.tensor_copy(dst[:, NLAT:T].rearrange("p (j k) -> p k j", k=CK)[:, 4 * h:4 * h + 4], src[:, :, 0:JCTX])\
                        .then_inc(S["xT_out"], 1)
            dve.wait_ge(S["xT_out"], 2 * KD)

            def stage(first, count, n, epi, n_next):
                stage_turns(dve, count, lambda c, turn: lo(Chunk(first + c, turn), n),
                            lambda m, c, turn: epi(m, Chunk(first + c, turn), turn is None and c < 2),
                            lambda: n_next and lo(Chunk(first + count), n_next))

            def glu_epi(m, ch, early):
                a_l, _, a_c, _ = glu_psum(ch.slot)
                dve.wait_ge(S["sig_done"], ch.n - B_GLU + 1)
                bias = colsB[:, bass.ds(C_GLUB + m, 1)]
                for v, pa, cond in ((slice(0, NLAT), a_l, 0), (slice(NLAT, T), a_c, 1)):
                    s_ = sig[:, ch.slot, v]
                    last = dve.scalar_tensor_tensor(s_, pa, bias, s_, ALU.add, ALU.mult)
                last.then_inc(S["drained"], 1)
                dve.wait_ge(S["drained"], ch.n - B_GLU + 1)
                for v, cond in ((slice(0, NLAT), 0), (slice(NLAT, T), 1)):
                    xv = xT[:, bass.ds(m, 1), v].rearrange("p a t -> p (a t)")
                    g = modc[:, 0, bass.ds(G_M + m, 1), cond]
                    last = dve.scalar_tensor_tensor(xv, sig[:, ch.slot, v], g, xv, ALU.mult, ALU.add)
                last.then_inc(S["mix_done"], 1)

            stage(B_GLU, KD, SLOT, glu_epi, SLOT)

            def norm(j, toks):
                dve.wait_ge(S["std_done"], j + 1)
                chain.link(dve.reciprocal(rstd[:, 0:toks], rstd[:, 0:toks]))
                for b in range(KD):
                    if b >= HX:
                        dve.wait_ge(S["h_lo"], KD * j + b + 1 - HX)
                    dve.tensor_tensor(hx[:, b % HX, 0:toks], xT[:, b, 0:toks], rstd[:, 0:toks], ALU.mult)\
                        .then_inc(S["xn_done"], 1)

            def out_epi(l, at, toks):
                def epi(m, ch, early):
                    a_l, _, a_c, _ = glu_psum(ch.slot)
                    dve.wait_ge(S["w_used"], ch.done)
                    for (t0, t1), src, cond in (((0, NLAT), a_l, 0), ((NLAT, T), a_c, 1))[:1 if toks == NLAT else 2]:
                        xv = xT[:, bass.ds(m, 1), t0:t1].rearrange("p a t -> p (a t)")
                        last = dve.scalar_tensor_tensor(xv, src, modc[:, l, bass.ds(at + m, 1), cond], xv, ALU.mult, ALU.add)
                    last.then_inc(S["drained"], 1)
                return epi

            def ffn(l, toks):
                spans = ((0, NLAT), (NLAT, T))[:1 if toks == NLAT else 2]
                for g in range(2):
                    def epi(m, ch, early):
                        f = KF * l + GF * g + m
                        a_l, b_l, a_c, b_c = glu_psum(ch.slot)
                        dve.wait_ge(S["acc_set"], f + 1)
                        v = acc[:, ch.slot]
                        w = colsW[:, l]
                        for (t0, t1), src in zip(spans, (a_l, a_c)):
                            n = t1 - t0
                            op = dve.scalar_tensor_tensor(v[:, t0 + 1:t1], src[:, 0:n - 1], w[:, bass.ds(GF * g + m, 1)],
                                                          v[:, t0 + 1:t1], ALU.mult, ALU.add)
                        chain.link(op)
                        for (t0, t1), src in zip(spans, (a_l, a_c)):
                            n = t1 - t0
                            op = dve.scalar_tensor_tensor(v[:, t0:t1 - 1], src[:, 1:n], w[:, bass.ds(2 * KF + GF * g + m, 1)],
                                                          v[:, t0:t1 - 1], ALU.mult, ALU.add)
                        op.then_inc(S["conv_done"], 1)
                        dve.wait_ge(S["silu_done"], f + 1)
                        for (t0, t1), src in zip(spans, (b_l, b_c)):
                            op = dve.tensor_tensor(v[:, t0:t1], v[:, t0:t1], src, ALU.mult)
                        op.then_inc(S["drained"], 1)
                    first = B_FFN[l] + g * (GF + KD)
                    pairs = (GF - 3) // 2
                    def turned(m, c, turn):
                        if turn is not None and c == 0:
                            chain.enter(turn - 1, 2)
                        epi(m, Chunk(first + c, turn), turn is None and c < 2)
                        if turn is not None and c == 1:
                            chain.leave(pairs)
                    stage_turns(dve, GF, lambda c, turn: lo(Chunk(first + c, turn), SLOT), turned,
                                lambda: lo(Chunk(first + GF), GF * P))
                    stage(first + GF, KD, GF * P, out_epi(l, G_F, toks), after[l][g])

            norm(0, T)
            ffn(0, T)
            norm(1, T)

            def job(j, n, views, gains):
                dve.wait_ge(S["job_std"], j + 1)
                chain.link(dve.reciprocal(rs[j % 2][:, 0:n], rs[j % 2][:, 0:n]))
                for v, g in zip(views, gains):
                    op = dve.scalar_tensor_tensor(v, v, colsB[:, g:g + 1], rs[j % 2][:, 0:n], ALU.mult, ALU.mult)
                    op.then_inc(S["job_out"], 1)

            def rotate(n):
                v = rotated[n]
                t = pr[:, 0, 0:NLAT]
                dve.wait_ge(S["swap_T"], n + 1)
                dve.tensor_tensor(v, v, rope_cs[:, 0], ALU.mult)
                chain.link(dve.tensor_tensor(t, ps[:, SWAP_BANKS[n % 2], :], rope_cs[:, 1], ALU.mult))
                dve.tensor_tensor(v, v, t, ALU.add).then_inc(S["rot_done"], 1)
                dve.wait_ge(S["rot_done"], n + 1)

            lo(Chunk(B_DKV + 1), KD * P)
            lo(Chunk(B_DKV + 2), KD * P)
            for m in range(6):
                lo(Chunk(B_DQ + m), KD * P)
                if m == 1:
                    job(0, T, [ckv_raw[:, b, :] for b in range(2)], (C_GKV, C_GKV + 1))
                if m == 2:
                    job(1, T, [kr[:]], (C_GKR,))
            job(2, NLAT, [cq_raw[:, b, :] for b in range(6)], range(C_GQ, C_GQ + 6))
            for h in range(HEADS):
                job(3 + h, T, [kn[:, h, :]], (C_GKN,))
            for m in range(12):
                if m >= 1:
                    job(11 + m - 1, NLAT, [q_block(m - 1)], (C_GQR if m - 1 < ROPE_PAIRS else C_GQN,))
                if m == 2:
                    dve.wait_ge(S["rope_in"], 16)
                    dve.wait_ge(S["w_used"], used_after(B_UQ - 1))
                    rotate(0)
                if 4 <= m < 4 + ROPE_PAIRS:
                    rotate(m - 3)
            job(22, NLAT, [q_block(11)], (C_GQN,))

            def maxes(i):
                dve.wait_ge(S["sc_done"], i + 1)
                if i >= 2:
                    dve.wait_ge(S["pr_set"], i - 1)
                chain.link(dve.reduce_max(smax[:, i % 2, 0:1], flat[:, 1024 * (i % 2):1024 * (i % 2) + T], AX.X))
                dve.tensor_scalar(smax[:, i % 2, 1:2], smax[:, i % 2, 0:1], -SCALE, None, ALU.mult).then_inc(S["mx_set"], 1)

            maxes(0)
            for i in range(4 * HEADS):
                dve.wait_ge(S["ex_done"], i + 1)
                chain.link(dve.reciprocal(smax[:, i % 2, 3:4], smax[:, i % 2, 2:3]))
                dve.tensor_scalar(pr[:, i % 2, :], pr[:, i % 2, :], smax[:, i % 2, 3:4], None, ALU.mult)\
                    .then_inc(S["pr_set"], 1)
                if i + 1 < 4 * HEADS:
                    maxes(i + 1)
                if i % 4 == 1 and i > 4:
                    h = i // 4 - 1
                    dve.wait_ge(S["pv_done"], h + 1)
                    dve.tensor_copy(ot[:, h, :], ps[:, 6 + h % 2, :]).then_inc(S["ot_out"], 1)
            dve.wait_ge(S["pv_done"], HEADS)
            dve.tensor_copy(ot[:, HEADS - 1, :], ps[:, 7, :]).then_inc(S["ot_out"], 1)
            dve.wait_ge(S["lo_ready"], B_WO + 1)
            for m in range(KD):
                lo(Chunk(B_WO + m + 1), KD * P if m < KD - 1 else SLOT)
                out_epi(1, G_M, NLAT)(m, Chunk(B_WO + m), False)
            norm(2, NLAT)
            ffn(1, NLAT)

            for t in range(4):
                for h in range(2):
                    dve.wait_ge(S["fin_T"], 2 * t + h + 1)
                    dve.tensor_copy(hhi_out(t)[:, 512 * h:512 * h + 512], ps[:, (2 * t + h) % 4, :]).then_inc(S["fin_out"], 1)

        @block.tensor
        def _(pe):
            pe.wait_ge(S["params_in"], 16 * 21)
            pe.transpose(flat[0:CH, 400:464], drow[:], ident[0:GROUPS, 0:GROUPS])
            pe.transpose(flat[:, 128:216], rowsB[:], ident[0:88, 0:88])
            pe.transpose(flat[:, 0:128], rowsA[:], ident[:])
            for l in range(2):
                last = pe.transpose(flat[:, 256 + 66 * l:322 + 66 * l], rowsW[:, l, :], ident[0:66, 0:66])
            last.then_inc(S["cols_T"], 1)
            pe.wait_ge(S["cond_ready"], 1)

            def ada_fold(l, n, col):
                pe.wait_ge(S["row_out"], n + 1)
                for b in range(2):
                    last = pe.matmul(ps[:, 7, bass.ds(col + 2 * b, 2)], ada_rows[:, b * P:(b + 1) * P], ident[0:2, 0:2],
                                     start=True, stop=True)
                last.then_inc(S["ada_folded"], 1)

            def ada_chunk(l, r, turn):
                m = ADA_RING * turn + r
                n = l * ADA_CHUNKS + m
                if not (isinstance(n, int) and n < 2):
                    pe.wait_ge(S["row_out"], n - 1)
                pe.wait_ge(ada_in[r], 16 * turn + 16 * (l * ADA_TURNS + 1))
                for k in range(KD):
                    last = pe.matmul(ps[0:2, 6 * (r % 2), 0:256], silu_c[:, k, :], ada_raw[l][r][:, 256 * k:256 * (k + 1)],
                                     start=k == 0, stop=k == KD - 1)
                last.then_inc(S["ada_used"], 1)
                if not (isinstance(m, int) and m == 0):
                    ada_fold(l, n - 1, 4 * (m - 1))

            def ada_turn(turn):
                for r in range(ADA_RING):
                    ada_chunk(0, r, turn)

            ada_turn(0)
            ada_turn(1)
            pe.wait_ge(S["disc_b"], 2)
            for q in range(4):
                last = pe.transpose(flat[:, 512 + DG * q:512 + DG * (q + 1)], disc[:, 8 + q, :], ident[0:DG, 0:DG])
            last.then_inc(S["disc_T"], 1)
            for n, (src, q, eq) in enumerate(((brow, 0, "p (h s c) -> p c h s"), (brow, 1, "p (h s c) -> p c h s"),
                                              (crow, 0, "p (c h s) -> p c h s"), (crow, 1, "p (c h s) -> p c h s"))):
                v = src[:, q, :].rearrange(eq, h=2, c=CH)
                perm = ident[0:DG, 0:DG].rearrange("p (d g) -> p g d", d=2)
                if n == 0:
                    pe.wait_ge(S["s5rows_in"], 16 * 6)
                if n == 2:
                    ada_turn(2)
                for h in range(4):
                    if n >= 1:
                        pe.wait_ge(S["bc_out"], 4 * (n - 1) + h + 1)
                    for c in range(4):
                        last = pe.matmul(ps[:, 2 + h, DG * c:DG * (c + 1)], v[:, 4 * h + c].rearrange("p h s -> p (h s)"), perm, start=True, stop=True)
                    last.then_inc(S["bc_T"], 1)

            for turn in range(3, ADA_TURNS):
                ada_turn(turn)
            ada_fold(0, ADA_CHUNKS - 1, 4 * (ADA_CHUNKS - 1))

            pe.wait_ge(S["ada0_set"], 1)
            pe.wait_ge(S["tabs_in"], 1)
            for g in range(KD):
                for v, rhs in enumerate((gain[:, 0, 0], modc[:, 0, SH_M:SH_M + KD, :])):
                    at = 32 * g + 16 * v
                    last = pe.matmul(ps[:, 6, at:at + 16], pick[:, g].rearrange("p k c -> p (k c)"),
                                     rhs.rearrange("p b c -> p (b c)"), start=True, stop=True)
            last.then_inc(S["rep_done"], 1)
            pe.wait_ge(S["rstd_set"], 1)
            for q in range(GROUPS // 4):
                if q >= 4:
                    pe.wait_ge(S["u_act" if q % 2 else "u_dve"], q // 2 - 1)
                for r in range(4):
                    g = 4 * q + r
                    last = pe.transpose(ps[:, q % 4, P * r:P * r + J], xn[:, g].rearrange("j k c -> j (k c)"), ident[0:J, 0:J])
                last.then_inc(S["u_T"], 1)

            def s5_block(b, q, n, first):
                pe.wait_ge(S["m_ready"], n + 1)
                pe.wait_ge(S["n_ready"], n + 1)
                pe.wait_ge(S["n_im"], n + 1)
                if not first:
                    pe.wait_ge(S["kext_ready"], n)
                if first:
                    pe.wait_ge(S["u_dve"], GROUPS // 8)
                    pe.wait_ge(S["u_act"], GROUPS // 8)
                else:
                    pe.wait_ge(S["mt_out"], n)
                for r in range(2):
                    for g in range(4):
                        last = pe.transpose(ps[:, r, P * g:P * (g + 1)], Mr[:, q, r, g, :], ident[:])
                last.then_inc(S["mt_T"], 1)
                for g in range(2):
                    for dirn in range(2):
                        k0 = CK - 1 if dirn == 0 else 0
                        for r in range(2):
                            last = pe.matmul(ps[0:CH, 2 + g, 256 * dirn:256 * (dirn + 1)],
                                             Mr[:, q, r, 2 * g + dirn, CH * k0:CH * (k0 + 1)],
                                             N_loop[:, q, r, 2 * g + dirn].rearrange("p h x -> p (h x)"),
                                             start=r == 0, stop=r == 1)
                last.then_inc(S["k_done"], 1)
                pe.wait_ge(S["mt_out"], n + 1)
                if not first:
                    pe.wait_ge(S["sf_out"], n)
                    pe.wait_ge(S["sb_out"], n)
                for dirn in range(2):
                    for r in range(2):
                        for g in range(2):
                            last = pe.matmul(ps[:, 4 + 2 * dirn + r, 256 * g:256 * g + 2 * J], MT[:, r, 2 * g + dirn, :],
                                             U[:, bass.ds(4 * b + 2 * g, 2), :].rearrange("p a j -> p (a j)"),
                                             start=True, stop=True)
                last.then_inc(S["s_done"], 1)

            s5_block(0, 0, 0, True)
            s5_block(1, 1, 1, False)
            with pe.Fori(1, GP // 4) as i:
                for q in range(2):
                    s5_block(2 * i + q, q, 2 * i + q, False)

            pe.wait_ge(S["sf_out"], GP // 2)
            pe.wait_ge(S["sb_out"], GP // 2)
            for r in range(ADA_RING):
                ada_chunk(1, r, 0)
            with pe.Fori(1, ADA_TURNS) as i:
                for r in range(ADA_RING):
                    ada_chunk(1, r, i)
            ada_fold(1, 2 * ADA_CHUNKS - 1, 4 * (ADA_CHUNKS - 1))

            for q in range(2):
                pe.wait_ge(tt_in[q], 128 * (GP // 4))
            pe.wait_ge(S["scanned"], 2)

            def z_T(b):
                pe.wait_ge(S["y_out"], b + 1)
                for h in range(2):
                    if b >= 2:
                        pe.wait_ge(S["z_out"], 2 * (b - 2) + h + 1)
                    for k in range(4):
                        last = pe.transpose(ps[:, 4 + 2 * (b % 2) + h, P * k:P * k + J], yst[:, 4 * h + k, :], ident[0:J, 0:J])
                    last.then_inc(S["z_T"], 1)

            for hb in range(GP // 2):
                if hb >= 4:
                    pe.wait_ge(S["y_out"], (hb - 4) // 2 + 1)
                pe.wait_ge(S["n2_re"], hb + 1)
                pe.wait_ge(S["n2_im"], hb + 1)
                for pl in range(2):
                    gp = 2 * hb + pl
                    dst = ps[0:J, 2 * (hb // 2 % 2) + hb % 2, 2 * P * pl:2 * P * (pl + 1)]
                    for dirn in range(2):
                        for r in range(2):
                            last = pe.matmul(dst, Sarr[:, dirn, 0:J, r, gp],
                                             N_out[:, hb % 2, r, 2 * pl + dirn].rearrange("p h x -> p (h x)"),
                                             start=dirn == 0 and r == 0, stop=dirn == 1 and r == 1)
                        if dirn == 0:
                            for h in range(2):
                                pe.matmul(dst[:, P * h:P * (h + 1)], U[:, 2 * gp + h, :], TT[:, 2 * gp + h, :],
                                          start=False, stop=False)
                last.then_inc(S["y_done"], 1)
                if hb % 2 and hb >= 3:
                    z_T((hb - 3) // 2)
            z_T(KD - 1)

            pe.wait_ge(S["x2_in"], 32)
            for b in range(KD):
                for h in range(2):
                    if b >= 2:
                        pe.wait_ge(S["xT_out"], 2 * (b - 2) + h + 1)
                    else:
                        pe.wait_ge(S["z_out"], 2 * KD)
                    for k in range(4):
                        last = pe.transpose(ps[:, 4 + 2 * (b % 2) + h, P * k:P * k + J],
                                            xin2[:, 4 * h + k, P * b:P * (b + 1)], ident[0:J, 0:J])
                    last.then_inc(S["xT_T"], 1)

            def psum_free(ch, early):
                if not early:
                    pe.wait_ge(S["drained"], ch.drains - 2)

            def products(ch, dst, w0, nk, hi_, lo_, toks, per_block=None):
                wh, wl = (wview(w, ch.slot, w0 + nk) for w in (whi, wlo))
                for k in range(nk):
                    if per_block is not None:
                        pe.wait_ge(per_block[0], per_block[1] + k + 1)
                    for w, h, first, final in ((wh, hi_, k == 0, False), (wh, lo_, False, False),
                                               (wl, hi_, False, k == nk - 1)):
                        for (t0, t1), d in zip(((0, NLAT), (NLAT, T))[:1 if toks == NLAT else 2], dst):
                            last = pe.matmul(d, w[:, w0 + k, :], h[:, k, t0:t1], start=first, stop=final)
                return last

            def pair_stage(first, count, toks, ready):
                def one(m, c, turn):
                    ch = Chunk(first + c, turn)
                    a_l, b_l, a_c, b_c = glu_psum(ch.slot)
                    pe.wait_ge(S["lo_ready"], ch.n + 1)
                    psum_free(ch, turn is None and first + c < B_GLU + 2)
                    products(ch, (a_l, a_c), 0, KD, hhi, hlo, toks, ready if turn is None and c == 0 else None)
                    products(ch, (b_l, b_c), KD, KD, hhi, hlo, toks).then_inc(S["w_used"], 1)
                chunk_turns(pe, count, one)

            def plain_stage(first, count, nk, hi_, lo_, toks, ready=None):
                def one(m, c, turn):
                    ch = Chunk(first + c, turn)
                    a_l, _, a_c, _ = glu_psum(ch.slot)
                    pe.wait_ge(S["lo_ready"], ch.n + 1)
                    psum_free(ch, False)
                    products(ch, (a_l, a_c), 0, nk, hi_, lo_, toks, ready if turn is None and c == 0 else None)\
                        .then_inc(S["w_used"], 1)
                chunk_turns(pe, count, one)

            def norm(j, toks):
                for q, src in enumerate(squares[j]):
                    if q == 0:
                        pe.wait_ge(S["sq_added"], SQ_ADDS * (j + 1))
                    else:
                        pe.wait_ge(S["sq_done"], KD * (j + 1))
                    for t0, t1 in ((0, NLAT), (NLAT, T))[:1 if toks == NLAT else 2]:
                        last = pe.matmul(flat[:, 3072 + t0:3072 + t1], ones[:], src[:, t0:t1], start=q == 0, stop=q == 1)
                last.then_inc(S["stat_T"], 1)

            def ffn(l, toks, j):
                for g in range(2):
                    first = B_FFN[l] + g * (GF + KD)
                    pair_stage(first, GF, toks, (S["h_lo"], KD * j) if g == 0 else None)
                    plain_stage(first + GF, KD, GF, ghi, glo, toks, (S["g_lo"], KF * l + GF * g))

            pe.wait_ge(S["xT_out"], 2 * KD)
            pair_stage(B_GLU, KD, T, (S["z_lo"], 0))
            norm(0, T)
            ffn(0, T, 0)
            norm(1, T)

            unit = [0]
            job = [0]

            def sums(n, lhs, first, final):
                u = unit[0]
                unit[0] += 1
                pe.wait_ge(S["unit_sq"], u + 1)
                if first and job[0] >= 1:
                    pe.wait_ge(S["job_std"], job[0])
                for t0, t1 in ((0, NLAT), (NLAT, T))[:1 if n == NLAT else 2]:
                    last = pe.matmul(flat[:, 3072 + t0:3072 + t1], lhs[:], sqr[:, u % 2, t0:t1], start=first, stop=final)
                last.then_inc(S["unit_used"], 1)
                if final:
                    job[0] += 1

            def low_rank(c, nk, toks, ready=None):
                ch = Chunk(c)
                a_l, _, a_c, _ = glu_psum(ch.slot)
                pe.wait_ge(S["lo_ready"], ch.n + 1)
                psum_free(ch, False)
                products(ch, (a_l, a_c), 0, nk, *((hhi, hlo) if nk == KD else (cq_hi, cq_lo)), toks, ready)\
                    .then_inc(S["w_used"], 1)

            for m in range(3):
                low_rank(B_DKV + m, KD, T, (S["h_lo"], KD) if m == 0 else None)
                if m >= 1:
                    sums(T, ones, m == 1, m == 2)
            for m in range(6):
                low_rank(B_DQ + m, KD, NLAT)
                if m == 0:
                    sums(T, half_ones, True, True)
                else:
                    sums(NLAT, ones, m == 1, False)
            sums(NLAT, ones, False, True)
            use = used_after(B_UKV - 1)
            for m in range(4):
                ch = Chunk(B_UKV + m)
                pe.wait_ge(S["lo_ready"], ch.n + 1)
                wh, wl = (wview(w, ch.slot, 2, 4 * P) for w in (whi, wlo))
                for t in range(KV_USES[m]):
                    use += 1
                    a_l, _, a_c, _ = glu_psum((use - 1) % 2)
                    pe.wait_ge(S["drained"], use - B_GLU - 2)
                    if m == 0 and t == 0:
                        pe.wait_ge(S["ckv_lo_s"], 2)
                    for k in range(2):
                        for w, h, first, final in ((wh, ckv_hi, k == 0, False), (wh, ckv_lo, False, False),
                                                   (wl, ckv_hi, False, k == 1)):
                            if m < 2:
                                for (t0, t1), d in zip(((0, NLAT), (NLAT, T)), (a_l, a_c)):
                                    last = pe.matmul(d, w[:, k, P * t:P * (t + 1)], h[:, k, t0:t1], start=first, stop=final)
                            else:
                                last = pe.matmul(a_l, h[:, k, P * t:P * (t + 1)], w[:, k, :], start=first, stop=final)
                    last.then_inc(S["w_used"], 1)
                    if m < 2 and 4 * m + t >= 1:
                        sums(T, ones, True, True)
                    if m == 2 and t == 0:
                        sums(T, ones, True, True)
            def swap_halves(n, ready):
                pe.wait_ge(S["job_out"], ready)
                if n >= 2:
                    pe.wait_ge(S["rot_done"], n - 1)
                pe.matmul(ps[:, SWAP_BANKS[n % 2], :], swap[:], rotated[n], start=True, stop=True).then_inc(S["swap_T"], 1)

            for m in range(12):
                low_rank(B_UQ + m, 6, NLAT, (S["cq_lo_s"], 0) if m == 0 else None)
                if m >= 1:
                    sums(NLAT, half_ones if m - 1 < ROPE_PAIRS else ones, True, True)
                if m == 1:
                    swap_halves(0, JOB_UNITS[1])
                if 3 <= m < 3 + ROPE_PAIRS:
                    swap_halves(m - 2, JOB_UNITS[11 + m - 3])
            sums(NLAT, ones, True, True)
            pe.wait_ge(S["rot_done"], 1 + ROPE_PAIRS)
            pe.wait_ge(S["drained"], Chunk(B_UQ + 11).drains)

            def scores(i):
                h, t = i // 4, i % 4
                if t == 0:
                    pe.wait_ge(S["job_out"], JOB_UNITS[15 + h])
                if i >= 2:
                    pe.wait_ge(S["ex_done"], i - 1)
                rows = slice(ROPE * (h % 2), ROPE * (h % 2 + 1))
                for t0, t1 in ((0, NLAT), (NLAT, T)):
                    d = flat[:, 1024 * (i % 2) + t0:1024 * (i % 2) + t1]
                    pe.matmul(d, q_all[:, h, P * t:P * (t + 1)], kn[:, h, t0:t1], start=True, stop=False)
                    last = pe.matmul(d, q_all[rows, HEADS + h // 2, P * t:P * (t + 1)], kr[rows, t0:t1], start=False, stop=True)
                last.then_inc(S["sc_done"], 1)

            def head_out(h):
                pe.wait_ge(S["pT_out"], 4 * h + 4)
                if h >= 2:
                    pe.wait_ge(S["ot_out"], h - 1)
                if h == 0:
                    pe.wait_ge(S["job_std"], 23)
                for b in range(6):
                    last = pe.matmul(ps[:, 6 + h % 2, :], val[:, b, VD * h:VD * (h + 1)], pT[:, h % 2, b, :],
                                     start=b == 0, stop=b == 5)
                last.then_inc(S["pv_done"], 1)

            scores(0)
            for i in range(4 * HEADS):
                if i + 1 < 4 * HEADS:
                    scores(i + 1)
                pe.wait_ge(S["pr_set"], i + 1)
                if i >= 1:
                    pe.wait_ge(S["pT_out"], i)
                for b in range(6):
                    last = pe.transpose(flat[:, 2048 + P * b:2048 + P * (b + 1)], pr[:, i % 2, P * b:P * (b + 1)], ident[:])
                last.then_inc(S["p_T"], 1)
                if i % 4 == 0 and i:
                    head_out(i // 4 - 1)
            head_out(HEADS - 1)
            plain_stage(B_WO, KD, KD, hhi, hlo, NLAT, (S["o_lo"], 0))
            norm(2, NLAT)
            ffn(1, NLAT, 2)

            pe.wait_ge(S["drained"], used_after(B_FFN[1] + 2 * (GF + KD) - 1) - B_GLU)
            for t in range(4):
                for h in range(2):
                    if 2 * t + h >= 4:
                        pe.wait_ge(S["fin_out"], 2 * t + h - 3)
                    for b in range(4):
                        last = pe.transpose(ps[:, (2 * t + h) % 4, P * b:P * (b + 1)], xT[:, 4 * h + b, P * t:P * (t + 1)],
                                            ident[:])
                    last.then_inc(S["fin_T"], 1)


INPUTS = ("x", "c", "ctx", "c_ctx", "ada_w", "ada_b", "norm_mix", "norm_ffn", "s5_lam_re", "s5_lam_im", "s5_log_dt",
          "s5_b_re", "s5_b_im", "s5_c_re", "s5_c_im", "s5_d", "s5_glu_w", "s5_glu_b", "mla_w_dq", "mla_g_q", "mla_w_uq",
          "mla_w_dkv", "mla_g_kv", "mla_w_ukv", "mla_g_qn", "mla_g_qr", "mla_g_kn", "mla_g_kr", "mla_w_o",
          "ffn_w_in", "ffn_conv_w", "ffn_conv_b", "ffn_w_out")


def tables():
    grid, axis, freqs = 64, ROPE // 2, ROPE // 4
    tabs = np.zeros((P, TAB_N), np.float32)
    tabs[:, TAB_IDENT:TAB_IDENT + P] = np.eye(P, dtype=np.float32)
    inv = (np.float32(10000.0) ** (-np.arange(freqs, dtype=np.float32) / np.float32(freqs))).astype(np.float32)
    tok = np.arange(NLAT)
    for p in range(P):
        q, f = p % axis, p % freqs
        pos = tok // grid if (p % ROPE) < axis else tok % grid
        ang = pos.astype(np.float32) * inv[f]
        tabs[p, TAB_COS:TAB_COS + NLAT] = np.cos(ang)
        tabs[p, TAB_SIN:TAB_SIN + NLAT] = np.sin(ang)
        if q < freqs:
            tabs[p + freqs, TAB_SWAP + p] = -1.0
        else:
            tabs[p - freqs, TAB_SWAP + p] = 1.0
        h = p // ROPE
        tabs[p, TAB_HALF + h * ROPE:TAB_HALF + (h + 1) * ROPE] = 1.0
    return tabs


def kernel(**inputs):
    import concourse.bacc as bacc
    from concourse.bass_utils import run_bass_kernel_spmd

    nc = bacc.Bacc("TRN2", target_bir_lowering=False, num_devices=1)
    arrays = {f"in_{n}": np.ascontiguousarray(inputs[n]) for n in INPUTS}
    arrays["in_tabs"] = tables()
    a = {n[3:]: nc.dram_tensor(n, v.shape, mybir.dt.from_np(v.dtype), kind="ExternalInput").ap()
         for n, v in arrays.items()}
    a["out"] = nc.dram_tensor("out", (1, NLAT, D), F32, kind="ExternalOutput").ap()
    build(nc, a)
    r = run_bass_kernel_spmd(nc, [arrays], core_ids=[0])
    return r.results[0]["out"]
```
